# Optimizing a Trainium2 kernel written in Bass

```python
import jax
import jax.numpy as jnp
from jax import lax
import numpy as np

D_MODEL = 1024
BATCH = 1
SEQ = 128
DEPTH = 2
DEC_BATCH = 1
DEC_SEQ = 128
PAST_LEN = 128

GRID_W = 64
N_EVEN = (DEPTH + 1) // 2
N_ODD = DEPTH // 2
MIX_HALF = D_MODEL // 2
RET_HEADS = 4
RET_DV = MIX_HALF // RET_HEADS
RET_DK = RET_DV // 2
RET_CHUNK = 128
NA_HEADS = 4
NA_DH = MIX_HALF // NA_HEADS
NA_WIN_R = 8
NA_WIN_C = 16
CONV_CH = MIX_HALF
ATT_HEADS = 4
ATT_KV_HEADS = 2
ATT_DH = MIX_HALF // ATT_HEADS
ROPE_THETA = 10000.0
Q_BLOCK = 128
N_EXPERTS = 64
EXPERT_HIDDEN = D_MODEL // 8
SHARED_HIDDEN = EXPERT_HIDDEN
TOP_K = 8
N_GROUPS = 8
TOPK_GROUPS = 4
ROUTED_SCALE = 2.5
DEEPNORM_ALPHA = (2 * DEPTH) ** 0.25
DEEPNORM_BETA = (8 * DEPTH) ** -0.25
LN_EPS = 1e-5
RMS_EPS = 1e-6
EVEN_SIZES = (RET_HEADS * RET_DK, RET_HEADS * RET_DK, RET_HEADS * RET_DV, RET_HEADS * RET_DV,
              NA_HEADS * NA_DH, NA_HEADS * NA_DH, NA_HEADS * NA_DH)
ODD_SIZES = (CONV_CH, CONV_CH, CONV_CH, ATT_HEADS * ATT_DH, ATT_KV_HEADS * ATT_DH, ATT_KV_HEADS * ATT_DH)
IN_EVEN = sum(EVEN_SIZES)
IN_ODD = sum(ODD_SIZES)
MIX_EVEN = RET_HEADS * RET_DV + NA_HEADS * NA_DH
MIX_ODD = CONV_CH + ATT_HEADS * ATT_DH

kernel_name = 'hybrid_prefix_diffusion_trunk_step'

def _split(p, sizes):
    out, s = [], 0
    for n in sizes:
        out.append(p[..., s:s + n])
        s += n
    return out

def layer_norm(x, g, b):
    xf = x.astype(jnp.float32)
    mu = xf.mean(-1, keepdims=True)
    var = jnp.square(xf - mu).mean(-1, keepdims=True)
    return ((xf - mu) * lax.rsqrt(var + LN_EPS) * g + b).astype(x.dtype)

def rms_norm(x, g):
    xf = x.astype(jnp.float32)
    return (xf * lax.rsqrt(jnp.square(xf).mean(-1, keepdims=True) + RMS_EPS) * g).astype(x.dtype)

def head_norm(x):
    xf = x.astype(jnp.float32)
    mu = xf.mean(-1, keepdims=True)
    var = jnp.square(xf - mu).mean(-1, keepdims=True)
    return (xf - mu) * lax.rsqrt(var + LN_EPS)

def adaln(cond, w_mod, b_mod):
    m = jax.nn.silu(cond) @ w_mod + b_mod
    return jnp.split(m, 6, axis=-1)

def modulate(x, shift, scale):
    return x * (1.0 + scale) + shift

def post_norm(x, y, gate, g, b):
    return layer_norm(DEEPNORM_ALPHA * x + (1.0 + gate) * y, g, b)

def attend_blocked(q, k, v):
    B, Lq, Hq, dh = q.shape
    hkv = k.shape[2]
    g = Hq // hkv
    nb = Lq // Q_BLOCK
    scale = dh ** -0.5
    qb = q.reshape(B, nb, Q_BLOCK, hkv, g, dh).transpose(1, 0, 2, 3, 4, 5)

    def blk(qi):
        s = jnp.einsum('bqkgd,blkd->bkgql', qi, k) * scale
        p = jax.nn.softmax(s.astype(jnp.float32), axis=-1).astype(v.dtype)
        return jnp.einsum('bkgql,blkd->bqkgd', p, v)

    o = lax.map(blk, qb)
    return o.transpose(1, 0, 2, 3, 4, 5).reshape(B, Lq, Hq * dh)

def axial_rope(x):
    B, N, H, dh = x.shape
    t = jnp.arange(N)
    row = (t // GRID_W).astype(jnp.float32)
    col = (t % GRID_W).astype(jnp.float32)
    n_freq = dh // 4
    freqs = ROPE_THETA ** (-jnp.arange(n_freq, dtype=jnp.float32) / n_freq)
    ang = jnp.concatenate([row[:, None] * freqs, col[:, None] * freqs], axis=-1)
    cos = jnp.cos(ang)[None, :, None, :]
    sin = jnp.sin(ang)[None, :, None, :]
    x1 = x[..., 0::2].astype(jnp.float32)
    x2 = x[..., 1::2].astype(jnp.float32)
    out = jnp.stack([x1 * cos - x2 * sin, x1 * sin + x2 * cos], axis=-1).reshape(x.shape)
    return out.astype(x.dtype)

def retention_scan(q, k, v, log_gamma, s0):
    q, k, v, s0 = (t.astype(jnp.float32) for t in (q, k, v, s0))
    B, H, L, _ = q.shape
    C = RET_CHUNK
    n = L // C

    def chunks(t):
        return t.reshape(B, H, n, C, t.shape[-1]).transpose(2, 0, 1, 3, 4)

    pos = jnp.arange(C, dtype=jnp.float32)
    lg = log_gamma.astype(jnp.float32)[:, None]
    rel = pos[:, None] - pos[None, :]
    intra = jnp.where(rel >= 0, jnp.exp(lg[..., None] * jnp.maximum(rel, 0.0)), 0.0)
    q_decay = jnp.exp(lg * (pos + 1.0))
    k_decay = jnp.exp(lg * (C - 1.0 - pos))
    chunk_decay = jnp.exp(lg[:, 0] * C)

    def step(s, qkv):
        qc, kc, vc = qkv
        att = jnp.einsum('bhid,bhjd->bhij', qc, kc) * intra
        o = jnp.einsum('bhij,bhjv->bhiv', att, vc) + jnp.einsum('bhid,bhdv->bhiv', qc * q_decay[..., None], s)
        s = s * chunk_decay[:, None, None] + jnp.einsum('bhjd,bhjv->bhdv', kc * k_decay[..., None], vc)
        return s, o

    s, o = lax.scan(step, s0, (chunks(q), chunks(k), chunks(v)))
    o = o.transpose(1, 2, 0, 3, 4).reshape(B, H, L, -1)
    return o, s

def retention_branch(q, k, v, g, decay_logit, s0):
    B, L = q.shape[:2]
    log_gamma = jax.nn.log_sigmoid(decay_logit.astype(jnp.float32))
    qt, kt, vt = (t.transpose(0, 2, 1, 3) for t in (q, k, v))
    o_f, s_f = retention_scan(qt, kt, vt, log_gamma[0], s0[:, 0])
    o_b, s_b = retention_scan(jnp.flip(qt, 2), jnp.flip(kt, 2), jnp.flip(vt, 2), log_gamma[1], s0[:, 1])
    o = (o_f + jnp.flip(o_b, 2)).transpose(0, 2, 1, 3)
    out = (head_norm(o).reshape(B, L, -1) * jax.nn.silu(g.astype(jnp.float32))).astype(g.dtype)
    return out, jnp.stack([s_f, s_b], axis=1)

def na_latent(q, k, v, kc, vc, rpb):
    B, N, H, dh = q.shape
    rows = N // GRID_W
    wr = min(NA_WIN_R, rows)
    wc = NA_WIN_C
    nk = wr * GRID_W
    qg = q.reshape(B, rows, GRID_W, H, dh)
    kg = k.reshape(B, rows, GRID_W, H, dh)
    vg = v.reshape(B, rows, GRID_W, H, dh)
    col = jnp.arange(GRID_W)
    col_start = jnp.clip(col - wc // 2, 0, GRID_W - wc)
    col_in = (col[None, :] >= col_start[:, None]) & (col[None, :] < col_start[:, None] + wc)
    col_off = jnp.clip(col[None, :] - col[:, None] + NA_WIN_C - 1, 0, 2 * NA_WIN_C - 2)
    band_mask = jnp.broadcast_to(col_in[:, None, :], (GRID_W, wr, GRID_W)).reshape(GRID_W, nk)
    scale = dh ** -0.5

    def one_row(r):
        rs = jnp.clip(r - wr // 2, 0, rows - wr)
        qr = lax.dynamic_index_in_dim(qg, r, axis=1, keepdims=False)
        kb = lax.dynamic_slice_in_dim(kg, rs, wr, axis=1).reshape(B, nk, H, dh)
        vb = lax.dynamic_slice_in_dim(vg, rs, wr, axis=1).reshape(B, nk, H, dh)
        row_off = rs + jnp.arange(wr) - r + NA_WIN_R - 1
        bias = rpb[:, row_off[None, :, None], col_off[:, None, :]].reshape(H, GRID_W, nk)
        s_band = jnp.einsum('bqhd,bkhd->bhqk', qr, kb) * scale + bias
        s_band = jnp.where(band_mask, s_band, -jnp.inf)
        s_ctx = jnp.einsum('bqhd,blhd->bhql', qr, kc) * scale
        s = jnp.concatenate([s_band.astype(jnp.float32), s_ctx.astype(jnp.float32)], axis=-1)
        p = jax.nn.softmax(s, axis=-1).astype(v.dtype)
        return (jnp.einsum('bhqk,bkhd->bqhd', p[..., :nk], vb)
                + jnp.einsum('bhql,blhd->bqhd', p[..., nk:], vc))

    out = lax.map(one_row, jnp.arange(rows))
    return out.transpose(1, 0, 2, 3, 4).reshape(B, N, H * dh)

def even_project(h, w_in):
    B, L, _ = h.shape
    qr, kr, vr, gr, qn, kn, vn = _split(h @ w_in, EVEN_SIZES)
    qr = qr.reshape(B, L, RET_HEADS, RET_DK)
    kr = kr.reshape(B, L, RET_HEADS, RET_DK) * (RET_DK ** -0.5)
    vr = vr.reshape(B, L, RET_HEADS, RET_DV)
    qn, kn, vn = (t.reshape(B, L, NA_HEADS, NA_DH) for t in (qn, kn, vn))
    return qr, kr, vr, gr, qn, kn, vn

def even_mixer_ctx(h, w_in, w_out, decay_logit):
    qr, kr, vr, gr, qn, kn, vn = even_project(h, w_in)
    s0 = jnp.zeros((h.shape[0], 2, RET_HEADS, RET_DK, RET_DV), jnp.float32)
    ret, state = retention_branch(qr, kr, vr, gr, decay_logit, s0)
    na = attend_blocked(qn, kn, vn)
    out = jnp.concatenate([ret, na.astype(ret.dtype)], axis=-1) @ w_out
    return out, state, kn, vn

def even_mixer_lat(h, w_in, w_out, decay_logit, rpb, state, kc, vc):
    qr, kr, vr, gr, qn, kn, vn = even_project(h, w_in)
    ret, _ = retention_branch(qr, kr, vr, gr, decay_logit, state)
    na = na_latent(qn, kn, vn, kc, vc, rpb)
    return jnp.concatenate([ret, na.astype(ret.dtype)], axis=-1) @ w_out

def short_conv(u, w):
    up = jnp.pad(u, ((0, 0), (1, 1), (0, 0)))
    return up[:, :-2] * w[0] + up[:, 1:-1] * w[1] + up[:, 2:] * w[2]

def odd_project(h, w_in, conv_w, qn_g, kn_g):
    B, L, _ = h.shape
    b_g, c_g, u, q, k, v = _split(h @ w_in, ODD_SIZES)
    conv = b_g * short_conv(c_g * u, conv_w)
    q = rms_norm(q.reshape(B, L, ATT_HEADS, ATT_DH), qn_g)
    k = rms_norm(k.reshape(B, L, ATT_KV_HEADS, ATT_DH), kn_g)
    v = v.reshape(B, L, ATT_KV_HEADS, ATT_DH)
    return conv, q, k, v

def odd_mixer_ctx(h, w_in, w_out, conv_w, qn_g, kn_g):
    conv, q, k, v = odd_project(h, w_in, conv_w, qn_g, kn_g)
    att = attend_blocked(q, k, v)
    out = jnp.concatenate([conv, att.astype(conv.dtype)], axis=-1) @ w_out
    return out, k, v

def odd_mixer_lat(h, w_in, w_out, conv_w, qn_g, kn_g, kc, vc):
    conv, q, k, v = odd_project(h, w_in, conv_w, qn_g, kn_g)
    q = axial_rope(q)
    k = axial_rope(k)
    keys = jnp.concatenate([k, kc.astype(k.dtype)], axis=1)
    vals = jnp.concatenate([v, vc.astype(v.dtype)], axis=1)
    att = attend_blocked(q, keys, vals)
    return jnp.concatenate([conv, att.astype(conv.dtype)], axis=-1) @ w_out

def moe_ffn(h, router_w, router_b, wg, wu, wd, sg, su, sd):
    shp = h.shape
    x = h.reshape(-1, shp[-1])
    T = x.shape[0]
    scores = jax.nn.sigmoid((x @ router_w).astype(jnp.float32))
    sel = scores + router_b.astype(jnp.float32)
    grp_score = lax.top_k(sel.reshape(T, N_GROUPS, -1), 2)[0].sum(-1)
    _, gidx = lax.top_k(grp_score, TOPK_GROUPS)
    gmask = jax.nn.one_hot(gidx, N_GROUPS).sum(1) > 0
    emask = jnp.repeat(gmask, N_EXPERTS // N_GROUPS, axis=1)
    _, eidx = lax.top_k(jnp.where(emask, sel, -jnp.inf), TOP_K)
    w = jnp.take_along_axis(scores, eidx, axis=-1)
    w = w / w.sum(-1, keepdims=True) * ROUTED_SCALE
    gate = jnp.einsum('tk,tke->te', w, jax.nn.one_hot(eidx, N_EXPERTS, dtype=jnp.float32)).astype(x.dtype)
    hg = jnp.einsum('td,edf->tef', x, wg)
    hu = jnp.einsum('td,edf->tef', x, wu)
    y = jnp.einsum('tef,efd->td', jax.nn.silu(hg) * hu * gate[:, :, None], wd)
    y = y + (jax.nn.silu(x @ sg) * (x @ su)) @ sd
    return y.reshape(shp)

def setup_inputs(seed: int = 0) -> dict:
    key = jax.random.key(seed)
    ks = jax.random.split(key, 30)

    def nrm(k, shape, scale):
        return jax.random.normal(k, shape, jnp.float32) * scale

    gam = 1.0 - 2.0 ** (-5.0 - jnp.arange(RET_HEADS, dtype=jnp.float32))
    base_logit = jnp.log(gam) - jnp.log1p(-gam)
    return {
        'x_prompt': nrm(ks[0], (BATCH, SEQ, D_MODEL), 1.0),
        'x_sample': nrm(ks[1], (DEC_BATCH, DEC_SEQ, D_MODEL), 1.0),
        'c': nrm(ks[2], (DEC_BATCH, D_MODEL), 1.0),
        'state_ret': nrm(ks[3], (DEC_BATCH, N_EVEN, 2, RET_HEADS, RET_DK, RET_DV), 1.0),
        'cache_na_k': nrm(ks[4], (DEC_BATCH, N_EVEN, PAST_LEN, NA_HEADS, NA_DH), 1.0),
        'cache_na_v': nrm(ks[5], (DEC_BATCH, N_EVEN, PAST_LEN, NA_HEADS, NA_DH), 1.0),
        'cache_att_k': nrm(ks[6], (DEC_BATCH, N_ODD, PAST_LEN, ATT_KV_HEADS, ATT_DH), 1.0),
        'cache_att_v': nrm(ks[7], (DEC_BATCH, N_ODD, PAST_LEN, ATT_KV_HEADS, ATT_DH), 1.0),
        'c_ctx': nrm(ks[8], (D_MODEL,), 1.0),
        'w_mod': nrm(ks[9], (DEPTH, D_MODEL, 6 * D_MODEL), 0.2 * D_MODEL ** -0.5),
        'b_mod': nrm(ks[10], (DEPTH, 6 * D_MODEL), 0.01),
        'ln_g': 1.0 + nrm(ks[11], (DEPTH, 2, D_MODEL), 0.02),
        'ln_b': nrm(ks[12], (DEPTH, 2, D_MODEL), 0.02),
        'w_in_even': nrm(ks[13], (N_EVEN, D_MODEL, IN_EVEN), D_MODEL ** -0.5),
        'w_out_even': nrm(ks[14], (N_EVEN, MIX_EVEN, D_MODEL), DEEPNORM_BETA * MIX_EVEN ** -0.5),
        'ret_decay_logit': jnp.broadcast_to(base_logit, (N_EVEN, 2, RET_HEADS)) + nrm(ks[15], (N_EVEN, 2, RET_HEADS), 0.05),
        'na_rpb': nrm(ks[16], (N_EVEN, NA_HEADS, 2 * NA_WIN_R - 1, 2 * NA_WIN_C - 1), 0.1),
        'w_in_odd': nrm(ks[17], (N_ODD, D_MODEL, IN_ODD), D_MODEL ** -0.5),
        'w_out_odd': nrm(ks[18], (N_ODD, MIX_ODD, D_MODEL), DEEPNORM_BETA * MIX_ODD ** -0.5),
        'conv_w': nrm(ks[19], (N_ODD, 3, CONV_CH), 3.0 ** -0.5),
        'q_norm_g': 1.0 + nrm(ks[20], (N_ODD, ATT_DH), 0.02),
        'k_norm_g': 1.0 + nrm(ks[21], (N_ODD, ATT_DH), 0.02),
        'router_w': nrm(ks[22], (DEPTH, D_MODEL, N_EXPERTS), D_MODEL ** -0.5),
        'router_b': nrm(ks[23], (DEPTH, N_EXPERTS), 0.01),
        'exp_w_gate': nrm(ks[24], (DEPTH, N_EXPERTS, D_MODEL, EXPERT_HIDDEN), D_MODEL ** -0.5),
        'exp_w_up': nrm(ks[25], (DEPTH, N_EXPERTS, D_MODEL, EXPERT_HIDDEN), D_MODEL ** -0.5),
        'exp_w_down': nrm(ks[26], (DEPTH, N_EXPERTS, EXPERT_HIDDEN, D_MODEL), DEEPNORM_BETA * EXPERT_HIDDEN ** -0.5),
        'sh_w_gate': nrm(ks[27], (DEPTH, D_MODEL, SHARED_HIDDEN), D_MODEL ** -0.5),
        'sh_w_up': nrm(ks[28], (DEPTH, D_MODEL, SHARED_HIDDEN), D_MODEL ** -0.5),
        'sh_w_down': nrm(ks[29], (DEPTH, SHARED_HIDDEN, D_MODEL), DEEPNORM_BETA * SHARED_HIDDEN ** -0.5),
    }

def reference(x_prompt, x_sample, c, state_ret, cache_na_k, cache_na_v, cache_att_k, cache_att_v, c_ctx,
              w_mod, b_mod, ln_g, ln_b, w_in_even, w_out_even, ret_decay_logit, na_rpb,
              w_in_odd, w_out_odd, conv_w, q_norm_g, k_norm_g, router_w, router_b,
              exp_w_gate, exp_w_up, exp_w_down, sh_w_gate, sh_w_up, sh_w_down):
    ctx_cond = c_ctx[None, None, :]
    lat_cond = c[:, None, :]
    yp, ys = x_prompt, x_sample
    ret_states, na_k, na_v, att_k, att_v = [], [], [], [], []
    for l in range(DEPTH):
        i = l // 2
        mp = adaln(ctx_cond, w_mod[l], b_mod[l])
        ms = adaln(lat_cond, w_mod[l], b_mod[l])
        hp = modulate(yp, mp[0], mp[1])
        hs = modulate(ys, ms[0], ms[1])
        if l % 2 == 0:
            op, st, kp, vp = even_mixer_ctx(hp, w_in_even[i], w_out_even[i], ret_decay_logit[i])
            os_ = even_mixer_lat(hs, w_in_even[i], w_out_even[i], ret_decay_logit[i], na_rpb[i],
                                 state_ret[:, i], cache_na_k[:, i], cache_na_v[:, i])
            ret_states.append(st)
            na_k.append(kp)
            na_v.append(vp)
        else:
            op, kp, vp = odd_mixer_ctx(hp, w_in_odd[i], w_out_odd[i], conv_w[i], q_norm_g[i], k_norm_g[i])
            os_ = odd_mixer_lat(hs, w_in_odd[i], w_out_odd[i], conv_w[i], q_norm_g[i], k_norm_g[i],
                                cache_att_k[:, i], cache_att_v[:, i])
            att_k.append(kp)
            att_v.append(vp)
        yp = post_norm(yp, op, mp[2], ln_g[l, 0], ln_b[l, 0])
        ys = post_norm(ys, os_, ms[2], ln_g[l, 0], ln_b[l, 0])
        moe_w = (router_w[l], router_b[l], exp_w_gate[l], exp_w_up[l], exp_w_down[l], sh_w_gate[l], sh_w_up[l], sh_w_down[l])
        yp = post_norm(yp, moe_ffn(modulate(yp, mp[3], mp[4]), *moe_w), mp[5], ln_g[l, 1], ln_b[l, 1])
        ys = post_norm(ys, moe_ffn(modulate(ys, ms[3], ms[4]), *moe_w), ms[5], ln_g[l, 1], ln_b[l, 1])
    new_state_ret = jnp.stack(ret_states, axis=1)
    new_na_k = jnp.stack(na_k, axis=1)
    new_na_v = jnp.stack(na_v, axis=1)
    new_att_k = jnp.stack(att_k, axis=1)
    new_att_v = jnp.stack(att_v, axis=1)
    return (yp, ys, new_state_ret, new_na_k, new_na_v, new_att_k, new_att_v)


_drawn_inputs = setup_inputs


def setup_inputs(seed=0):
    import zlib

    import numpy as np

    out = dict(_drawn_inputs(seed))
    spreads = {}
    factors = {'na_rpb': 5.042,
     'q_norm_g': 8.0,
     'k_norm_g': 2.813,
     'cache_att_k': 8.0,
     'cache_att_v': 8.0}
    for name, (base, spread) in spreads.items():
        noise = np.random.default_rng([zlib.crc32(name.encode()), seed]).standard_normal(out[name].shape)
        drawn = base * np.exp(spread * noise) if base else spread * noise
        out[name] = jnp.asarray(drawn.astype(out[name].dtype))
    for name, factor in factors.items():
        out[name] = (out[name] * factor).astype(out[name].dtype)
    return out
```

```python
from contextlib import ExitStack

import numpy as np

import concourse.bass as bass
from concourse import mybir

F32 = mybir.dt.float32
F32R = mybir.dt.float32r
ACT = mybir.ActivationFunctionType
ALU = mybir.AluOpType
AX = mybir.AxisListType

P = 128
D = 1024
KC = D // P
G = 2
TOK = G * P
DEPTH = 2
GRID_W = 64
H = 4
DK = 64
KVH = 2
UNIT = 256
EXPERTS = 64
HID = 128
GROUPS = 8
PER_GROUP = EXPERTS // GROUPS
TOPK_GROUPS = 4
ROUTED_SCALE = 2.5
ALPHA = (2 * DEPTH) ** 0.25
LN_EPS = 1e-5
RMS_EPS = 1e-6
ATT_SCALE = float(P) ** -0.5
KEY_SCALE = float(DK) ** -0.5
LOW = -1.0e30
GONE = -3.0e38

MOD_UNITS = 6 * D // UNIT
SEC = D // UNIT
IN_UNITS = (12, 10)
OUT_UNITS = D // UNIT
TURNS = EXPERTS + 1
LOOPS = (TURNS - 5) // 4
FIRST_MODS = 2 * SEC

BASE = [0]
for _l in range(DEPTH):
    BASE.append(BASE[-1] + MOD_UNITS + IN_UNITS[_l] + OUT_UNITS + TURNS)


def mod_unit(l, n):
    return BASE[l] + n + (IN_UNITS[l] if n >= FIRST_MODS else 0)


def in_unit(l, n):
    return BASE[l] + FIRST_MODS + n


def out_unit(l, n):
    return BASE[l] + MOD_UNITS + IN_UNITS[l] + n


def turn_unit(l, t):
    return BASE[l] + MOD_UNITS + IN_UNITS[l] + OUT_UNITS + t


def pair(l, t):
    return (l * TURNS + t) % 2


def in_before(l):
    return sum(IN_UNITS[:l])


KIND = {}
for _l in range(DEPTH):
    for _n in range(MOD_UNITS):
        KIND[mod_unit(_l, _n)] = ("mod", _l, _n)
    for _n in range(IN_UNITS[_l]):
        KIND[in_unit(_l, _n)] = ("in", _l, _n)
    for _n in range(OUT_UNITS):
        KIND[out_unit(_l, _n)] = ("out", _l, _n)
    for _n in range(TURNS):
        KIND[turn_unit(_l, _n)] = ("turn", _l, _n)

RAW = 4
LOADED, _at = {}, [0] * RAW
for _u in range(BASE[-1]):
    _at[_u % RAW] += 32 if KIND[_u][0] == "turn" else 16
    LOADED[_u] = _at[_u % RAW]

KEPT = dict(ident=128, cos=64, sin=64, window=128, pick=2 * 128, fold=2, plus=1, one=1, ln_eps=1, rms_eps=1)
EARLY = dict(rel_f=128, rel_b=128, mask_f=128, mask_b=128, pos_row=128, pos_col=2)


def columns(widths, at=0):
    out = {}
    for name, w in widths.items():
        out[name] = (at, at + w)
        at += w
    return out, at


KEPT_AT, KEPT_N = columns(KEPT)
EARLY_AT, EARLY_END = columns(EARLY, KEPT_N)
EARLY_N = EARLY_END - KEPT_N


def shape_constants():
    c = np.zeros((P, EARLY_END), np.float32)

    def put(name, value):
        a, b = {**KEPT_AT, **EARLY_AT}[name]
        c[:, a:b] = value

    i = np.arange(P)
    put("ident", np.eye(P))
    n_freq = P // 4
    freqs = np.float32(10000.0) ** (-np.arange(n_freq, dtype=np.float32) / np.float32(n_freq))
    row, col = (i // GRID_W).astype(np.float32), (i % GRID_W).astype(np.float32)
    ang = np.concatenate([row[:, None] * freqs, col[:, None] * freqs], axis=1)
    put("cos", np.cos(ang))
    put("sin", np.sin(ang))
    start = np.clip(i % GRID_W - 8, 0, GRID_W - 16)
    kc = (i % GRID_W)[None, :]
    put("window", np.where((kc >= start[:, None]) & (kc < start[:, None] + 16), 0.0, LOW))
    pick = np.zeros((P, G, P))
    for g in range(G):
        pick[g, g] = pick[g + G, g] = 1.0
    put("pick", pick.reshape(P, G * P))
    fold = np.zeros((P, G))
    for g in range(G):
        fold[g, g] = fold[g + G, g] = 1.0
    put("fold", fold)
    plus = np.zeros((P, 1))
    plus[:G] = 1.0
    put("plus", plus)
    put("one", 1.0)
    put("ln_eps", LN_EPS)
    put("rms_eps", RMS_EPS)
    rel = (i[None, :] - i[:, None]).astype(np.float32)
    put("rel_f", np.maximum(rel, 0))
    put("rel_b", np.maximum(-rel, 0))
    put("mask_f", rel >= 0)
    put("mask_b", rel <= 0)
    put("pos_row", np.where(i[:, None] < DK, i[None, :] + 1.0, P - i[None, :]))
    put("pos_col", np.stack([P - 1.0 - i, i], axis=1))
    return c


def build(nc, A, O):
    with ExitStack() as ctx:
        def sb(name, shape, dt=F32):
            return ctx.enter_context(nc.sbuf_tensor(name, shape, dt))

        def sem(name):
            return ctx.enter_context(nc.semaphore(name))

        raw_main = sb("raw_main", [P, RAW, KC * UNIT])
        raw_down = sb("raw_down", [P, 2, D])
        hi_main = sb("hi_main", [P, 2, KC * UNIT], F32R)
        lo_main = sb("lo_main", [P, 2, KC * UNIT], F32R)
        hi_down = sb("hi_down", [P, 2, D], F32R)
        lo_down = sb("lo_down", [P, 2, D], F32R)
        x_tok = sb("x_tok", [P, G, D])
        x_feat = sb("x_feat", [P, KC, TOK])
        x_hi = sb("x_hi", [P, KC, TOK], F32R)
        x_lo = sb("x_lo", [P, KC, TOK], F32R)
        proj = sb("proj", [P, 14, 512])
        temp = sb("temp", [P, 7168])
        const = sb("const", [P, KEPT_N])
        cond_parts = sb("cond_parts", [P, KC, P], F32R)
        cond = sb("cond", [P, G, KC])
        cond_s = sb("cond_s", [P, G, KC])
        b_rows = sb("b_rows", [2 * G, RAW, UNIT])
        mod_row = sb("mod_row", [2 * G, D])
        gate_row = sb("gate_row", [2 * G, 2, D])
        mod_feat = sb("mod_feat", [P, 4, KC, G])
        hid_hi = sb("hid_hi", [P, 2, TOK], F32R)
        hid_lo = sb("hid_lo", [P, 2, TOK], F32R)
        small = sb("small", [P, 192])
        decay = sb("decay", [P, 5 * 12])

        ps = ctx.enter_context(nc.psum_tensor("ps", [P, 8, 512], F32))

        def K(name, rows=P):
            a, b = KEPT_AT[name]
            return const[0:rows, a:b]

        early = proj[:, :, :].rearrange("p a b -> p (a b)")[:, 0:EARLY_N]

        def E(name):
            a, b = EARLY_AT[name]
            return early[:, a - KEPT_N:b - KEPT_N]

        def T(at, *shape):
            n = int(np.prod(shape))
            flat = temp[:, at:at + n]
            if len(shape) == 1:
                return flat
            letters = "abcd"[:len(shape)]
            return flat.rearrange(f"p ({' '.join(letters)}) -> p {' '.join(letters)}",
                                  **{x: s for x, s in zip(letters[1:], shape[1:])})

        sc_ctx = T(0, H, P)
        sc_lat = T(512, H, 2 * P)
        att_d = T(1536, 2, G, 2, P)
        pr_t = T(1536, 3, H, P)
        dmat = T(3072, H, P)
        k_out = T(3072, H, P)
        q_dec = T(3584, H, P)
        k_dec = T(4096, H, 2, DK)
        q_pow = T(4608, H, P)
        st_out = T(4608, H, P)
        kc_t = T(5120, H, P)
        vc = T(5632, H, P)
        s0 = T(6144, H, P)
        bias = T(6656, H, 2, GRID_W)
        kc_in = T(1536, H, P)
        rows_pad = T(0, H * 3, 127)
        dec_e = T(2048, 2, H, P)
        z_pad = T(3072, 2 * 2 * G, P + 2)
        conv_o = T(4112, 4, G, P)
        cv_w = small[:, 60:72].rearrange("p (w t) -> p w t", w=3)
        kc_t1 = T(5632, KVH, P)
        vc1 = T(5888, KVH, P)
        kc_in1 = T(6144, KVH, P)
        gains = T(6400, 2, P)
        sq = T(1536, 12, P)
        roped = T(3072, 6, P)
        qk_t = T(0, 0 + 12, P)
        ln_g = T(0, D)
        ln_b = T(1024, D)
        z = T(2048, G, D)
        rw = T(6144, KC, EXPERTS)
        rb = T(6656, EXPERTS)
        pf = proj[:, :, :].rearrange("p a b -> p (a b)")
        ex_silu = pf[:, 0:512].rearrange("p (a b) -> p a b", a=2)
        ex_up = pf[:, 512:1024].rearrange("p (a b) -> p a b", a=2)
        ex_h = pf[:, 1024:1536].rearrange("p (a b) -> p a b", a=2)
        ex_gate = pf[:, 1536:2560].rearrange("p (a b) -> p a b", a=4)
        score = pf[:, 2560:2688]
        select = pf[:, 2688:2816]
        gsel = pf[:, 2816:2944]
        taken = pf[:, 2944:3072]
        top = pf[:, 3072:3200].rearrange("p (a b) -> p a b", b=8)
        gscore = pf[:, 3200:3216]
        gtaken = pf[:, 3216:3232]
        gmask = pf[:, 3232:3248]
        gpen = pf[:, 3248:3264]
        top4 = pf[:, 3264:3280].rearrange("p (a b) -> p a b", a=2)
        top8 = pf[:, 3280:3296].rearrange("p (a b) -> p a b", a=2)
        wsum = pf[:, 3296:3298]
        gate_t = pf[0:EXPERTS, 3328:3328 + TOK]

        q_dup = proj[:, 0:2, :].rearrange("p a (b c) -> p (a b) c", b=2)
        k_low = proj[0:DK, 2:4, :].rearrange("p a (b c) -> p (a b) c", b=2)

        def even_v(h, g):
            return proj[:, 4 + h // 2, g * UNIT + (h % 2) * P:g * UNIT + (h % 2) * P + P]

        def even_gate(h, g):
            return proj[:, 6 + h // 2, g * UNIT + (h % 2) * P:g * UNIT + (h % 2) * P + P]

        def na_q(h, g):
            return proj[:, 8 + h // 2, (h % 2) * TOK + g * P:(h % 2) * TOK + g * P + P]

        def na_k(h, g):
            return proj[:, 10 + h // 2, (h % 2) * TOK + g * P:(h % 2) * TOK + g * P + P]

        def na_v(h, g):
            return proj[:, 12 + h // 2, g * UNIT + (h % 2) * P:g * UNIT + (h % 2) * P + P]

        def att_v(h, g):
            return proj[:, 9, g * UNIT + h * P:g * UNIT + h * P + P]

        pad_dram = nc.dram_tensor("pad_rows", [GRID_W, H * 3 * 127], F32, kind="Internal").ap()
        gate_dram = [nc.dram_tensor(f"gates{l}", [EXPERTS, TOK], F32, kind="Internal").ap() for l in range(DEPTH)]

        main_loaded = [sem(f"main_loaded{i}") for i in range(RAW)]
        down_loaded = [sem(f"down_loaded{i}") for i in range(2)]
        bias_loaded = [sem(f"bias_loaded{i}") for i in range(RAW)]
        gate_loaded = [sem(f"gate_loaded{i}") for i in range(4)]
        main_hi, main_lo, main_used = sem("main_hi"), sem("main_lo"), sem("main_used")
        down_hi, down_lo, down_used = sem("down_hi"), sem("down_lo"), sem("down_used")
        consts_in, early_in, x_in, cond_in = sem("consts_in"), sem("early_in"), sem("x_in"), sem("cond_in")
        decay_in, cache_k_in, cache_v_in = sem("decay_in"), sem("cache_k_in"), sem("cache_v_in")
        state_in, rpb_in, bias_in, pad_out = sem("state_in"), sem("rpb_in"), sem("bias_in"), sem("pad_out")
        ln_in, router_in, small_in = sem("ln_in"), sem("router_in"), sem("small_in")
        pad_zero = sem("pad_zero")
        cond_ready = sem("cond_ready")
        mod_rows_out, mod_t, mod_t_out = sem("mod_rows_out"), sem("mod_t"), sem("mod_t_out")
        xt_done, x_feat_act, x_feat_dve = sem("xt_done"), sem("x_feat_act"), sem("x_feat_dve")
        x_hi_done, x_lo_done = sem("x_hi_done"), sem("x_lo_done")
        in_out = sem("in_out")
        act_chain, dve_chain, pool_chain = sem("act_chain"), sem("dve_chain"), sem("pool_chain")
        decay_ready = sem("decay_ready")
        cache_t, cache_t_out = sem("cache_t"), sem("cache_t_out")
        att_s, att_d_ready, k_t, k_dec_ready = sem("att_s"), sem("att_d_ready"), sem("k_t"), sem("k_dec_ready")
        scores, centred, exped, probs = sem("scores"), sem("centred"), sem("exped"), sem("probs")
        state_mm, state_copied = sem("state_mm"), sem("state_copied")
        ret_o, ret_var, ret_sd, ret_ready = sem("ret_o"), sem("ret_var"), sem("ret_sd"), sem("ret_ready")
        probs_t, probs_t_out, att_o = sem("probs_t"), sem("probs_t_out"), sem("att_o")
        ret_t, kn_t, kn_out = sem("ret_t"), sem("kn_t"), sem("kn_out")
        cat_ready = sem("cat_ready")
        qk_normed, roped_ready, sq_ready = sem("qk_normed"), sem("roped_ready"), sem("sq_ready")
        ms_ready, rms_ready = sem("ms_ready"), sem("rms_ready")
        qk_tr, qk_t_out = sem("qk_tr"), sem("qk_t_out")
        gates_mm, gate_copied, ln_var, ln_sd, normed = sem("gates_mm"), sem("gate_copied"), sem("ln_var"), sem("ln_sd"), sem("normed")
        logits, sigmoid_out, gates_made = sem("logits"), sem("sigmoid_out"), sem("gates_made")
        gates_t, gates_t_out, gates_stored = sem("gates_t"), sem("gates_t_out"), sem("gates_stored")
        ones_set = sem("ones_set")
        silu_out, up_read, h_ready, h_hi, h_lo = sem("silu_out"), sem("up_read"), sem("h_ready"), sem("h_hi"), sem("h_lo")
        stored = sem("stored")

        block = ctx.enter_context(nc.Block())

        w_in = (A["w_in_even"][0], A["w_in_odd"][0])
        w_out = (A["w_out_even"][0], A["w_out_odd"][0])

        @block.sync
        def _(sp):
            def slot_free(u):
                if u >= RAW:
                    sp.wait_ge(main_lo, u - RAW + 1)

            def load_unit(u, source):
                slot_free(u)
                sp.dma_start(raw_main[:, u % RAW, :].rearrange("p (k n) -> p k n", k=KC), source) \
                    .then_inc(main_loaded[u % RAW], 16)

            def load_mod(l, n):
                cols = slice(n * UNIT, (n + 1) * UNIT)
                load_unit(mod_unit(l, n), A["w_mod"][l].rearrange("(p k) n -> p k n", k=KC)[:, :, cols])
                at = l * MOD_UNITS + n
                if at == 0:
                    sp.wait_ge(pad_zero, 2)
                if at >= RAW:
                    sp.wait_ge(mod_rows_out, at - RAW + 1)
                sp.dma_start(b_rows[0:G, at % RAW, :], A["b_mod"][l:l + 1, cols].partition_broadcast(G)) \
                    .then_inc(bias_loaded[at % RAW], 16)

            def load_turn(l, t, slot, down, gate, up, out_w):
                u = turn_unit(l, 0) + t
                sp.wait_ge(main_lo, u - RAW + 1)
                view = raw_main[:, slot, :].rearrange("p (k w n) -> p w k n", k=KC, w=2)
                sp.dma_start(view[:, 0], gate.rearrange("(p k) n -> p k n", k=KC)).then_inc(main_loaded[slot], 16)
                sp.dma_start(view[:, 1], up.rearrange("(p k) n -> p k n", k=KC)).then_inc(main_loaded[slot], 16)
                if not (isinstance(t, int) and l * TURNS + t < 2):
                    sp.wait_ge(down_lo, l * TURNS - 1 + t)
                sp.dma_start(raw_down[:, down, :], out_w).then_inc(down_loaded[down], 16)

            def expert(l, e):
                return A["exp_w_gate"][l, e], A["exp_w_up"][l, e], A["exp_w_down"][l, e]

            for l in range(DEPTH):
                for n in range(FIRST_MODS):
                    load_mod(l, n)
                for n in range(IN_UNITS[l]):
                    load_unit(in_unit(l, n), w_in[l].rearrange("(p k) n -> p k n", k=KC)[:, :, n * UNIT:(n + 1) * UNIT])
                for n in range(FIRST_MODS, MOD_UNITS):
                    load_mod(l, n)
                for n in range(OUT_UNITS):
                    load_unit(out_unit(l, n), w_out[l].rearrange("(k p) n -> p k n", k=KC)[:, :, n * UNIT:(n + 1) * UNIT])
                u0 = turn_unit(l, 0)
                load_turn(l, 0, u0 % RAW, pair(l, 0), A["sh_w_gate"][l], A["sh_w_up"][l], A["sh_w_down"][l])
                for t in range(1, 5):
                    load_turn(l, t, (u0 + t) % RAW, pair(l, t), *expert(l, t - 1))
                with sp.Fori(0, LOOPS) as i:
                    for j in range(4):
                        load_turn(l, 5 + j + 4 * i, (u0 + 5 + j) % RAW, pair(l, 5 + j), *expert(l, 4 + j + 4 * i))

        @block.gpsimd
        def _(pool):
            nc.gpsimd.memset(rows_pad[0:GRID_W], 0.0).then_inc(pad_zero, 1)
            nc.gpsimd.memset(b_rows[:, :, :], 0.0).then_inc(pad_zero, 1)
            pool.wait_ge(pad_zero, 1)
            for h in range(H):
                pool.dma_start(rows_pad[0:GRID_W, 3 * h:3 * h + 3, 48:79],
                               A["na_rpb"][0, h, 6:9, :].partition_broadcast(GRID_W)).then_inc(rpb_in, 16)
            pool.dma_start(kc_in, A["cache_na_k"][0, 0]).then_inc(cache_k_in, 16)
            pool.dma_start(vc, A["cache_na_v"][0, 0]).then_inc(cache_v_in, 16)
            for d in range(2):
                pool.dma_start(s0[d * DK:(d + 1) * DK], A["state_ret"][0, 0, d].rearrange("h k v -> k h v")) \
                    .then_inc(state_in, 16)
            pool.wait_ge(rpb_in, 16 * H)
            pool.dma_start(pad_dram, rows_pad[0:GRID_W].rearrange("p a b -> p (a b)")).then_inc(pad_out, 16)
            pool.wait_ge(pad_out, 16)
            for r in range(2):
                for h in range(H):
                    skew = bass.AP(pad_dram.tensor, 63 + (3 * h + 1 - r) * 127,
                                   [[H * 3 * 127 - 1, GRID_W], [127, 2], [1, GRID_W]])
                    pool.dma_start(bias[r * GRID_W:(r + 1) * GRID_W, h], skew).then_inc(bias_in, 16)

            for l in range(DEPTH):
                if l == 1:
                    pool.wait_ge(normed, 2 * G)
                    pool.dma_start(kc_in1, A["cache_att_k"][0, 0]).then_inc(cache_k_in, 16)
                    pool.dma_start(vc1, A["cache_att_v"][0, 0]).then_inc(cache_v_in, 16)
                    pool.dma_start(gains[:, 0:1], A["q_norm_g"][0:1].partition_broadcast(P)).then_inc(small_in, 16)
                    pool.dma_start(gains[:, 1:2], A["k_norm_g"][0:1].partition_broadcast(P)).then_inc(small_in, 16)
                    with nc.allow_non_contiguous_dma("1,536 values of the convolution"):
                        for w in range(3):
                            pool.dma_start(cv_w[:, w], A["conv_w"][0, w].rearrange("(t p) -> p t", p=P)) \
                                .then_inc(small_in, 16)
                if l == 0:
                    pool.wait_ge(in_out, 12)
                    pool.dma_start(O["na_v"][0, 0].rearrange("t h d -> t (h d)").rearrange("t (u c) -> t u c", u=2),
                                   proj[:, 12:14, 0:UNIT]).then_inc(stored, 16)
                    pool.wait_ge(state_copied, 1)
                    for d in range(2):
                        pool.dma_start(O["state"][0, 0, d].rearrange("h k v -> k h v"), st_out[d * DK:(d + 1) * DK]) \
                            .then_inc(stored, 16)
                    pool.wait_ge(kn_out, 1)
                    pool.dma_start(O["na_k"][0, 0], k_out).then_inc(stored, 16)
                else:
                    pool.wait_ge(in_out, in_before(1) + 10)
                    pool.dma_start(O["att_v"][0, 0].rearrange("t h d -> t (h d)"), proj[:, 9, 0:UNIT]).then_inc(stored, 16)
                    pool.wait_ge(qk_normed, 2)
                    pool.dma_start(O["att_k"][0, 0].rearrange("t h d -> t (h d)"), proj[:, 8, 0:UNIT]).then_inc(stored, 16)
                pool.wait_ge(cat_ready, l + 1)
                pool.wait_ge(stored, 16 * (4 if l == 0 else 6))
                for n in range(2):
                    if n == 1:
                        pool.wait_ge(normed, (2 * l + 1) * G)
                    pool.dma_start(ln_g, A["ln_g"][l, n:n + 1, :].partition_broadcast(P)).then_inc(ln_in, 16)
                    pool.dma_start(ln_b, A["ln_b"][l, n:n + 1, :].partition_broadcast(P)).then_inc(ln_in, 16)
                    if n == 0:
                        pool.dma_start(rw, A["router_w"][l].rearrange("(p k) e -> p k e", k=KC)).then_inc(router_in, 16)
                        pool.dma_start(rb, A["router_b"][l:l + 1, :].partition_broadcast(P)).then_inc(router_in, 16)
                        nc.gpsimd.memset(ex_gate[:, 0, :], 1.0).then_inc(ones_set, 1)
                pool.wait_ge(gates_t_out, l + 1)
                pool.dma_start(gate_dram[l], gate_t).then_inc(gates_stored, 16)
                pool.wait_ge(gates_stored, 16 * (l + 1))

                def load_gate(t, slot):
                    if not (isinstance(t, int) and t < 4):
                        pool.wait_ge(h_ready, l * TURNS - 3 + t)
                    pool.dma_start(ex_gate[:, slot, :], gate_dram[l][bass.ds(t - 1, 1), :].partition_broadcast(P)) \
                        .then_inc(gate_loaded[slot], 16)

                for t in range(1, 5):
                    load_gate(t, t % 4)
                with pool.Fori(0, LOOPS) as i:
                    for j in range(4):
                        load_gate(5 + j + 4 * i, (5 + j) % 4)

            for g, y in enumerate((O["y_prompt"], O["y_sample"])):
                pool.wait_ge(normed, 3 * G + g + 1)
                pool.dma_start(y[0], x_tok[:, g, :]).then_inc(stored, 16)
            pool.wait_ge(stored, 16 * 8)

        @block.scalar
        def _(act):
            chain = [0]

            def link(ins):
                chain[0] += 1
                ins.then_inc(act_chain, 1)
                act.wait_ge(act_chain, chain[0])

            split = [0]

            def hi_main_of(u, slot, half, loaded):
                act.wait_ge(main_loaded[slot], loaded)
                if not isinstance(u, int) or u >= 2:
                    act.wait_ge(main_used, u - 1)
                nc.scalar.activation(hi_main[:, half, :], raw_main[:, slot, :], ACT.Copy).then_inc(main_hi, 1)

            def split_to(u):
                while split[0] <= u:
                    v = split[0]
                    hi_main_of(v, v % RAW, v % 2, LOADED[v])
                    split[0] += 1

            act.dma_start(const[:, :], A["shape_consts"][:, 0:KEPT_N]).then_inc(consts_in, 16)
            act.dma_start(cond[:, 0, :], A["c_ctx"].rearrange("(p k) -> p k", k=KC)).then_inc(cond_in, 16)
            act.dma_start(cond[:, 1, :], A["c"][0].rearrange("(p k) -> p k", k=KC)).then_inc(cond_in, 16)
            act.dma_start(x_tok[:, 0, :], A["x_prompt"][0]).then_inc(x_in, 16)
            act.dma_start(x_tok[:, 1, :], A["x_sample"][0]).then_inc(x_in, 16)
            act.dma_start(early, A["shape_consts"][:, KEPT_N:EARLY_END]).then_inc(early_in, 16)
            logit = decay[:, 0:12]
            flat = A["ret_decay_logit"].rearrange("a d h -> a (d h)")
            act.dma_start(logit[:, 0:8], flat.partition_broadcast(P)).then_inc(decay_in, 16)
            for d in range(2):
                act.dma_start(logit[d * DK:(d + 1) * DK, 8:12],
                              A["ret_decay_logit"][:, d].partition_broadcast(DK)).then_inc(decay_in, 16)
            act.wait_ge(cond_in, 32)
            nc.scalar.activation(cond_s[:, :, :], cond[:, :, :], ACT.Silu).then_inc(cond_ready, 1)

            act.wait_ge(decay_in, 48)
            act.wait_ge(consts_in, 16)
            link(nc.scalar.activation(decay[:, 12:24], logit, ACT.Abs))
            link(nc.scalar.activation(decay[:, 24:36], decay[:, 12:24], ACT.Exp, scale=-1.0))
            nc.scalar.activation(decay[:, 36:48], decay[:, 24:36], ACT.Ln, bias=K("one")).then_inc(decay_ready, 1)
            split_to(1)
            act.wait_ge(decay_ready, 2)
            act.wait_ge(early_in, 16)
            for d, rel in enumerate(("rel_f", "rel_b")):
                for h in range(H):
                    nc.scalar.activation(dec_e[:, d, h], E(rel), ACT.Exp,
                                         scale=decay[:, 48 + 4 * d + h:49 + 4 * d + h]).then_inc(decay_ready, 1)
            for h in range(H):
                nc.scalar.activation(q_pow[:, h], E("pos_row"), ACT.Exp, scale=decay[:, 56 + h:57 + h]) \
                    .then_inc(decay_ready, 1)
            act.wait_ge(decay_ready, 16)
            nc.scalar.activation(small[:, 0:8], small[:, 8:16], ACT.Exp).then_inc(decay_ready, 1)
            act.wait_ge(cache_t, 1)
            nc.scalar.activation(kc_t, ps[:, 7, :].rearrange("p (h t) -> p h t", h=H), ACT.Copy).then_inc(cache_t_out, 1)

            def make_x(l, n, shift, scale):
                act.wait_ge(mod_t_out, 4 * l + 2 * n + 2)
                act.wait_ge(xt_done, 2 * (2 * l + n) + 1)
                for k in range(KC):
                    ins = nc.scalar.activation(x_feat[:, k, 0:P], ps[:, k // 4, (k % 4) * P:(k % 4 + 1) * P], ACT.Identity,
                                               scale=mod_feat[:, scale, k, 0:1], bias=mod_feat[:, shift, k, 0:1])
                ins.then_inc(x_feat_act, 1)
                act.wait_ge(x_feat_act, 2 * l + n + 1)
                nc.scalar.activation(x_hi[:, :, 0:P], x_feat[:, :, 0:P], ACT.Copy).then_inc(x_hi_done, 1)
                act.wait_ge(x_feat_dve, 2 * l + n + 1)
                nc.scalar.activation(x_hi[:, :, P:TOK], x_feat[:, :, P:TOK], ACT.Copy).then_inc(x_hi_done, 1)

            def cat_hi(l):
                act.wait_ge(cat_ready, l + 1)
                nc.scalar.activation(x_hi[:, :, :], x_feat[:, :, :], ACT.Copy).then_inc(x_hi_done, 2)

            def unit_copy(l, n):
                u = in_unit(l, n)
                act.wait_ge(main_used, u + 1)
                bank = ps[:, 4 + u % 2, :]
                if l == 0 and n == 0:
                    act.wait_ge(k_dec_ready, 1)
                    b3 = bank.rearrange("p (t c) -> p t c", t=2)
                    for odd in range(2):
                        for half in range(2):
                            ins = nc.scalar.activation(q_dup[half * DK:(half + 1) * DK, odd::2, :],
                                                       b3[odd * DK:(odd + 1) * DK], ACT.Copy)
                    ins.then_inc(in_out, 1)
                elif l == 0 and n == 1:
                    b3 = bank.rearrange("p (t c) -> p t c", t=2)
                    for odd in range(2):
                        ins = nc.scalar.activation(k_low[:, odd::2, :], b3[odd * DK:(odd + 1) * DK], ACT.Copy,
                                                   scale=KEY_SCALE)
                    ins.then_inc(in_out, 1)
                elif l == 0:
                    nc.scalar.activation(proj[:, n + 2, :], bank, ACT.Silu if n in (4, 5) else ACT.Copy).then_inc(in_out, 1)
                else:
                    nc.scalar.activation(proj[:, n, :], bank, ACT.Copy).then_inc(in_out, 1)

            def softmax_exp(l):
                for n, s in enumerate((sc_ctx, sc_lat)):
                    act.wait_ge(centred, 2 * l + n + 1)
                    nc.scalar.activation(s, s, ACT.Exp).then_inc(exped, 1)

            def probs_copy(l, banks):
                for n in range(3):
                    act.wait_ge(probs_t, 3 * l + n + 1)
                    nc.scalar.activation(pr_t[:, n], ps[:, banks[n], :].rearrange("p (h t) -> p h t", h=H), ACT.Copy) \
                        .then_inc(probs_t_out, 1)

            def norm_sd(l, n):
                act.wait_ge(ln_in, 32 * (2 * l + n + 1))
                for g in range(G):
                    act.wait_ge(gates_mm, G * (2 * l + n) + g + 1)
                    nc.scalar.activation(z[:, g, :], ps[:, 4 + 2 * g:6 + 2 * g, :].rearrange("p a b -> p (a b)"), ACT.Copy) \
                        .then_inc(gate_copied, 1)
                for g in range(G):
                    act.wait_ge(ln_var, G * (2 * l + n) + g + 1)
                    nc.scalar.activation(small[:, 40 + g:41 + g], small[:, 33 + 2 * g:34 + 2 * g], ACT.Sqrt, bias=K("ln_eps")) \
                        .then_inc(ln_sd, 1)

            def experts(l):
                u0 = turn_unit(l, 0)

                def hi_down_of(t, slot, loaded):
                    act.wait_ge(down_loaded[slot], loaded)
                    if not (isinstance(t, int) and l * TURNS + t < 2):
                        act.wait_ge(down_used, l * TURNS - 1 + t)
                    nc.scalar.activation(hi_down[:, slot, :], raw_down[:, slot, :], ACT.Copy).then_inc(down_hi, 1)

                def silu_of(t, slot, bank):
                    act.wait_ge(main_used, u0 + 1 + t)
                    if not (isinstance(t, int) and l * TURNS + t < 2):
                        act.wait_ge(up_read, l * TURNS - 1 + t)
                    nc.scalar.activation(ex_silu[:, slot, :], ps[:, bank, 0:TOK], ACT.Silu).then_inc(silu_out, 1)

                def down_count(t):
                    return 16 * ((l * TURNS + t) // 2 + 1)

                def turn(t, j, extra=0):
                    b = pair(l, j - 1)
                    hi_down_of(t - 1, b, down_count(j - 1) + 8 * extra)
                    hi_main_of(u0 + t, (u0 + j) % RAW, (u0 + j) % 2, LOADED[u0 + j] + 8 * extra)
                    silu_of(t - 1, b, 4 + (u0 + j - 1) % 2)

                split_to(u0)
                for t in range(1, 5):
                    turn(t, t)
                with act.Fori(0, LOOPS) as i:
                    for j in range(4):
                        turn(5 + j + 4 * i, 5 + j, 4 * i)
                hi_down_of(TURNS - 1, pair(l, TURNS - 1), down_count(TURNS - 1))
                silu_of(TURNS - 1, pair(l, TURNS - 1), 4 + (u0 + TURNS - 1) % 2)
                split[0] = u0 + TURNS

            for l in range(DEPTH):
                split_to(mod_unit(l, FIRST_MODS - 1) + 2)
                make_x(l, 0, 0, 1)
                for n in range(IN_UNITS[l]):
                    split_to(in_unit(l, n) + 1)
                    unit_copy(l, n)
                split_to(in_unit(l, IN_UNITS[l] - 1) + 2)
                if l == 1:
                    act.wait_ge(in_out, in_before(1) + 9)
                    nc.scalar.activation(sq, proj[:, 6:9, :].rearrange("p a (b c) -> p (a b) c", b=4), ACT.Square) \
                        .then_inc(sq_ready, 1)
                    act.wait_ge(ms_ready, 1)
                    nc.scalar.activation(small[:, 80:92], small[:, 92:104], ACT.Sqrt, scale=1.0 / P, bias=K("rms_eps")) \
                        .then_inc(rms_ready, 1)
                    for n in range(4):
                        act.wait_ge(qk_tr, n + 1)
                        first, count = ((0, 4), (4, 2), (6, 4), (10, 2))[n]
                        nc.scalar.activation(qk_t[:, first:first + count],
                                             ps[:, n, 0:count * P].rearrange("p (h t) -> p h t", h=count), ACT.Copy) \
                            .then_inc(qk_t_out, 1)
                    act.wait_ge(cache_t, 2)
                    nc.scalar.activation(kc_t1, ps[:, 7, 0:KVH * P].rearrange("p (h t) -> p h t", h=KVH), ACT.Copy) \
                        .then_inc(cache_t_out, 1)
                softmax_exp(l)
                split_to(mod_unit(l, 15) + 2)
                if l == 0:
                    act.wait_ge(ret_var, 1)
                    nc.scalar.activation(small[:, 16:24], small[:, 24:32], ACT.Sqrt, bias=K("ln_eps")).then_inc(ret_sd, 1)
                probs_copy(l, (0, 1, 2) if l == 0 else (6, 7, 0))
                split_to(mod_unit(l, 19) + 2)
                if l == 0:
                    act.wait_ge(kn_t, 1)
                    nc.scalar.activation(k_out, ps[:, 2, :].rearrange("p (h t) -> p h t", h=H), ACT.Copy).then_inc(kn_out, 1)
                split_to(mod_unit(l, 23) + 2)
                cat_hi(l)
                split_to(out_unit(l, OUT_UNITS - 1) + 1)
                norm_sd(l, 0)
                make_x(l, 1, 2, 3)
                act.wait_ge(logits, l + 1)
                nc.scalar.activation(score, ps[:, 6, 0:G * EXPERTS], ACT.Sigmoid).then_inc(sigmoid_out, 1)
                experts(l)
                norm_sd(l, 1)

        @block.vector
        def _(dve):
            chain = [0]
            V = nc.vector

            def link(ins):
                chain[0] += 1
                ins.then_inc(dve_chain, 1)
                dve.wait_ge(dve_chain, chain[0])

            split = [0]

            def lo_main_of(u, slot, half):
                dve.wait_ge(main_hi, u + 1)
                V.tensor_tensor(lo_main[:, half, :], raw_main[:, slot, :], hi_main[:, half, :].bitcast(F32), ALU.subtract) \
                    .then_inc(main_lo, 1)

            def split_to(u):
                while split[0] <= u:
                    lo_main_of(split[0], split[0] % RAW, split[0] % 2)
                    split[0] += 1

            def along(ap, n):
                return ap.unsqueeze(2).broadcast_to([ap.shape[0], ap.shape[1], n])

            def over(ap, n):
                return ap.unsqueeze(1).broadcast_to([ap.shape[0], n, ap.shape[1]])

            def mod_row_out(l, n):
                u, sec, at = mod_unit(l, n), n // SEC, l * MOD_UNITS + n
                cols = slice((n % SEC) * UNIT, (n % SEC + 1) * UNIT)
                out = gate_row[:, sec // 3, cols] if sec % 3 == 2 else mod_row[:, cols]
                dve.wait_ge(main_used, u + 1)
                dve.wait_ge(bias_loaded[at % RAW], 16 * (at // RAW + 1))
                src = ps[0:2 * G, 4 + u % 2, 0:UNIT]
                if sec % 3 == 0:
                    V.tensor_tensor(out, src, b_rows[:, at % RAW, :], ALU.add).then_inc(mod_rows_out, 1)
                else:
                    V.scalar_tensor_tensor(out=out, in0=src, scalar=K("plus", 2 * G), in1=b_rows[:, at % RAW, :],
                                           op0=ALU.add, op1=ALU.add).then_inc(mod_rows_out, 1)
                if sec % 3 < 2 and n % SEC == SEC - 1:
                    s = (0, 1, None, 2, 3)[sec]
                    dve.wait_ge(mod_t, 4 * l + s + 1)
                    V.tensor_copy(mod_feat[:, s].rearrange("p k g -> p (k g)"), ps[:, 4 + (u + 1) % 2, 0:KC * G]) \
                        .then_inc(mod_t_out, 1)

            def mods(l, first, count):
                for n in range(first, first + count):
                    split_to(mod_unit(l, n) + 1)
                    mod_row_out(l, n)

            def make_x(l, n, shift, scale):
                dve.wait_ge(mod_t_out, 4 * l + 2 * n + 2)
                dve.wait_ge(xt_done, 2 * (2 * l + n) + 2)
                for k in range(KC):
                    ins = V.tensor_scalar(x_feat[:, k, P:TOK], ps[:, 2 + k // 4, (k % 4) * P:(k % 4 + 1) * P],
                                          mod_feat[:, scale, k, 1:2], mod_feat[:, shift, k, 1:2], ALU.mult, ALU.add)
                ins.then_inc(x_feat_dve, 1)
                for g in range(G):
                    dve.wait_ge(x_hi_done, 2 * (3 * l + 2 * n) + g + 1)
                    V.tensor_tensor(x_lo[:, :, g * P:(g + 1) * P], x_feat[:, :, g * P:(g + 1) * P],
                                    x_hi[:, :, g * P:(g + 1) * P].bitcast(F32), ALU.subtract).then_inc(x_lo_done, 1)

            def cat_lo(l):
                dve.wait_ge(x_hi_done, 2 * (3 * l + 2))
                V.tensor_tensor(x_lo[:, :, :], x_feat[:, :, :], x_hi[:, :, :].bitcast(F32), ALU.subtract) \
                    .then_inc(x_lo_done, 2)

            def centre(s, keys):
                mx = small[:, 104:108] if keys == P else small[:, 152:156]
                link(V.tensor_reduce(mx, s, AX.X, ALU.max))
                V.tensor_tensor(s, s, along(mx, keys), ALU.subtract).then_inc(centred, 1)

            def normalise(s, keys, n):
                den = small[:, 108:112] if keys == P else small[:, 156:160]
                dve.wait_ge(exped, n)
                link(V.tensor_reduce(den, s, AX.X, ALU.add))
                link(V.reciprocal(den, den))
                V.tensor_tensor(s, s, along(den, keys), ALU.mult).then_inc(probs, 1)

            def softmax_in(l, banks):
                dve.wait_ge(scores, 2 * l + 1)
                link(V.tensor_scalar(sc_ctx, ps[:, banks[0], :].rearrange("p (h t) -> p h t", h=H), ATT_SCALE, None, ALU.mult))
                centre(sc_ctx, P)
                dve.wait_ge(scores, 2 * l + 2)
                own = ps[:, banks[1], :].rearrange("p (h t) -> p h t", h=H)
                if l == 0:
                    link(V.scalar_tensor_tensor(out=sc_lat[:, :, 0:P], in0=own, scalar=ATT_SCALE,
                                                in1=bias.rearrange("p h a c -> p h (a c)"), op0=ALU.mult, op1=ALU.add))
                else:
                    link(V.tensor_scalar(sc_lat[:, :, 0:P], own, ATT_SCALE, None, ALU.mult))
                link(V.tensor_scalar(sc_lat[:, :, P:2 * P], ps[:, banks[2], :].rearrange("p (h t) -> p h t", h=H),
                                     ATT_SCALE, None, ALU.mult))
                centre(sc_lat, 2 * P)

            def att_out(l, n, bank):
                dve.wait_ge(att_o, G * l + n + 1)
                link(V.tensor_copy(x_feat[:, H:2 * H, n * P:(n + 1) * P], ps[:, bank, :].rearrange("p (h t) -> p h t", h=H)))

            def post_norm(l, n):
                dve.wait_ge(ln_in, 32 * (2 * l + n + 1))
                for g in range(G):
                    dve.wait_ge(gate_copied, G * (2 * l + n) + g + 1)
                    zg = z[:, g, :]
                    if n == 0:
                        y = ps[:, 0:4, g * UNIT:(g + 1) * UNIT]
                        zv = zg.rearrange("p (a b) -> p a b", b=UNIT)
                    else:
                        y = ps[:, 2 * g:2 * g + 2, :]
                        zv = zg.rearrange("p (a b) -> p a b", b=512)
                    link(V.tensor_tensor(zv, zv, y, ALU.mult))
                    link(V.scalar_tensor_tensor(out=zg, in0=x_tok[:, g, :], scalar=ALPHA, in1=zg, op0=ALU.mult, op1=ALU.add))
                    stats = small[:, 112 + 48 * g:124 + 48 * g]
                    V.bn_stats(stats[:, 0:6], zg[:, 0:512])
                    link(V.bn_stats(stats[:, 6:12], zg[:, 512:1024]))
                    V.bn_aggr(small[:, 32 + 2 * g:34 + 2 * g], stats).then_inc(ln_var, 1)
                    dve.wait_ge(ln_var, G * (2 * l + n) + g + 1)
                for g in range(G):
                    zg = z[:, g, :]
                    dve.wait_ge(ln_sd, G * (2 * l + n) + g + 1)
                    link(V.reciprocal(small[:, 42 + g:43 + g], small[:, 40 + g:41 + g]))
                    link(V.scalar_tensor_tensor(out=zg, in0=zg, scalar=small[:, 32 + 2 * g:33 + 2 * g], in1=ln_g,
                                                op0=ALU.subtract, op1=ALU.mult))
                    V.scalar_tensor_tensor(out=x_tok[:, g, :], in0=zg, scalar=small[:, 42 + g:43 + g], in1=ln_b,
                                           op0=ALU.mult, op1=ALU.add).then_inc(normed, 1)

            def route(l):
                dve.wait_ge(router_in, 32 * (l + 1))
                dve.wait_ge(sigmoid_out, l + 1)
                sel3 = select.rearrange("p (g e) -> p g e", g=G)
                link(V.tensor_tensor(sel3, score.rearrange("p (g e) -> p g e", g=G), over(rb, G), ALU.add))
                for n in range(G * GROUPS):
                    ins = V.max(top[:, n], select[:, n * PER_GROUP:(n + 1) * PER_GROUP])
                link(ins)
                link(V.tensor_tensor(gscore, top[:, :, 0], top[:, :, 1], ALU.add))
                for g in range(G):
                    ins = V.max(top4[:, g], gscore[:, g * GROUPS:(g + 1) * GROUPS])
                link(ins)
                link(V.memset(top4[:, :, TOPK_GROUPS:GROUPS], GONE / 2))
                for g in range(G):
                    ins = V.match_replace(gtaken[:, g * GROUPS:(g + 1) * GROUPS], top4[:, g],
                                          gscore[:, g * GROUPS:(g + 1) * GROUPS], GONE)
                link(ins)
                link(V.tensor_tensor(gmask, gtaken, gscore, ALU.not_equal))
                link(V.tensor_scalar(gpen, gmask, -LOW, LOW, ALU.mult, ALU.add))
                gsel3 = gsel.rearrange("p (a b) -> p a b", b=PER_GROUP)
                link(V.tensor_tensor(gsel3, select.rearrange("p (a b) -> p a b", b=PER_GROUP), along(gmask, PER_GROUP), ALU.mult))
                link(V.tensor_tensor(gsel3, gsel3, along(gpen, PER_GROUP), ALU.add))
                for g in range(G):
                    ins = V.max(top8[:, g], gsel[:, g * EXPERTS:(g + 1) * EXPERTS])
                link(ins)
                for g in range(G):
                    ins = V.match_replace(taken[:, g * EXPERTS:(g + 1) * EXPERTS], top8[:, g],
                                          gsel[:, g * EXPERTS:(g + 1) * EXPERTS], GONE)
                link(ins)
                link(V.tensor_tensor(taken, taken, gsel, ALU.not_equal))
                link(V.tensor_tensor(taken, taken, score, ALU.mult))
                taken3 = taken.rearrange("p (g e) -> p g e", g=G)
                link(V.tensor_reduce(wsum, taken3, AX.X, ALU.add))
                link(V.reciprocal(wsum, wsum))
                link(V.tensor_tensor(taken3, taken3, along(wsum, EXPERTS), ALU.mult))
                V.tensor_scalar(taken, taken, ROUTED_SCALE, None, ALU.mult).then_inc(gates_made, 1)
                dve.wait_ge(gates_t, l + 1)
                V.tensor_copy(gate_t, ps[0:EXPERTS, 7, 0:TOK]).then_inc(gates_t_out, 1)

            def experts(l):
                u0 = turn_unit(l, 0)

                def lo_down_of(t, slot):
                    dve.wait_ge(down_hi, l * TURNS + 1 + t)
                    V.tensor_tensor(lo_down[:, slot, :], raw_down[:, slot, :], hi_down[:, slot, :].bitcast(F32), ALU.subtract) \
                        .then_inc(down_lo, 1)

                def hidden_of(t, slot, bank, gslot, gate_count):
                    done = l * TURNS + 1 + t
                    dve.wait_ge(silu_out, done)
                    V.tensor_tensor(ex_up[:, slot, :], ex_silu[:, slot, :], ps[:, bank, TOK:2 * TOK], ALU.mult).then_inc(up_read, 1)
                    dve.wait_ge(up_read, done)
                    if gate_count is None:
                        dve.wait_ge(ones_set, l + 1)
                    else:
                        dve.wait_ge(gate_loaded[gslot], gate_count)
                    V.tensor_tensor(ex_h[:, slot, :], ex_up[:, slot, :], ex_gate[:, gslot, :], ALU.mult).then_inc(h_ready, 1)
                    dve.wait_ge(h_ready, done)
                    if not (isinstance(t, int) and l * TURNS + t < 2):
                        dve.wait_ge(down_used, l * TURNS - 1 + t)
                    V.tensor_copy(hid_hi[:, slot, :], ex_h[:, slot, :]).then_inc(h_hi, 1)
                    dve.wait_ge(h_hi, done)
                    V.tensor_tensor(hid_lo[:, slot, :], ex_h[:, slot, :], hid_hi[:, slot, :].bitcast(F32), ALU.subtract) \
                        .then_inc(h_lo, 1)

                def gate_count(t):
                    return None if t == 0 else 16 * (l * (EXPERTS // 4) + (t + 3) // 4)

                def turn(t, j, extra=0):
                    b = pair(l, j - 1)
                    lo_down_of(t - 1, b)
                    lo_main_of(u0 + t, (u0 + j) % RAW, (u0 + j) % 2)
                    c = gate_count(j - 1)
                    hidden_of(t - 1, b, 4 + (u0 + j - 1) % 2, (j - 1) % 4, None if c is None else c + 4 * extra)

                for t in range(1, 5):
                    turn(t, t)
                with dve.Fori(0, LOOPS) as i:
                    for j in range(4):
                        turn(5 + j + 4 * i, 5 + j, 4 * i)
                last = TURNS - 1
                lo_down_of(last, pair(l, last))
                hidden_of(last, pair(l, last), 4 + (u0 + last) % 2, last % 4, gate_count(last))
                split[0] = u0 + TURNS

            link(V.memset(cond_parts[:, :, :].bitcast(F32), 0.0))
            dve.wait_ge(cond_ready, 1)
            cs = cond_s[:, :, :].rearrange("p g k -> p k g")
            link(V.tensor_copy(cond_parts[:, :, 0:G], cs))
            V.tensor_tensor(cond_parts[:, :, G:2 * G], cs, cond_parts[:, :, 0:G].bitcast(F32), ALU.subtract).then_inc(cond_ready, 1)
            dve.wait_ge(decay_ready, 1)
            link(V.tensor_scalar(decay[:, 48:60], decay[:, 0:12], 0.0, None, ALU.min))
            V.tensor_tensor(decay[:, 48:60], decay[:, 48:60], decay[:, 36:48], ALU.subtract).then_inc(decay_ready, 1)
            dve.wait_ge(decay_ready, 2)
            dve.wait_ge(early_in, 16)
            for d in range(2):
                ins = V.tensor_scalar(small[:, 8 + 4 * d:12 + 4 * d], decay[:, 48 + 4 * d:52 + 4 * d], E("pos_col")[:, d:d + 1],
                                      None, ALU.mult)
                ins.then_inc(decay_ready, 1)
            split_to(1)
            dve.wait_ge(decay_ready, 16)
            for d, mask in enumerate(("mask_f", "mask_b")):
                ins = V.tensor_tensor(dec_e[:, d], dec_e[:, d], over(E(mask), H), ALU.mult)
            link(ins)
            link(V.tensor_tensor(dmat, dec_e[:, 0], dec_e[:, 1], ALU.add))
            dve.wait_ge(decay_ready, 17)
            V.memset(small[:, 48:49], 0.0).then_inc(k_dec_ready, 1)
            dve.wait_ge(consts_in, 16)
            dve.wait_ge(pad_zero, 2)

            for l in range(DEPTH):
                mods(l, 0, FIRST_MODS)
                make_x(l, 0, 0, 1)
                split_to(in_unit(l, IN_UNITS[l] - 1) + 2)
                if l == 0:
                    dve.wait_ge(in_out, 1)
                    link(V.tensor_tensor(q_dec, q_dup[:, :, P:TOK], q_pow, ALU.mult))
                    dve.wait_ge(att_s, 1)
                    for par in range(2):
                        for g in range(G):
                            ins = V.tensor_tensor(att_d[:, par, g],
                                                  ps[:, 6 + par, g * 2 * P:(g + 1) * 2 * P].rearrange("p (h t) -> p h t", h=2),
                                                  dmat[:, par::2, :], ALU.mult)
                    ins.then_inc(att_d_ready, 1)
                    dve.wait_ge(k_t, 1)
                    kt = ps[:, 3, 0:H * DK].rearrange("p (h d) -> p h d", h=H)
                    for d in range(2):
                        ins = V.tensor_tensor(k_dec[:, :, d, :], kt, along(small[:, 4 * d:4 * d + 4], DK), ALU.mult)
                    ins.then_inc(k_dec_ready, 1)
                    dve.wait_ge(bias_in, 16 * 2 * H)
                    bias3 = bias.rearrange("p h a c -> p h (a c)")
                    link(V.tensor_tensor(bias3, bias3, over(K("window"), H), ALU.add))
                    softmax_in(0, (0, 1, 2))
                else:
                    qk = proj[:, 6:9, :].rearrange("p a (b c) -> p (a b) c", b=4)
                    dve.wait_ge(sq_ready, 1)
                    V.tensor_reduce(small[:, 92:104], sq, AX.X, ALU.add).then_inc(ms_ready, 1)
                    dve.wait_ge(small_in, 80)
                    dve.wait_ge(rms_ready, 1)
                    link(V.reciprocal(small[:, 124:136], small[:, 80:92]))
                    link(V.tensor_tensor(qk, qk, along(small[:, 124:136], P), ALU.mult))
                    V.tensor_tensor(qk[:, 0:8], qk[:, 0:8], over(gains[:, 0], 8), ALU.mult).then_inc(qk_normed, 1)
                    V.tensor_tensor(qk[:, 8:12], qk[:, 8:12], over(gains[:, 1], 4), ALU.mult).then_inc(qk_normed, 1)
                    dve.wait_ge(qk_normed, 2)
                    lat = proj[:, 6:9, UNIT:2 * UNIT].rearrange("p a (b c e) -> p a b c e", b=2, e=2)
                    ro = roped.rearrange("p (a b) (c e) -> p a b c e", b=2, e=2)
                    tmp = sq.rearrange("p h t -> p (h t)")
                    t1 = tmp[:, 0:384].rearrange("p (a b c) -> p a b c", a=3, b=2)
                    t2 = tmp[:, 384:768].rearrange("p (a b c) -> p a b c", a=3, b=2)

                    def ang(x):
                        return x.unsqueeze(1).unsqueeze(1).broadcast_to([P, 3, 2, P // 2])

                    V.tensor_tensor(ro[:, :, :, :, 0], lat[:, :, :, :, 0], ang(K("cos")), ALU.mult)
                    V.tensor_tensor(ro[:, :, :, :, 1], lat[:, :, :, :, 0], ang(K("sin")), ALU.mult)
                    V.tensor_tensor(t1, lat[:, :, :, :, 1], ang(K("sin")), ALU.mult)
                    link(V.tensor_tensor(t2, lat[:, :, :, :, 1], ang(K("cos")), ALU.mult))
                    V.tensor_tensor(ro[:, :, :, :, 0], ro[:, :, :, :, 0], t1, ALU.subtract)
                    V.tensor_tensor(ro[:, :, :, :, 1], ro[:, :, :, :, 1], t2, ALU.add).then_inc(roped_ready, 1)
                    softmax_in(1, (6, 7, 0))
                    dve.wait_ge(qk_tr, 4)
                    cg = proj[:, 2:4, :].rearrange("p a (b c) -> p (a b) c", b=4)
                    ug = proj[:, 4:6, :].rearrange("p a (b c) -> p (a b) c", b=4)
                    link(V.memset(z_pad, 0.0))
                    link(V.tensor_tensor(z_pad[:, :, 1:P + 1], cg, ug, ALU.mult))
                    for w in range(3):
                        for t in range(4):
                            zi = z_pad[:, 2 * t:2 * t + 2, w:w + P]
                            if w == 0:
                                ins = V.tensor_scalar(conv_o[:, t], zi, cv_w[:, w, t:t + 1], None, ALU.mult)
                            else:
                                ins = V.scalar_tensor_tensor(out=conv_o[:, t], in0=zi, scalar=cv_w[:, w, t:t + 1],
                                                             in1=conv_o[:, t], op0=ALU.mult, op1=ALU.add)
                        link(ins)
                    bg = proj[:, 0:2, :].rearrange("p a (b c) -> p (a b) c", b=2)
                    link(V.tensor_tensor(x_feat[:, 0:4, :], bg, conv_o.rearrange("p t g n -> p t (g n)"), ALU.mult))
                mods(l, 8, 4)
                normalise(sc_ctx, P, 2 * l + 1)
                normalise(sc_lat, 2 * P, 2 * l + 2)
                if l == 0:
                    dve.wait_ge(state_mm, 1)
                    V.tensor_copy(st_out, ps[:, 3, :].rearrange("p (h v) -> p h v", h=H)).then_inc(state_copied, 1)
                mods(l, 12, 4)
                if l == 0:
                    stats = decay.rearrange("p (n c) -> p n c", c=6)
                    for g in range(G):
                        dve.wait_ge(ret_o, g + 1)
                        for h in range(H):
                            ins = V.bn_stats(stats[:, 4 * g + h], ps[:, 6 + g, h * P:(h + 1) * P])
                    link(ins)
                    for n in range(G * H):
                        ins = V.bn_aggr(small[:, 136 + 2 * n:138 + 2 * n], stats[:, n])
                    link(ins)
                    mv = small[:, 136:152].rearrange("p (n c) -> p n c", c=2)
                    V.tensor_copy(small[:, 24:32], mv[:, :, 1]).then_inc(ret_var, 1)
                    dve.wait_ge(ret_sd, 1)
                    link(V.reciprocal(small[:, 50:58], small[:, 16:24]))
                    for g in range(G):
                        for h in range(H):
                            ins = V.scalar_tensor_tensor(out=even_gate(h, g), in0=ps[:, 6 + g, h * P:(h + 1) * P],
                                                         scalar=mv[:, 4 * g + h, 0:1], in1=even_gate(h, g),
                                                         op0=ALU.subtract, op1=ALU.mult)
                    link(ins)
                    for g in range(G):
                        for h in range(H):
                            ins = V.tensor_scalar(even_gate(h, g), even_gate(h, g), small[:, 50 + 4 * g + h:51 + 4 * g + h], None,
                                                  ALU.mult)
                    ins.then_inc(ret_ready, 1)
                mods(l, 16, 4)
                att_out(l, 0, 3 if l == 0 else 1)
                att_out(l, 1, 0 if l == 0 else 2)
                if l == 0:
                    for g in range(G):
                        dve.wait_ge(ret_t, g + 1)
                        link(V.tensor_copy(x_feat[:, 0:H, g * P:(g + 1) * P], ps[:, 6 + g, :].rearrange("p (h t) -> p h t", h=H)))
                V.memset(small[:, 48:49], 0.0).then_inc(cat_ready, 1)
                mods(l, 20, 4)
                cat_lo(l)
                split_to(out_unit(l, OUT_UNITS - 1) + 1)
                post_norm(l, 0)
                make_x(l, 1, 2, 3)
                route(l)
                experts(l)
                post_norm(l, 1)

        @block.tensor
        def _(pe):
            def mm(out, w, x, start, stop):
                return nc.tensor.matmul(out, w, x, start=start, stop=stop)

            def turned(out, x, ident=None):
                return nc.tensor.transpose(out, x, K("ident") if ident is None else ident)

            def parts(out, pairs, first=True, last=True):
                n = len(pairs)
                for i, (w, x) in enumerate(pairs):
                    ins = mm(out, w, x, first and i == 0, last and i == n - 1)
                return ins

            def bank_free(u):
                kind, l, n = KIND.get(u - 2, ("none", 0, 0))
                if kind == "mod":
                    pe.wait_ge(mod_rows_out, l * MOD_UNITS + n + 1)
                if kind == "in":
                    pe.wait_ge(in_out, in_before(l) + n + 1)
                kind, l, n = KIND.get(u - 1, ("none", 0, 0))
                if kind == "mod" and n % SEC == SEC - 1 and n // SEC % 3 < 2:
                    pe.wait_ge(mod_t_out, 4 * l + (0, 1, 0, 2, 3)[n // SEC] + 1)

            def mod(l, n):
                u, sec = mod_unit(l, n), n // SEC
                bank_free(u)
                if u == 0:
                    pe.wait_ge(cond_ready, 2)
                out = ps[:, 4 + u % 2, 0:UNIT]
                w = [t[:, u % 2, :].rearrange("p (k n) -> p k n", k=KC) for t in (hi_main, lo_main)]
                pe.wait_ge(main_hi, u + 1)
                for k in range(KC):
                    mm(out, cond_parts[:, k, :], w[0][:, k], k == 0, False)
                pe.wait_ge(main_lo, u + 1)
                for k in range(KC):
                    ins = mm(out, cond_parts[:, k, :], w[1][:, k], False, k == KC - 1)
                ins.then_inc(main_used, 1)
                if sec % 3 < 2 and n % SEC == SEC - 1:
                    pe.wait_ge(mod_rows_out, l * MOD_UNITS + n + 1)
                    rows = mod_row[:, :].rearrange("r (p k) -> r k p", k=KC)
                    for k in range(KC):
                        ins = mm(ps[:, 4 + (u + 1) % 2, G * k:G * k + G], rows[:, k], K("fold", 2 * G), True, True)
                    ins.then_inc(mod_t, 1)

            def mods(l, first, count):
                for n in range(first, first + count):
                    mod(l, n)

            def x_turned(l, n):
                for g in range(G):
                    if l == 0 and n == 0:
                        pe.wait_ge(x_in, 32)
                    else:
                        pe.wait_ge(normed, G * (2 * l + n - 1) + g + 1)
                    v = x_tok[:, g, :].rearrange("p (m k) -> p k m", k=KC)
                    for k in range(KC):
                        ins = turned(ps[:, 2 * g + k // 4, (k % 4) * P:(k % 4 + 1) * P], v[:, k])
                    ins.then_inc(xt_done, 1)

            def x_parts_ready(l, n):
                pe.wait_ge(x_hi_done, 2 * (3 * l + n + 1))
                pe.wait_ge(x_lo_done, 2 * (3 * l + n + 1))

            def by_features(u, bank):
                w = [t[:, u % 2, :].rearrange("p (k n) -> p k n", k=KC) for t in (hi_main, lo_main)]
                for t in range(2):
                    c = slice(t * P, (t + 1) * P)
                    if t == 0:
                        pe.wait_ge(main_hi, u + 1)
                    hh = [(w[0][:, k, c], x_hi[:, k, :]) for k in range(KC)] + [(w[0][:, k, c], x_lo[:, k, :]) for k in range(KC)]
                    lh = [(w[1][:, k, c], x_hi[:, k, :]) for k in range(KC)]
                    parts(ps[:, bank, t * TOK:(t + 1) * TOK], hh, last=False)
                    if t == 0:
                        pe.wait_ge(main_lo, u + 1)
                    ins = parts(ps[:, bank, t * TOK:(t + 1) * TOK], lh, first=False)
                ins.then_inc(main_used, 1)

            def by_tokens(u, bank):
                w = [t[:, u % 2, :].rearrange("p (k n) -> p k n", k=KC) for t in (hi_main, lo_main)]
                for g in range(G):
                    c = slice(g * P, (g + 1) * P)
                    if g == 0:
                        pe.wait_ge(main_hi, u + 1)
                    hh = [(x_hi[:, k, c], w[0][:, k]) for k in range(KC)] + [(x_lo[:, k, c], w[0][:, k]) for k in range(KC)]
                    hl = [(x_hi[:, k, c], w[1][:, k]) for k in range(KC)]
                    parts(ps[:, bank, g * UNIT:(g + 1) * UNIT], hh, last=False)
                    if g == 0:
                        pe.wait_ge(main_lo, u + 1)
                    ins = parts(ps[:, bank, g * UNIT:(g + 1) * UNIT], hl, first=False)
                ins.then_inc(main_used, 1)

            def head(bank, h, width=P):
                return ps[:, bank, h * width:(h + 1) * width]

            def probs_turned(l, banks):
                pe.wait_ge(probs, 2 * l + 1)
                for h in range(H):
                    ins = turned(head(banks[0], h), sc_ctx[:, h])
                ins.then_inc(probs_t, 1)
                pe.wait_ge(probs, 2 * l + 2)
                for n in range(2):
                    for h in range(H):
                        ins = turned(head(banks[1 + n], h), sc_lat[:, h, n * P:(n + 1) * P])
                    ins.then_inc(probs_t, 1)

            def attended(l, values, cached, banks):
                pe.wait_ge(probs_t_out, 3 * l + 1)
                for h in range(H):
                    ins = mm(head(banks[0], h), values(h, 0), pr_t[:, 0, h], True, True)
                ins.then_inc(att_o, 1)
                pe.wait_ge(probs_t_out, 3 * l + 3)
                pe.wait_ge(cache_v_in, 16 * (l + 1))
                for h in range(H):
                    mm(head(banks[1], h), values(h, 1), pr_t[:, 1, h], True, False)
                    ins = mm(head(banks[1], h), cached(h), pr_t[:, 2, h], False, True)
                ins.then_inc(att_o, 1)

            def gates_spread(l, n):
                for g in range(G):
                    sel = K("pick", 2 * G)[:, g * P:(g + 1) * P]
                    for c in range(2):
                        ins = mm(ps[:, 4 + 2 * g + c, :], sel, gate_row[:, n, c * 512:(c + 1) * 512], True, True)
                    ins.then_inc(gates_mm, 1)

            def experts(l):
                u0 = turn_unit(l, 0)

                def gate_up(u, half, bank):
                    w = [t[:, half, :].rearrange("p (k w n) -> p w k n", k=KC, w=2) for t in (hi_main, lo_main)]
                    pe.wait_ge(main_hi, u + 1)
                    for i in range(2):
                        out = ps[:, bank, i * TOK:(i + 1) * TOK]
                        hh = [(w[0][:, i, k], x_hi[:, k, :]) for k in range(KC)] + [(w[0][:, i, k], x_lo[:, k, :]) for k in range(KC)]
                        lh = [(w[1][:, i, k], x_hi[:, k, :]) for k in range(KC)]
                        parts(out, hh, last=False)
                        if i == 0:
                            pe.wait_ge(main_lo, u + 1)
                        ins = parts(out, lh, first=False)
                    ins.then_inc(main_used, 1)

                def down(t, slot, first, last):
                    done = l * TURNS + 1 + t
                    pe.wait_ge(down_hi, done)
                    pe.wait_ge(down_lo, done)
                    pe.wait_ge(h_hi, done)
                    pe.wait_ge(h_lo, done)
                    for g in range(G):
                        hh, hl = (x[:, slot, g * P:(g + 1) * P] for x in (hid_hi, hid_lo))
                        for c in range(2):
                            wh, wl = (x[:, slot, c * 512:(c + 1) * 512] for x in (hi_down, lo_down))
                            ins = parts(ps[:, 2 * g + c, :], [(hh, wh), (hh, wl), (hl, wh)], first=first, last=last)
                    ins.then_inc(down_used, 1)

                def turn(t, j):
                    gate_up(u0 + t, (u0 + j) % 2, 4 + (u0 + j) % 2)
                    down(t - 1, pair(l, j - 1), j == 1, False)

                gate_up(u0, u0 % 2, 4 + u0 % 2)
                for t in range(1, 5):
                    turn(t, t)
                with pe.Fori(0, LOOPS) as i:
                    for j in range(4):
                        turn(5 + j + 4 * i, 5 + j)
                down(TURNS - 1, pair(l, TURNS - 1), False, True)

            pe.wait_ge(consts_in, 16)
            pe.wait_ge(cache_k_in, 16)
            for h in range(H):
                ins = turned(head(7, h), kc_in[:, h])
            ins.then_inc(cache_t, 1)

            for l in range(DEPTH):
                mods(l, 0, FIRST_MODS)
                x_turned(l, 0)
                x_parts_ready(l, 0)
                for n in range(IN_UNITS[l]):
                    u = in_unit(l, n)
                    bank_free(u)
                    feat = n in (0, 1, 6, 7, 8, 9) if l == 0 else n < 6
                    (by_features if feat else by_tokens)(u, 4 + u % 2)
                pe.wait_ge(in_out, in_before(l) + IN_UNITS[l])
                if l == 0:
                    pe.wait_ge(cache_t_out, 1)
                    for h in range(H):
                        for g in range(G):
                            at = (2 * g + h // 2) * P
                            ins = mm(ps[:, 6 + h % 2, at:at + P], k_low[:, h, g * P:(g + 1) * P],
                                     q_dup[0:DK, h, g * P:(g + 1) * P], True, True)
                    ins.then_inc(att_s, 1)
                    for h in range(H):
                        ins = turned(head(3, h, DK), k_low[:, h, 0:P], K("ident", DK)[:, 0:DK])
                    ins.then_inc(k_t, 1)
                    for h in range(H):
                        ins = mm(head(0, h), na_q(h, 0), na_k(h, 0), True, True)
                    ins.then_inc(scores, 1)
                    for h in range(H):
                        mm(head(1, h), na_q(h, 1), na_k(h, 1), True, True)
                    for h in range(H):
                        ins = mm(head(2, h), na_q(h, 1), kc_t[:, h], True, True)
                    ins.then_inc(scores, 1)
                    mods(l, 8, 4)
                    pe.wait_ge(k_dec_ready, 2)
                    for h in range(H):
                        ins = mm(head(3, h), k_dec[:, h].rearrange("p d k -> p (d k)"), even_v(h, 0), True, True)
                    ins.then_inc(state_mm, 1)
                    pe.wait_ge(att_d_ready, 1)
                    pe.wait_ge(state_in, 32)
                    for g in range(G):
                        for h in range(H):
                            ins = mm(head(6 + g, h), att_d[:, h % 2, g, h // 2], even_v(h, g), True, g == 0)
                            if g == 1:
                                ins = mm(head(6 + g, h), q_dec[:, h], s0[:, h], False, True)
                        ins.then_inc(ret_o, 1)
                    mods(l, 12, 4)
                    probs_turned(l, (0, 1, 2))
                    mods(l, 16, 4)
                    pe.wait_ge(state_copied, 1)
                    attended(l, na_v, lambda h: vc[:, h], (3, 0))
                    pe.wait_ge(ret_ready, 1)
                    for g in range(G):
                        for h in range(H):
                            ins = turned(head(6 + g, h), even_gate(h, g))
                        ins.then_inc(ret_t, 1)
                    for h in range(H):
                        ins = turned(head(2, h), na_k(h, 0))
                    ins.then_inc(kn_t, 1)
                else:
                    pe.wait_ge(qk_normed, 2)
                    for n in range(6):
                        ins = turned(head(0 if n < 4 else 1, n % 4), proj[:, 6 + n // 2, (n % 2) * P:(n % 2) * P + P])
                        if n in (3, 5):
                            ins.then_inc(qk_tr, 1)
                    pe.wait_ge(roped_ready, 1)
                    for n in range(6):
                        ins = turned(head(2 if n < 4 else 3, n % 4), roped[:, n])
                        if n in (3, 5):
                            ins.then_inc(qk_tr, 1)
                    pe.wait_ge(cache_k_in, 32)
                    for h in range(KVH):
                        ins = turned(head(7, h), kc_in1[:, h])
                    ins.then_inc(cache_t, 1)
                    pe.wait_ge(qk_t_out, 4)
                    for h in range(H):
                        ins = mm(head(6, h), qk_t[:, h], qk_t[:, 4 + h // 2], True, True)
                    pe.wait_ge(cache_t_out, 2)
                    for h in range(H):
                        mm(head(7, h), qk_t[:, 6 + h], qk_t[:, 10 + h // 2], True, True)
                    for h in range(H):
                        ins = mm(head(0, h), qk_t[:, 6 + h], kc_t1[:, h // 2], True, True)
                    ins.then_inc(scores, 2)
                    mods(l, 8, 4)
                    mods(l, 12, 4)
                    probs_turned(l, (6, 7, 0))
                    mods(l, 16, 4)
                    attended(l, lambda h, g: att_v(h // 2, g), lambda h: vc1[:, h // 2], (1, 2))
                mods(l, 20, 4)
                x_parts_ready(l, 1)
                if l == 0:
                    pe.wait_ge(kn_out, 1)
                for n in range(OUT_UNITS):
                    by_tokens(out_unit(l, n), n)
                pe.wait_ge(mod_rows_out, (l + 1) * MOD_UNITS)
                gates_spread(l, 0)
                x_turned(l, 1)
                x_parts_ready(l, 2)
                pe.wait_ge(router_in, 32 * (l + 1))
                for g in range(G):
                    for k in range(KC):
                        ins = mm(ps[:, 6, g * EXPERTS:(g + 1) * EXPERTS], x_feat[:, k, g * P:(g + 1) * P], rw[:, k], k == 0, k == KC - 1)
                ins.then_inc(logits, 1)
                pe.wait_ge(gates_made, l + 1)
                for g in range(G):
                    ins = turned(ps[0:EXPERTS, 7, g * P:(g + 1) * P], taken[:, g * EXPERTS:(g + 1) * EXPERTS])
                ins.then_inc(gates_t, 1)
                experts(l)
                gates_spread(l, 1)


_INS = ['x_prompt', 'x_sample', 'c', 'state_ret', 'cache_na_k', 'cache_na_v', 'cache_att_k', 'cache_att_v', 'c_ctx',
        'w_mod', 'b_mod', 'ln_g', 'ln_b', 'w_in_even', 'w_out_even', 'ret_decay_logit', 'na_rpb', 'w_in_odd', 'w_out_odd',
        'conv_w', 'q_norm_g', 'k_norm_g', 'router_w', 'router_b', 'exp_w_gate', 'exp_w_up', 'exp_w_down',
        'sh_w_gate', 'sh_w_up', 'sh_w_down']
_OUTS = [('y_prompt', (1, 128, 1024)), ('y_sample', (1, 128, 1024)), ('state', (1, 1, 2, 4, 64, 128)),
         ('na_k', (1, 1, 128, 4, 128)), ('na_v', (1, 1, 128, 4, 128)),
         ('att_k', (1, 1, 128, 2, 128)), ('att_v', (1, 1, 128, 2, 128))]


def kernel(**inputs):
    import concourse.bacc as _bacc
    from concourse.bass_utils import run_bass_kernel_spmd as _run

    nc = _bacc.Bacc("TRN2", target_bir_lowering=False, num_devices=1)
    arrays = {name: np.ascontiguousarray(inputs[name]) for name in _INS}
    arrays["shape_consts"] = shape_constants()
    ins = {}
    for name, a in arrays.items():
        ins[name] = nc.dram_tensor(f"in_{name}", a.shape, mybir.dt.from_np(a.dtype), kind="ExternalInput").ap()
    outs = {name: nc.dram_tensor(f"out_{name}", shape, F32, kind="ExternalOutput").ap() for name, shape in _OUTS}
    build(nc, ins, outs)
    r = _run(nc, [{f"in_{name}": a for name, a in arrays.items()}], core_ids=[0])
    return tuple(r.results[0][f"out_{name}"] for name, _ in _OUTS)
```

```python
from contextlib import ExitStack

import numpy as np

import concourse.bass as bass
from concourse import mybir

F32 = mybir.dt.float32
F32R = mybir.dt.float32r
ACT = mybir.ActivationFunctionType
ALU = mybir.AluOpType
AX = mybir.AxisListType

P = 128
D = 1024
KC = D // P
G = 2
TOK = G * P
DEPTH = 2
GRID_W = 64
H = 4
DK = 64
KVH = 2
UNIT = 256
COL = 32
EXPERTS = 64
HID = 128
GROUPS = 8
PER_GROUP = EXPERTS // GROUPS
TOPK_GROUPS = 4
ROUTED_SCALE = 2.5
ALPHA = (2 * DEPTH) ** 0.25
LN_EPS = 1e-5
RMS_EPS = 1e-6
ATT_SCALE = float(P) ** -0.5
KEY_SCALE = float(DK) ** -0.5
LOW = -1.0e30
GONE = -3.0e38

MOD_UNITS = 6 * D // UNIT
SEC = D // UNIT
IN_UNITS = (12, 10)
OUT_UNITS = D // UNIT
TURNS = EXPERTS + 1
LOOPS = (TURNS - 5) // 4

MIX_MODS = [[[(l, n) for n in range(8 + 4 * i, 12 + 4 * i)] for i in range(3)] for l in range(DEPTH)]
NORM_MODS = [[(1, n) for n in range(0, 3)], [(1, n) for n in range(20, 22)]]
ROUTE_MODS = [[(0, n) for n in range(20, 24)], [(1, n) for n in range(22, 24)]]
LAST_MODS = [[(1, n) for n in range(3, 8)], []]
FIRST_MODS = [(0, n) for n in range(8)]


def stream():
    out = [("mod", *m) for m in FIRST_MODS]
    for l in range(DEPTH):
        out += [("in", l, n) for n in range(IN_UNITS[l])]
        out += [("mod", *m) for point in MIX_MODS[l] for m in point]
        out += [("out", l, n) for n in range(OUT_UNITS)]
        out += [("mod", *m) for m in NORM_MODS[l] + ROUTE_MODS[l]]
        out += [("turn", l, t) for t in range(TURNS)]
        out += [("mod", *m) for m in LAST_MODS[l]]
    return out


STREAM = stream()
UNIT_NO = {key: u for u, key in enumerate(STREAM)}
KIND = dict(enumerate(STREAM))
SPLIT = [u for u, key in KIND.items() if key[0] != "mod"]
SPLIT_NO = {u: s for s, u in enumerate(SPLIT)}
MOD_NO = {key: i for i, key in enumerate(k for k in STREAM if k[0] == "mod")}
FOLDS = [k for k in MOD_NO if k[2] % SEC == SEC - 1 and k[2] // SEC % 3 < 2]
FOLD_NO = {key: i for i, key in enumerate(FOLDS)}


def mod_unit(l, n):
    return UNIT_NO["mod", l, n]


def in_unit(l, n):
    return UNIT_NO["in", l, n]


def out_unit(l, n):
    return UNIT_NO["out", l, n]


def turn_unit(l, t):
    return UNIT_NO["turn", l, t]


def pair(l, t):
    return (l * TURNS + t) % 2


def in_before(l):
    return sum(IN_UNITS[:l])


def mods_before(u):
    return (sum(UNIT_NO[k] < u for k in MOD_NO), sum(UNIT_NO[k] < u for k in FOLDS))


RAW = 4
LOADED, _at = {}, [0] * RAW
for _u, _key in KIND.items():
    _at[_u % RAW] += 32 if _key[0] == "turn" else 16
    LOADED[_u] = _at[_u % RAW]

KEPT = dict(ident=128, cos=64, sin=64, window=128, pick=2 * 128, one=1, ln_eps=1, rms_eps=1, fold=2, plus=1)
EARLY = dict(rel_f=128, rel_b=128, mask_f=128, mask_b=128, pos_row=128, pos_col=2)


def columns(widths, at=0):
    out = {}
    for name, w in widths.items():
        out[name] = (at, at + w)
        at += w
    return out, at


KEPT_AT, KEPT_N = columns(KEPT)
EARLY_AT, EARLY_END = columns(EARLY, KEPT_N)
EARLY_N = EARLY_END - KEPT_N


def shape_constants():
    c = np.zeros((P, EARLY_END), np.float32)

    def put(name, value):
        a, b = {**KEPT_AT, **EARLY_AT}[name]
        c[:, a:b] = value

    i = np.arange(P)
    put("ident", np.eye(P))
    n_freq = P // 4
    freqs = np.float32(10000.0) ** (-np.arange(n_freq, dtype=np.float32) / np.float32(n_freq))
    row, col = (i // GRID_W).astype(np.float32), (i % GRID_W).astype(np.float32)
    ang = np.concatenate([row[:, None] * freqs, col[:, None] * freqs], axis=1)
    put("cos", np.cos(ang))
    put("sin", np.sin(ang))
    start = np.clip(i % GRID_W - 8, 0, GRID_W - 16)
    kc = (i % GRID_W)[None, :]
    put("window", np.where((kc >= start[:, None]) & (kc < start[:, None] + 16), 0.0, LOW))
    pick = np.zeros((P, G, P))
    for g in range(G):
        pick[g::COL, g] = 1.0
    put("pick", pick.reshape(P, G * P))
    put("one", 1.0)
    fold = np.zeros((P, G))
    for g in range(G):
        fold[g::COL, g] = 1.0
    put("fold", fold)
    plus = np.zeros((P, 1))
    plus[:G] = 1.0
    put("plus", plus)
    put("ln_eps", LN_EPS)
    put("rms_eps", RMS_EPS)
    rel = (i[None, :] - i[:, None]).astype(np.float32)
    put("rel_f", np.maximum(rel, 0))
    put("rel_b", np.maximum(-rel, 0))
    put("mask_f", rel >= 0)
    put("mask_b", rel <= 0)
    put("pos_row", np.where(i[:, None] < DK, i[None, :] + 1.0, P - i[None, :]))
    put("pos_col", np.stack([P - 1.0 - i, i], axis=1))
    return c


def build(nc, A, O):
    with ExitStack() as ctx:
        def sb(name, shape, dt=F32):
            return ctx.enter_context(nc.sbuf_tensor(name, shape, dt))

        def sem(name):
            return ctx.enter_context(nc.semaphore(name))

        raw_main = sb("raw_main", [P, RAW, KC * UNIT])
        raw_down = sb("raw_down", [P, 2, D])
        hi_main = sb("hi_main", [P, 2, KC * UNIT], F32R)
        lo_main = sb("lo_main", [P, 2, KC * UNIT], F32R)
        hi_down = sb("hi_down", [P, 2, D], F32R)
        lo_down = sb("lo_down", [P, 2, D], F32R)
        x_tok = sb("x_tok", [P, G, D])
        x_feat = sb("x_feat", [P, KC, TOK])
        x_hi = sb("x_hi", [P, KC, TOK], F32R)
        x_lo = sb("x_lo", [P, KC, TOK], F32R)
        proj = sb("proj", [P, 14, 512])
        temp = sb("temp", [P, 7168])
        const = sb("const", [P, KEPT_N])
        cond = sb("cond", [P, G, KC])
        cond_s = sb("cond_s", [P, G, KC])
        cond_pad = sb("cond_pad", [P, KC, COL])
        b_rows = sb("b_rows", [P, RAW, UNIT])
        mod_row = sb("mod_row", [P, D])
        gate_row = sb("gate_row", [P, 2, D])
        mod_feat = sb("mod_feat", [P, 4, KC, G])
        hid_hi = sb("hid_hi", [P, 2, TOK], F32R)
        hid_lo = sb("hid_lo", [P, 2, TOK], F32R)
        small = sb("small", [P, 192])
        decay = sb("decay", [P, 5 * 12])

        ps = ctx.enter_context(nc.psum_tensor("ps", [P, 8, 512], F32))

        def K(name, rows=P):
            a, b = KEPT_AT[name]
            return const[0:rows, a:b]

        early = proj[:, :, :].rearrange("p a b -> p (a b)")[:, 0:EARLY_N]

        def E(name):
            a, b = EARLY_AT[name]
            return early[:, a - KEPT_N:b - KEPT_N]

        def T(at, *shape):
            n = int(np.prod(shape))
            flat = temp[:, at:at + n]
            if len(shape) == 1:
                return flat
            letters = "abcd"[:len(shape)]
            return flat.rearrange(f"p ({' '.join(letters)}) -> p {' '.join(letters)}",
                                  **{x: s for x, s in zip(letters[1:], shape[1:])})

        sc_ctx = T(0, H, P)
        sc_lat = T(512, H, 2 * P)
        att_d = T(1536, 2, G, 2, P)
        pr_t = T(1536, 3, H, P)
        dmat = T(3072, H, P)
        k_out = T(3072, H, P)
        q_dec = T(3584, H, P)
        k_dec = T(4096, H, 2, DK)
        q_pow = T(4608, H, P)
        st_out = T(4608, H, P)
        kc_t = T(5120, H, P)
        vc = T(5632, H, P)
        s0 = T(6144, H, P)
        bias = T(6656, H, 2, GRID_W)
        kc_in = T(1536, H, P)
        rows_pad = T(0, H * 3, 127)
        dec_e = T(2048, 2, H, P)
        z_pad = T(3072, 2 * 2 * G, P + 2)
        conv_o = T(4112, 4, G, P)
        cv_w = small[:, 60:72].rearrange("p (w t) -> p w t", w=3)
        kc_t1 = T(5632, KVH, P)
        vc1 = T(5888, KVH, P)
        kc_in1 = T(6144, KVH, P)
        gains = T(6400, 2, P)
        sq = T(1536, 12, P)
        roped = T(3072, 6, P)
        qk_t = T(0, 0 + 12, P)
        ln_g = T(0, D)
        ln_b = T(1024, D)
        z = T(2048, G, D)
        rw = T(6144, KC, EXPERTS)
        rb = T(6656, EXPERTS)
        pf = proj[:, :, :].rearrange("p a b -> p (a b)")
        ex_silu = pf[:, 0:512].rearrange("p (a b) -> p a b", a=2)
        ex_up = pf[:, 512:1024].rearrange("p (a b) -> p a b", a=2)
        ex_h = pf[:, 1024:1536].rearrange("p (a b) -> p a b", a=2)
        ex_gate = pf[:, 1536:2560].rearrange("p (a b) -> p a b", a=4)
        score = pf[:, 2560:2688]
        select = pf[:, 2688:2816]
        gsel = pf[:, 2816:2944]
        taken = pf[:, 2944:3072]
        top = pf[:, 3072:3200].rearrange("p (a b) -> p a b", b=8)
        gscore = pf[:, 3200:3216]
        gtaken = pf[:, 3216:3232]
        gmask = pf[:, 3232:3248]
        gpen = pf[:, 3248:3264]
        top4 = pf[:, 3264:3280].rearrange("p (a b) -> p a b", a=2)
        top8 = pf[:, 3280:3296].rearrange("p (a b) -> p a b", a=2)
        wsum = pf[:, 3296:3298]
        gate_t = pf[0:EXPERTS, 3328:3328 + TOK]

        q_dup = proj[:, 0:2, :].rearrange("p a (b c) -> p (a b) c", b=2)
        k_low = proj[0:DK, 2:4, :].rearrange("p a (b c) -> p (a b) c", b=2)

        def even_v(h, g):
            return proj[:, 4 + h // 2, g * UNIT + (h % 2) * P:g * UNIT + (h % 2) * P + P]

        def even_gate(h, g):
            return proj[:, 6 + h // 2, g * UNIT + (h % 2) * P:g * UNIT + (h % 2) * P + P]

        def na_q(h, g):
            return proj[:, 8 + h // 2, (h % 2) * TOK + g * P:(h % 2) * TOK + g * P + P]

        def na_k(h, g):
            return proj[:, 10 + h // 2, (h % 2) * TOK + g * P:(h % 2) * TOK + g * P + P]

        def na_v(h, g):
            return proj[:, 12 + h // 2, g * UNIT + (h % 2) * P:g * UNIT + (h % 2) * P + P]

        def att_v(h, g):
            return proj[:, 9, g * UNIT + h * P:g * UNIT + h * P + P]

        pad_dram = nc.dram_tensor("pad_rows", [GRID_W, H * 3 * 127], F32, kind="Internal").ap()
        gate_dram = [nc.dram_tensor(f"gates{l}", [EXPERTS, TOK], F32, kind="Internal").ap() for l in range(DEPTH)]

        main_loaded = [sem(f"main_loaded{i}") for i in range(RAW)]
        down_loaded = [sem(f"down_loaded{i}") for i in range(2)]
        bias_loaded = [sem(f"bias_loaded{i}") for i in range(RAW)]
        gate_loaded = [sem(f"gate_loaded{i}") for i in range(4)]
        main_hi, main_lo, main_used = sem("main_hi"), sem("main_lo"), sem("main_used")
        down_hi, down_lo, down_used = sem("down_hi"), sem("down_lo"), sem("down_used")
        consts_in, early_in, x_in, cond_in = sem("consts_in"), sem("early_in"), sem("x_in"), sem("cond_in")
        decay_in, cache_k_in, cache_v_in = sem("decay_in"), sem("cache_k_in"), sem("cache_v_in")
        state_in, rpb_in, bias_in, pad_out = sem("state_in"), sem("rpb_in"), sem("bias_in"), sem("pad_out")
        ln_in, router_in, small_in = sem("ln_in"), sem("router_in"), sem("small_in")
        pad_zero, bias_zero = sem("pad_zero"), sem("bias_zero")
        cond_ready = sem("cond_ready")
        mod_rows_out, mod_t, mod_t_out = sem("mod_rows_out"), sem("mod_t"), sem("mod_t_out")
        xt_done, x_feat_act, x_feat_dve = sem("xt_done"), sem("x_feat_act"), sem("x_feat_dve")
        x_hi_done, x_lo_done = sem("x_hi_done"), sem("x_lo_done")
        in_out = sem("in_out")
        act_chain, dve_chain, pool_chain = sem("act_chain"), sem("dve_chain"), sem("pool_chain")
        decay_ready = sem("decay_ready")
        cache_t, cache_t_out = sem("cache_t"), sem("cache_t_out")
        att_s, att_d_ready, k_t, k_dec_ready = sem("att_s"), sem("att_d_ready"), sem("k_t"), sem("k_dec_ready")
        scores, centred, exped, probs = sem("scores"), sem("centred"), sem("exped"), sem("probs")
        state_mm, state_copied = sem("state_mm"), sem("state_copied")
        ret_o, ret_var, ret_sd, ret_ready = sem("ret_o"), sem("ret_var"), sem("ret_sd"), sem("ret_ready")
        probs_t, probs_t_out, att_o = sem("probs_t"), sem("probs_t_out"), sem("att_o")
        ret_t, kn_t, kn_out = sem("ret_t"), sem("kn_t"), sem("kn_out")
        cat_ready = sem("cat_ready")
        qk_normed, roped_ready, sq_ready = sem("qk_normed"), sem("roped_ready"), sem("sq_ready")
        ms_ready, rms_ready = sem("ms_ready"), sem("rms_ready")
        qk_tr, qk_t_out = sem("qk_tr"), sem("qk_t_out")
        gates_mm, gate_copied, ln_var, ln_sd, normed = sem("gates_mm"), sem("gate_copied"), sem("ln_var"), sem("ln_sd"), sem("normed")
        logits, sigmoid_out, gates_made = sem("logits"), sem("sigmoid_out"), sem("gates_made")
        gates_t, gates_t_out, gates_stored = sem("gates_t"), sem("gates_t_out"), sem("gates_stored")
        ones_set = sem("ones_set")
        silu_out, up_read, h_ready, h_hi, h_lo = sem("silu_out"), sem("up_read"), sem("h_ready"), sem("h_hi"), sem("h_lo")
        stored = sem("stored")

        block = ctx.enter_context(nc.Block())

        w_in = (A["w_in_even"][0], A["w_in_odd"][0])
        w_out = (A["w_out_even"][0], A["w_out_odd"][0])

        @block.sync
        def _(sp):
            def slot_free(u):
                v = u - RAW
                if v in SPLIT_NO:
                    sp.wait_ge(main_lo, SPLIT_NO[v] + 1)
                elif v >= 0:
                    sp.wait_ge(main_used, v + 1)

            def load_unit(u, source):
                slot_free(u)
                sp.dma_start(raw_main[:, u % RAW, :].rearrange("p (k n) -> p k n", k=KC), source) \
                    .then_inc(main_loaded[u % RAW], 16)

            def load_mod(l, n):
                cols = slice(n * UNIT, (n + 1) * UNIT)
                load_unit(mod_unit(l, n), A["w_mod"][l].rearrange("(p k) n -> p k n", k=KC)[:, :, cols])
                at = MOD_NO["mod", l, n]
                if at == 0:
                    sp.wait_ge(bias_zero, 1)
                if at >= RAW:
                    sp.wait_ge(mod_rows_out, at - RAW + 1)
                sp.dma_start(b_rows[0:G, at % RAW, :], A["b_mod"][l:l + 1, cols].partition_broadcast(G)) \
                    .then_inc(bias_loaded[at % RAW], 16)

            def load_turn(l, t, slot, down, gate, up, out_w):
                if isinstance(t, int):
                    slot_free(turn_unit(l, t))
                else:
                    sp.wait_ge(main_lo, SPLIT_NO[turn_unit(l, 0)] - RAW + 1 + t)
                view = raw_main[:, slot, :].rearrange("p (k w n) -> p w k n", k=KC, w=2)
                sp.dma_start(view[:, 0], gate.rearrange("(p k) n -> p k n", k=KC)).then_inc(main_loaded[slot], 16)
                sp.dma_start(view[:, 1], up.rearrange("(p k) n -> p k n", k=KC)).then_inc(main_loaded[slot], 16)
                if not (isinstance(t, int) and l * TURNS + t < 2):
                    sp.wait_ge(down_lo, l * TURNS - 1 + t)
                sp.dma_start(raw_down[:, down, :], out_w).then_inc(down_loaded[down], 16)

            def expert(l, e):
                return A["exp_w_gate"][l, e], A["exp_w_up"][l, e], A["exp_w_down"][l, e]

            for l, n in FIRST_MODS:
                load_mod(l, n)
            for l in range(DEPTH):
                for n in range(IN_UNITS[l]):
                    load_unit(in_unit(l, n), w_in[l].rearrange("(p k) n -> p k n", k=KC)[:, :, n * UNIT:(n + 1) * UNIT])
                for point in MIX_MODS[l]:
                    for m in point:
                        load_mod(*m)
                for n in range(OUT_UNITS):
                    load_unit(out_unit(l, n), w_out[l].rearrange("(k p) n -> p k n", k=KC)[:, :, n * UNIT:(n + 1) * UNIT])
                for m in NORM_MODS[l] + ROUTE_MODS[l]:
                    load_mod(*m)
                u0 = turn_unit(l, 0)
                load_turn(l, 0, u0 % RAW, pair(l, 0), A["sh_w_gate"][l], A["sh_w_up"][l], A["sh_w_down"][l])
                for t in range(1, 5):
                    load_turn(l, t, (u0 + t) % RAW, pair(l, t), *expert(l, t - 1))
                with sp.Fori(0, LOOPS) as i:
                    for j in range(4):
                        load_turn(l, 5 + j + 4 * i, (u0 + 5 + j) % RAW, pair(l, 5 + j), *expert(l, 4 + j + 4 * i))
                for m in LAST_MODS[l]:
                    load_mod(*m)

        @block.gpsimd
        def _(pool):
            nc.gpsimd.memset(b_rows[:, :, :], 0.0).then_inc(bias_zero, 1)
            nc.gpsimd.memset(rows_pad[0:GRID_W], 0.0).then_inc(pad_zero, 1)
            pool.wait_ge(pad_zero, 1)
            for h in range(H):
                pool.dma_start(rows_pad[0:GRID_W, 3 * h:3 * h + 3, 48:79],
                               A["na_rpb"][0, h, 6:9, :].partition_broadcast(GRID_W)).then_inc(rpb_in, 16)
            pool.dma_start(kc_in, A["cache_na_k"][0, 0]).then_inc(cache_k_in, 16)
            pool.dma_start(vc, A["cache_na_v"][0, 0]).then_inc(cache_v_in, 16)
            for d in range(2):
                pool.dma_start(s0[d * DK:(d + 1) * DK], A["state_ret"][0, 0, d].rearrange("h k v -> k h v")) \
                    .then_inc(state_in, 16)
            pool.wait_ge(rpb_in, 16 * H)
            pool.dma_start(pad_dram, rows_pad[0:GRID_W].rearrange("p a b -> p (a b)")).then_inc(pad_out, 16)
            pool.wait_ge(pad_out, 16)
            for r in range(2):
                for h in range(H):
                    skew = bass.AP(pad_dram.tensor, 63 + (3 * h + 1 - r) * 127,
                                   [[H * 3 * 127 - 1, GRID_W], [127, 2], [1, GRID_W]])
                    pool.dma_start(bias[r * GRID_W:(r + 1) * GRID_W, h], skew).then_inc(bias_in, 16)

            for l in range(DEPTH):
                if l == 1:
                    pool.wait_ge(normed, 2 * G)
                    pool.dma_start(kc_in1, A["cache_att_k"][0, 0]).then_inc(cache_k_in, 16)
                    pool.dma_start(vc1, A["cache_att_v"][0, 0]).then_inc(cache_v_in, 16)
                    pool.dma_start(gains[:, 0:1], A["q_norm_g"][0:1].partition_broadcast(P)).then_inc(small_in, 16)
                    pool.dma_start(gains[:, 1:2], A["k_norm_g"][0:1].partition_broadcast(P)).then_inc(small_in, 16)
                    with nc.allow_non_contiguous_dma("1,536 values of the convolution"):
                        for w in range(3):
                            pool.dma_start(cv_w[:, w], A["conv_w"][0, w].rearrange("(t p) -> p t", p=P)) \
                                .then_inc(small_in, 16)
                if l == 0:
                    pool.wait_ge(in_out, 12)
                    pool.dma_start(O["na_v"][0, 0].rearrange("t h d -> t (h d)").rearrange("t (u c) -> t u c", u=2),
                                   proj[:, 12:14, 0:UNIT]).then_inc(stored, 16)
                    pool.wait_ge(state_copied, 1)
                    for d in range(2):
                        pool.dma_start(O["state"][0, 0, d].rearrange("h k v -> k h v"), st_out[d * DK:(d + 1) * DK]) \
                            .then_inc(stored, 16)
                    pool.wait_ge(kn_out, 1)
                    pool.dma_start(O["na_k"][0, 0], k_out).then_inc(stored, 16)
                else:
                    pool.wait_ge(in_out, in_before(1) + 10)
                    pool.dma_start(O["att_v"][0, 0].rearrange("t h d -> t (h d)"), proj[:, 9, 0:UNIT]).then_inc(stored, 16)
                    pool.wait_ge(qk_normed, 2)
                    pool.dma_start(O["att_k"][0, 0].rearrange("t h d -> t (h d)"), proj[:, 8, 0:UNIT]).then_inc(stored, 16)
                pool.wait_ge(cat_ready, l + 1)
                pool.wait_ge(stored, 16 * (4 if l == 0 else 6))
                for n in range(2):
                    if n == 1:
                        pool.wait_ge(normed, (2 * l + 1) * G)
                    pool.dma_start(ln_g, A["ln_g"][l, n:n + 1, :].partition_broadcast(P)).then_inc(ln_in, 16)
                    pool.dma_start(ln_b, A["ln_b"][l, n:n + 1, :].partition_broadcast(P)).then_inc(ln_in, 16)
                    if n == 0:
                        pool.dma_start(rw, A["router_w"][l].rearrange("(p k) e -> p k e", k=KC)).then_inc(router_in, 16)
                        pool.dma_start(rb, A["router_b"][l:l + 1, :].partition_broadcast(P)).then_inc(router_in, 16)
                        nc.gpsimd.memset(ex_gate[:, 0, :], 1.0).then_inc(ones_set, 1)
                pool.wait_ge(gates_t_out, l + 1)
                pool.dma_start(gate_dram[l], gate_t).then_inc(gates_stored, 16)
                pool.wait_ge(gates_stored, 16 * (l + 1))

                def load_gate(t, slot):
                    if not (isinstance(t, int) and t < 4):
                        pool.wait_ge(h_ready, l * TURNS - 3 + t)
                    pool.dma_start(ex_gate[:, slot, :], gate_dram[l][bass.ds(t - 1, 1), :].partition_broadcast(P)) \
                        .then_inc(gate_loaded[slot], 16)

                for t in range(1, 5):
                    load_gate(t, t % 4)
                with pool.Fori(0, LOOPS) as i:
                    for j in range(4):
                        load_gate(5 + j + 4 * i, (5 + j) % 4)

            for g, y in enumerate((O["y_prompt"], O["y_sample"])):
                pool.wait_ge(normed, 3 * G + g + 1)
                pool.dma_start(y[0], x_tok[:, g, :]).then_inc(stored, 16)
            pool.wait_ge(stored, 16 * 8)

        @block.scalar
        def _(act):
            chain = [0]

            def link(ins):
                chain[0] += 1
                ins.then_inc(act_chain, 1)
                act.wait_ge(act_chain, chain[0])

            split = [0]

            def hi_main_of(slot, half, loaded, free):
                act.wait_ge(main_loaded[slot], loaded)
                if free is not None:
                    act.wait_ge(main_used, free)
                nc.scalar.activation(hi_main[:, half, :], raw_main[:, slot, :], ACT.Copy).then_inc(main_hi, 1)

            def split_to(u):
                while split[0] < len(SPLIT) and SPLIT[split[0]] <= u:
                    s = split[0]
                    v = SPLIT[s]
                    hi_main_of(v % RAW, s % 2, LOADED[v], SPLIT[s - 2] + 1 if s >= 2 else None)
                    split[0] += 1

            act.dma_start(const[:, :], A["shape_consts"][:, 0:KEPT_N]).then_inc(consts_in, 16)
            act.dma_start(cond[:, 0, :], A["c_ctx"].rearrange("(p k) -> p k", k=KC)).then_inc(cond_in, 16)
            act.dma_start(cond[:, 1, :], A["c"][0].rearrange("(p k) -> p k", k=KC)).then_inc(cond_in, 16)
            act.dma_start(x_tok[:, 0, :], A["x_prompt"][0]).then_inc(x_in, 16)
            act.dma_start(x_tok[:, 1, :], A["x_sample"][0]).then_inc(x_in, 16)
            act.dma_start(early, A["shape_consts"][:, KEPT_N:EARLY_END]).then_inc(early_in, 16)
            logit = decay[:, 0:12]
            flat = A["ret_decay_logit"].rearrange("a d h -> a (d h)")
            act.dma_start(logit[:, 0:8], flat.partition_broadcast(P)).then_inc(decay_in, 16)
            for d in range(2):
                act.dma_start(logit[d * DK:(d + 1) * DK, 8:12],
                              A["ret_decay_logit"][:, d].partition_broadcast(DK)).then_inc(decay_in, 16)
            act.wait_ge(cond_in, 32)
            nc.scalar.activation(cond_s[:, :, :], cond[:, :, :], ACT.Silu).then_inc(cond_ready, 1)

            act.wait_ge(decay_in, 48)
            act.wait_ge(consts_in, 16)
            link(nc.scalar.activation(decay[:, 12:24], logit, ACT.Abs))
            link(nc.scalar.activation(decay[:, 24:36], decay[:, 12:24], ACT.Exp, scale=-1.0))
            nc.scalar.activation(decay[:, 36:48], decay[:, 24:36], ACT.Ln, bias=K("one")).then_inc(decay_ready, 1)
            act.wait_ge(decay_ready, 2)
            act.wait_ge(early_in, 16)
            for d, rel in enumerate(("rel_f", "rel_b")):
                for h in range(H):
                    nc.scalar.activation(dec_e[:, d, h], E(rel), ACT.Exp,
                                         scale=decay[:, 48 + 4 * d + h:49 + 4 * d + h]).then_inc(decay_ready, 1)
            for h in range(H):
                nc.scalar.activation(q_pow[:, h], E("pos_row"), ACT.Exp, scale=decay[:, 56 + h:57 + h]) \
                    .then_inc(decay_ready, 1)
            act.wait_ge(decay_ready, 16)
            nc.scalar.activation(small[:, 0:8], small[:, 8:16], ACT.Exp).then_inc(decay_ready, 1)
            act.wait_ge(cache_t, 1)
            nc.scalar.activation(kc_t, ps[:, 7, :].rearrange("p (h t) -> p h t", h=H), ACT.Copy).then_inc(cache_t_out, 1)

            def make_x(l, n, shift, scale):
                act.wait_ge(mod_t_out, FOLD_NO["mod", l, 12 * n + 7] + 1)
                act.wait_ge(xt_done, 2 * (2 * l + n) + 1)
                for k in range(KC):
                    ins = nc.scalar.activation(x_feat[:, k, 0:P], ps[:, k // 4, (k % 4) * P:(k % 4 + 1) * P], ACT.Identity,
                                               scale=mod_feat[:, scale, k, 0:1], bias=mod_feat[:, shift, k, 0:1])
                ins.then_inc(x_feat_act, 1)
                act.wait_ge(x_feat_act, 2 * l + n + 1)
                nc.scalar.activation(x_hi[:, :, 0:P], x_feat[:, :, 0:P], ACT.Copy).then_inc(x_hi_done, 1)
                act.wait_ge(x_feat_dve, 2 * l + n + 1)
                nc.scalar.activation(x_hi[:, :, P:TOK], x_feat[:, :, P:TOK], ACT.Copy).then_inc(x_hi_done, 1)

            def cat_hi(l):
                act.wait_ge(cat_ready, l + 1)
                nc.scalar.activation(x_hi[:, :, :], x_feat[:, :, :], ACT.Copy).then_inc(x_hi_done, 2)

            def unit_copy(l, n):
                u = in_unit(l, n)
                act.wait_ge(main_used, u + 1)
                bank = ps[:, 4 + u % 2, :]
                if l == 0 and n == 0:
                    act.wait_ge(k_dec_ready, 1)
                    b3 = bank.rearrange("p (t c) -> p t c", t=2)
                    for odd in range(2):
                        for half in range(2):
                            ins = nc.scalar.activation(q_dup[half * DK:(half + 1) * DK, odd::2, :],
                                                       b3[odd * DK:(odd + 1) * DK], ACT.Copy)
                    ins.then_inc(in_out, 1)
                elif l == 0 and n == 1:
                    b3 = bank.rearrange("p (t c) -> p t c", t=2)
                    for odd in range(2):
                        ins = nc.scalar.activation(k_low[:, odd::2, :], b3[odd * DK:(odd + 1) * DK], ACT.Copy,
                                                   scale=KEY_SCALE)
                    ins.then_inc(in_out, 1)
                elif l == 0:
                    nc.scalar.activation(proj[:, n + 2, :], bank, ACT.Silu if n in (4, 5) else ACT.Copy).then_inc(in_out, 1)
                else:
                    nc.scalar.activation(proj[:, n, :], bank, ACT.Copy).then_inc(in_out, 1)

            def softmax_exp(l):
                for n, s in enumerate((sc_ctx, sc_lat)):
                    act.wait_ge(centred, 2 * l + n + 1)
                    nc.scalar.activation(s, s, ACT.Exp).then_inc(exped, 1)

            def probs_copy(l, banks):
                for n in range(3):
                    act.wait_ge(probs_t, 3 * l + n + 1)
                    nc.scalar.activation(pr_t[:, n], ps[:, banks[n], :].rearrange("p (h t) -> p h t", h=H), ACT.Copy) \
                        .then_inc(probs_t_out, 1)

            def norm_sd(l, n):
                act.wait_ge(ln_in, 32 * (2 * l + n + 1))
                for g in range(G):
                    act.wait_ge(gates_mm, G * (2 * l + n) + g + 1)
                    nc.scalar.activation(z[:, g, :], ps[:, 4 + 2 * g:6 + 2 * g, :].rearrange("p a b -> p (a b)"), ACT.Copy) \
                        .then_inc(gate_copied, 1)
                for g in range(G):
                    act.wait_ge(ln_var, G * (2 * l + n) + g + 1)
                    nc.scalar.activation(small[:, 40 + g:41 + g], small[:, 33 + 2 * g:34 + 2 * g], ACT.Sqrt, bias=K("ln_eps")) \
                        .then_inc(ln_sd, 1)

            def experts(l):
                u0 = turn_unit(l, 0)
                s0 = SPLIT_NO[u0]

                def hi_down_of(t, slot, loaded):
                    act.wait_ge(down_loaded[slot], loaded)
                    if not (isinstance(t, int) and l * TURNS + t < 2):
                        act.wait_ge(down_used, l * TURNS - 1 + t)
                    nc.scalar.activation(hi_down[:, slot, :], raw_down[:, slot, :], ACT.Copy).then_inc(down_hi, 1)

                def silu_of(t, slot, bank):
                    act.wait_ge(main_used, u0 + 1 + t)
                    if not (isinstance(t, int) and l * TURNS + t < 2):
                        act.wait_ge(up_read, l * TURNS - 1 + t)
                    nc.scalar.activation(ex_silu[:, slot, :], ps[:, bank, 0:TOK], ACT.Silu).then_inc(silu_out, 1)

                def down_count(t):
                    return 16 * ((l * TURNS + t) // 2 + 1)

                def turn(t, j, extra=0):
                    b = pair(l, j - 1)
                    hi_down_of(t - 1, b, down_count(j - 1) + 8 * extra)
                    hi_main_of((u0 + j) % RAW, (s0 + j) % 2, LOADED[u0 + j] + 8 * extra,
                               SPLIT[s0 + t - 2] + 1 if isinstance(t, int) else u0 + t - 1)
                    silu_of(t - 1, b, 4 + (u0 + j - 1) % 2)

                split_to(u0)
                for t in range(1, 5):
                    turn(t, t)
                with act.Fori(0, LOOPS) as i:
                    for j in range(4):
                        turn(5 + j + 4 * i, 5 + j, 4 * i)
                hi_down_of(TURNS - 1, pair(l, TURNS - 1), down_count(TURNS - 1))
                silu_of(TURNS - 1, pair(l, TURNS - 1), 4 + (u0 + TURNS - 1) % 2)
                split[0] = s0 + TURNS

            split_to(in_unit(0, 1))
            for l in range(DEPTH):
                make_x(l, 0, 0, 1)
                for n in range(IN_UNITS[l]):
                    split_to(in_unit(l, n) + 1)
                    unit_copy(l, n)
                if l == 1:
                    act.wait_ge(in_out, in_before(1) + 9)
                    nc.scalar.activation(sq, proj[:, 6:9, :].rearrange("p a (b c) -> p (a b) c", b=4), ACT.Square) \
                        .then_inc(sq_ready, 1)
                    act.wait_ge(ms_ready, 1)
                    nc.scalar.activation(small[:, 80:92], small[:, 92:104], ACT.Sqrt, scale=1.0 / P, bias=K("rms_eps")) \
                        .then_inc(rms_ready, 1)
                    for n in range(4):
                        act.wait_ge(qk_tr, n + 1)
                        first, count = ((0, 4), (4, 2), (6, 4), (10, 2))[n]
                        nc.scalar.activation(qk_t[:, first:first + count],
                                             ps[:, n, 0:count * P].rearrange("p (h t) -> p h t", h=count), ACT.Copy) \
                            .then_inc(qk_t_out, 1)
                    act.wait_ge(cache_t, 2)
                    nc.scalar.activation(kc_t1, ps[:, 7, 0:KVH * P].rearrange("p (h t) -> p h t", h=KVH), ACT.Copy) \
                        .then_inc(cache_t_out, 1)
                softmax_exp(l)
                if l == 0:
                    act.wait_ge(ret_var, 1)
                    nc.scalar.activation(small[:, 16:24], small[:, 24:32], ACT.Sqrt, bias=K("ln_eps")).then_inc(ret_sd, 1)
                probs_copy(l, (0, 1, 2) if l == 0 else (6, 7, 0))
                if l == 0:
                    act.wait_ge(kn_t, 1)
                    nc.scalar.activation(k_out, ps[:, 2, :].rearrange("p (h t) -> p h t", h=H), ACT.Copy).then_inc(kn_out, 1)
                split_to(out_unit(l, 1))
                cat_hi(l)
                split_to(out_unit(l, OUT_UNITS - 1))
                norm_sd(l, 0)
                make_x(l, 1, 2, 3)
                act.wait_ge(logits, l + 1)
                nc.scalar.activation(score, ps[:, 6, 0:G * EXPERTS], ACT.Sigmoid).then_inc(sigmoid_out, 1)
                experts(l)
                norm_sd(l, 1)
                if l + 1 < DEPTH:
                    split_to(in_unit(l + 1, 1))

        @block.vector
        def _(dve):
            chain = [0]
            V = nc.vector

            def link(ins):
                chain[0] += 1
                ins.then_inc(dve_chain, 1)
                dve.wait_ge(dve_chain, chain[0])

            split = [0]

            def lo_main_of(s, slot, half):
                dve.wait_ge(main_hi, s + 1)
                V.tensor_tensor(lo_main[:, half, :], raw_main[:, slot, :], hi_main[:, half, :].bitcast(F32), ALU.subtract) \
                    .then_inc(main_lo, 1)

            def split_to(u):
                while split[0] < len(SPLIT) and SPLIT[split[0]] <= u:
                    lo_main_of(split[0], SPLIT[split[0]] % RAW, split[0] % 2)
                    split[0] += 1

            def along(ap, n):
                return ap.unsqueeze(2).broadcast_to([ap.shape[0], ap.shape[1], n])

            def over(ap, n):
                return ap.unsqueeze(1).broadcast_to([ap.shape[0], n, ap.shape[1]])

            def mod_row_out(l, n):
                u, sec, at = mod_unit(l, n), n // SEC, MOD_NO["mod", l, n]
                cols = slice((n % SEC) * UNIT, (n % SEC + 1) * UNIT)
                out = gate_row[:, sec // 3, cols] if sec % 3 == 2 else mod_row[:, cols]
                dve.wait_ge(main_used, u + 1)
                dve.wait_ge(bias_loaded[at % RAW], 16 * (at // RAW + 1))
                src = ps[:, 4 + u % 2, 0:UNIT]
                if sec % 3 == 0:
                    V.tensor_tensor(out, src, b_rows[:, at % RAW, :], ALU.add).then_inc(mod_rows_out, 1)
                else:
                    V.scalar_tensor_tensor(out=out, in0=src, scalar=K("plus"), in1=b_rows[:, at % RAW, :],
                                           op0=ALU.add, op1=ALU.add).then_inc(mod_rows_out, 1)
                if sec % 3 < 2 and n % SEC == SEC - 1:
                    s = (0, 1, None, 2, 3)[sec]
                    dve.wait_ge(mod_t, FOLD_NO["mod", l, n] + 1)
                    V.tensor_copy(mod_feat[:, s].rearrange("p k g -> p (k g)"), ps[:, 4 + (u + 1) % 2, 0:KC * G]) \
                        .then_inc(mod_t_out, 1)

            def mods(these):
                for l, n in these:
                    mod_row_out(l, n)

            def make_x(l, n, shift, scale):
                dve.wait_ge(mod_t_out, FOLD_NO["mod", l, 12 * n + 7] + 1)
                dve.wait_ge(xt_done, 2 * (2 * l + n) + 2)
                for k in range(KC):
                    ins = V.tensor_scalar(x_feat[:, k, P:TOK], ps[:, 2 + k // 4, (k % 4) * P:(k % 4 + 1) * P],
                                          mod_feat[:, scale, k, 1:2], mod_feat[:, shift, k, 1:2], ALU.mult, ALU.add)
                ins.then_inc(x_feat_dve, 1)
                for g in range(G):
                    dve.wait_ge(x_hi_done, 2 * (3 * l + 2 * n) + g + 1)
                    V.tensor_tensor(x_lo[:, :, g * P:(g + 1) * P], x_feat[:, :, g * P:(g + 1) * P],
                                    x_hi[:, :, g * P:(g + 1) * P].bitcast(F32), ALU.subtract).then_inc(x_lo_done, 1)

            def cat_lo(l):
                dve.wait_ge(x_hi_done, 2 * (3 * l + 2))
                V.tensor_tensor(x_lo[:, :, :], x_feat[:, :, :], x_hi[:, :, :].bitcast(F32), ALU.subtract) \
                    .then_inc(x_lo_done, 2)

            def centre(s, keys):
                mx = small[:, 104:108] if keys == P else small[:, 152:156]
                link(V.tensor_reduce(mx, s, AX.X, ALU.max))
                V.tensor_tensor(s, s, along(mx, keys), ALU.subtract).then_inc(centred, 1)

            def normalise(s, keys, n):
                den = small[:, 108:112] if keys == P else small[:, 156:160]
                dve.wait_ge(exped, n)
                link(V.tensor_reduce(den, s, AX.X, ALU.add))
                link(V.reciprocal(den, den))
                V.tensor_tensor(s, s, along(den, keys), ALU.mult).then_inc(probs, 1)

            def softmax_in(l, banks):
                dve.wait_ge(scores, 2 * l + 1)
                link(V.tensor_scalar(sc_ctx, ps[:, banks[0], :].rearrange("p (h t) -> p h t", h=H), ATT_SCALE, None, ALU.mult))
                centre(sc_ctx, P)
                dve.wait_ge(scores, 2 * l + 2)
                own = ps[:, banks[1], :].rearrange("p (h t) -> p h t", h=H)
                if l == 0:
                    link(V.scalar_tensor_tensor(out=sc_lat[:, :, 0:P], in0=own, scalar=ATT_SCALE,
                                                in1=bias.rearrange("p h a c -> p h (a c)"), op0=ALU.mult, op1=ALU.add))
                else:
                    link(V.tensor_scalar(sc_lat[:, :, 0:P], own, ATT_SCALE, None, ALU.mult))
                link(V.tensor_scalar(sc_lat[:, :, P:2 * P], ps[:, banks[2], :].rearrange("p (h t) -> p h t", h=H),
                                     ATT_SCALE, None, ALU.mult))
                centre(sc_lat, 2 * P)

            def att_out(l, n, bank):
                dve.wait_ge(att_o, G * l + n + 1)
                link(V.tensor_copy(x_feat[:, H:2 * H, n * P:(n + 1) * P], ps[:, bank, :].rearrange("p (h t) -> p h t", h=H)))

            def post_norm(l, n, waiting):
                dve.wait_ge(ln_in, 32 * (2 * l + n + 1))
                for g in range(G):
                    dve.wait_ge(gate_copied, G * (2 * l + n) + g + 1)
                    zg = z[:, g, :]
                    if n == 0:
                        y = ps[:, 0:4, g * UNIT:(g + 1) * UNIT]
                        zv = zg.rearrange("p (a b) -> p a b", b=UNIT)
                    else:
                        y = ps[:, 2 * g:2 * g + 2, :]
                        zv = zg.rearrange("p (a b) -> p a b", b=512)
                    link(V.tensor_tensor(zv, zv, y, ALU.mult))
                    link(V.scalar_tensor_tensor(out=zg, in0=x_tok[:, g, :], scalar=ALPHA, in1=zg, op0=ALU.mult, op1=ALU.add))
                    stats = small[:, 112 + 48 * g:124 + 48 * g]
                    V.bn_stats(stats[:, 0:6], zg[:, 0:512])
                    link(V.bn_stats(stats[:, 6:12], zg[:, 512:1024]))
                    V.bn_aggr(small[:, 32 + 2 * g:34 + 2 * g], stats).then_inc(ln_var, 1)
                    dve.wait_ge(ln_var, G * (2 * l + n) + g + 1)
                mods(waiting[:1])
                for g in range(G):
                    zg = z[:, g, :]
                    dve.wait_ge(ln_sd, G * (2 * l + n) + g + 1)
                    link(V.reciprocal(small[:, 42 + g:43 + g], small[:, 40 + g:41 + g]))
                    link(V.scalar_tensor_tensor(out=zg, in0=zg, scalar=small[:, 32 + 2 * g:33 + 2 * g], in1=ln_g,
                                                op0=ALU.subtract, op1=ALU.mult))
                    V.scalar_tensor_tensor(out=x_tok[:, g, :], in0=zg, scalar=small[:, 42 + g:43 + g], in1=ln_b,
                                           op0=ALU.mult, op1=ALU.add).then_inc(normed, 1)
                    if g == 0:
                        mods(waiting[1:2])
                mods(waiting[2:])

            def route(l):
                dve.wait_ge(router_in, 32 * (l + 1))
                dve.wait_ge(sigmoid_out, l + 1)
                waiting = list(ROUTE_MODS[l])
                sel3 = select.rearrange("p (g e) -> p g e", g=G)
                link(V.tensor_tensor(sel3, score.rearrange("p (g e) -> p g e", g=G), over(rb, G), ALU.add))
                for n in range(G * GROUPS):
                    ins = V.max(top[:, n], select[:, n * PER_GROUP:(n + 1) * PER_GROUP])
                link(ins)
                mods(waiting[:1])
                link(V.tensor_tensor(gscore, top[:, :, 0], top[:, :, 1], ALU.add))
                for g in range(G):
                    ins = V.max(top4[:, g], gscore[:, g * GROUPS:(g + 1) * GROUPS])
                link(ins)
                link(V.memset(top4[:, :, TOPK_GROUPS:GROUPS], GONE / 2))
                for g in range(G):
                    ins = V.match_replace(gtaken[:, g * GROUPS:(g + 1) * GROUPS], top4[:, g],
                                          gscore[:, g * GROUPS:(g + 1) * GROUPS], GONE)
                link(ins)
                link(V.tensor_tensor(gmask, gtaken, gscore, ALU.not_equal))
                link(V.tensor_scalar(gpen, gmask, -LOW, LOW, ALU.mult, ALU.add))
                gsel3 = gsel.rearrange("p (a b) -> p a b", b=PER_GROUP)
                link(V.tensor_tensor(gsel3, select.rearrange("p (a b) -> p a b", b=PER_GROUP), along(gmask, PER_GROUP), ALU.mult))
                link(V.tensor_tensor(gsel3, gsel3, along(gpen, PER_GROUP), ALU.add))
                mods(waiting[1:2])
                split_to(turn_unit(l, 0))
                for g in range(G):
                    ins = V.max(top8[:, g], gsel[:, g * EXPERTS:(g + 1) * EXPERTS])
                link(ins)
                for g in range(G):
                    ins = V.match_replace(taken[:, g * EXPERTS:(g + 1) * EXPERTS], top8[:, g],
                                          gsel[:, g * EXPERTS:(g + 1) * EXPERTS], GONE)
                link(ins)
                link(V.tensor_tensor(taken, taken, gsel, ALU.not_equal))
                link(V.tensor_tensor(taken, taken, score, ALU.mult))
                taken3 = taken.rearrange("p (g e) -> p g e", g=G)
                link(V.tensor_reduce(wsum, taken3, AX.X, ALU.add))
                link(V.reciprocal(wsum, wsum))
                link(V.tensor_tensor(taken3, taken3, along(wsum, EXPERTS), ALU.mult))
                V.tensor_scalar(taken, taken, ROUTED_SCALE, None, ALU.mult).then_inc(gates_made, 1)
                mods(waiting[2:])
                dve.wait_ge(gates_t, l + 1)
                V.tensor_copy(gate_t, ps[0:EXPERTS, 7, 0:TOK]).then_inc(gates_t_out, 1)

            def experts(l):
                u0 = turn_unit(l, 0)
                s0 = SPLIT_NO[u0]

                def lo_down_of(t, slot):
                    dve.wait_ge(down_hi, l * TURNS + 1 + t)
                    V.tensor_tensor(lo_down[:, slot, :], raw_down[:, slot, :], hi_down[:, slot, :].bitcast(F32), ALU.subtract) \
                        .then_inc(down_lo, 1)

                def hidden_of(t, slot, bank, gslot, gate_count):
                    done = l * TURNS + 1 + t
                    dve.wait_ge(silu_out, done)
                    V.tensor_tensor(ex_up[:, slot, :], ex_silu[:, slot, :], ps[:, bank, TOK:2 * TOK], ALU.mult).then_inc(up_read, 1)
                    dve.wait_ge(up_read, done)
                    if gate_count is None:
                        dve.wait_ge(ones_set, l + 1)
                    else:
                        dve.wait_ge(gate_loaded[gslot], gate_count)
                    V.tensor_tensor(ex_h[:, slot, :], ex_up[:, slot, :], ex_gate[:, gslot, :], ALU.mult).then_inc(h_ready, 1)
                    dve.wait_ge(h_ready, done)
                    if not (isinstance(t, int) and l * TURNS + t < 2):
                        dve.wait_ge(down_used, l * TURNS - 1 + t)
                    V.tensor_copy(hid_hi[:, slot, :], ex_h[:, slot, :]).then_inc(h_hi, 1)
                    dve.wait_ge(h_hi, done)
                    V.tensor_tensor(hid_lo[:, slot, :], ex_h[:, slot, :], hid_hi[:, slot, :].bitcast(F32), ALU.subtract) \
                        .then_inc(h_lo, 1)

                def gate_count(t):
                    return None if t == 0 else 16 * (l * (EXPERTS // 4) + (t + 3) // 4)

                def turn(t, j, extra=0):
                    b = pair(l, j - 1)
                    lo_down_of(t - 1, b)
                    lo_main_of(s0 + t, (u0 + j) % RAW, (s0 + j) % 2)
                    c = gate_count(j - 1)
                    hidden_of(t - 1, b, 4 + (u0 + j - 1) % 2, (j - 1) % 4, None if c is None else c + 4 * extra)

                for t in range(1, 5):
                    turn(t, t)
                with dve.Fori(0, LOOPS) as i:
                    for j in range(4):
                        turn(5 + j + 4 * i, 5 + j, 4 * i)
                last = TURNS - 1
                lo_down_of(last, pair(l, last))
                hidden_of(last, pair(l, last), 4 + (u0 + last) % 2, last % 4, gate_count(last))
                split[0] = s0 + TURNS

            link(V.memset(cond_pad[:, :, :], 0.0))
            dve.wait_ge(cond_ready, 1)
            V.tensor_copy(cond_pad[:, :, 0:G], cond_s[:, :, :].rearrange("p g k -> p k g")).then_inc(cond_ready, 1)
            dve.wait_ge(decay_ready, 1)
            link(V.tensor_scalar(decay[:, 48:60], decay[:, 0:12], 0.0, None, ALU.min))
            V.tensor_tensor(decay[:, 48:60], decay[:, 48:60], decay[:, 36:48], ALU.subtract).then_inc(decay_ready, 1)
            dve.wait_ge(decay_ready, 2)
            dve.wait_ge(early_in, 16)
            for d in range(2):
                ins = V.tensor_scalar(small[:, 8 + 4 * d:12 + 4 * d], decay[:, 48 + 4 * d:52 + 4 * d], E("pos_col")[:, d:d + 1],
                                      None, ALU.mult)
                ins.then_inc(decay_ready, 1)
            dve.wait_ge(decay_ready, 16)
            for d, mask in enumerate(("mask_f", "mask_b")):
                ins = V.tensor_tensor(dec_e[:, d], dec_e[:, d], over(E(mask), H), ALU.mult)
            link(ins)
            link(V.tensor_tensor(dmat, dec_e[:, 0], dec_e[:, 1], ALU.add))
            dve.wait_ge(decay_ready, 17)
            V.memset(small[:, 48:49], 0.0).then_inc(k_dec_ready, 1)
            dve.wait_ge(consts_in, 16)

            for l in range(DEPTH):
                if l == 0:
                    mods(FIRST_MODS)
                split_to(in_unit(l, 1))
                make_x(l, 0, 0, 1)
                split_to(in_unit(l, IN_UNITS[l] - 1))
                if l == 0:
                    dve.wait_ge(in_out, 1)
                    link(V.tensor_tensor(q_dec, q_dup[:, :, P:TOK], q_pow, ALU.mult))
                    dve.wait_ge(att_s, 1)
                    for par in range(2):
                        for g in range(G):
                            ins = V.tensor_tensor(att_d[:, par, g],
                                                  ps[:, 6 + par, g * 2 * P:(g + 1) * 2 * P].rearrange("p (h t) -> p h t", h=2),
                                                  dmat[:, par::2, :], ALU.mult)
                    ins.then_inc(att_d_ready, 1)
                    dve.wait_ge(k_t, 1)
                    kt = ps[:, 3, 0:H * DK].rearrange("p (h d) -> p h d", h=H)
                    for d in range(2):
                        ins = V.tensor_tensor(k_dec[:, :, d, :], kt, along(small[:, 4 * d:4 * d + 4], DK), ALU.mult)
                    ins.then_inc(k_dec_ready, 1)
                    dve.wait_ge(bias_in, 16 * 2 * H)
                    bias3 = bias.rearrange("p h a c -> p h (a c)")
                    link(V.tensor_tensor(bias3, bias3, over(K("window"), H), ALU.add))
                    softmax_in(0, (0, 1, 2))
                else:
                    qk = proj[:, 6:9, :].rearrange("p a (b c) -> p (a b) c", b=4)
                    dve.wait_ge(sq_ready, 1)
                    V.tensor_reduce(small[:, 92:104], sq, AX.X, ALU.add).then_inc(ms_ready, 1)
                    dve.wait_ge(small_in, 80)
                    dve.wait_ge(rms_ready, 1)
                    link(V.reciprocal(small[:, 124:136], small[:, 80:92]))
                    link(V.tensor_tensor(qk, qk, along(small[:, 124:136], P), ALU.mult))
                    V.tensor_tensor(qk[:, 0:8], qk[:, 0:8], over(gains[:, 0], 8), ALU.mult).then_inc(qk_normed, 1)
                    V.tensor_tensor(qk[:, 8:12], qk[:, 8:12], over(gains[:, 1], 4), ALU.mult).then_inc(qk_normed, 1)
                    dve.wait_ge(qk_normed, 2)
                    lat = proj[:, 6:9, UNIT:2 * UNIT].rearrange("p a (b c e) -> p a b c e", b=2, e=2)
                    ro = roped.rearrange("p (a b) (c e) -> p a b c e", b=2, e=2)
                    tmp = sq.rearrange("p h t -> p (h t)")
                    t1 = tmp[:, 0:384].rearrange("p (a b c) -> p a b c", a=3, b=2)
                    t2 = tmp[:, 384:768].rearrange("p (a b c) -> p a b c", a=3, b=2)

                    def ang(x):
                        return x.unsqueeze(1).unsqueeze(1).broadcast_to([P, 3, 2, P // 2])

                    V.tensor_tensor(ro[:, :, :, :, 0], lat[:, :, :, :, 0], ang(K("cos")), ALU.mult)
                    V.tensor_tensor(ro[:, :, :, :, 1], lat[:, :, :, :, 0], ang(K("sin")), ALU.mult)
                    V.tensor_tensor(t1, lat[:, :, :, :, 1], ang(K("sin")), ALU.mult)
                    link(V.tensor_tensor(t2, lat[:, :, :, :, 1], ang(K("cos")), ALU.mult))
                    V.tensor_tensor(ro[:, :, :, :, 0], ro[:, :, :, :, 0], t1, ALU.subtract)
                    V.tensor_tensor(ro[:, :, :, :, 1], ro[:, :, :, :, 1], t2, ALU.add).then_inc(roped_ready, 1)
                    softmax_in(1, (6, 7, 0))
                    dve.wait_ge(qk_tr, 4)
                    cg = proj[:, 2:4, :].rearrange("p a (b c) -> p (a b) c", b=4)
                    ug = proj[:, 4:6, :].rearrange("p a (b c) -> p (a b) c", b=4)
                    link(V.memset(z_pad, 0.0))
                    link(V.tensor_tensor(z_pad[:, :, 1:P + 1], cg, ug, ALU.mult))
                    for w in range(3):
                        for t in range(4):
                            zi = z_pad[:, 2 * t:2 * t + 2, w:w + P]
                            if w == 0:
                                ins = V.tensor_scalar(conv_o[:, t], zi, cv_w[:, w, t:t + 1], None, ALU.mult)
                            else:
                                ins = V.scalar_tensor_tensor(out=conv_o[:, t], in0=zi, scalar=cv_w[:, w, t:t + 1],
                                                             in1=conv_o[:, t], op0=ALU.mult, op1=ALU.add)
                        link(ins)
                    bg = proj[:, 0:2, :].rearrange("p a (b c) -> p (a b) c", b=2)
                    link(V.tensor_tensor(x_feat[:, 0:4, :], bg, conv_o.rearrange("p t g n -> p t (g n)"), ALU.mult))
                mods(MIX_MODS[l][0])
                normalise(sc_ctx, P, 2 * l + 1)
                normalise(sc_lat, 2 * P, 2 * l + 2)
                if l == 0:
                    dve.wait_ge(state_mm, 1)
                    V.tensor_copy(st_out, ps[:, 3, :].rearrange("p (h v) -> p h v", h=H)).then_inc(state_copied, 1)
                mods(MIX_MODS[l][1])
                if l == 0:
                    stats = decay.rearrange("p (n c) -> p n c", c=6)
                    for g in range(G):
                        dve.wait_ge(ret_o, g + 1)
                        for h in range(H):
                            ins = V.bn_stats(stats[:, 4 * g + h], ps[:, 6 + g, h * P:(h + 1) * P])
                    link(ins)
                    for n in range(G * H):
                        ins = V.bn_aggr(small[:, 136 + 2 * n:138 + 2 * n], stats[:, n])
                    link(ins)
                    mv = small[:, 136:152].rearrange("p (n c) -> p n c", c=2)
                    V.tensor_copy(small[:, 24:32], mv[:, :, 1]).then_inc(ret_var, 1)
                    dve.wait_ge(ret_sd, 1)
                    link(V.reciprocal(small[:, 50:58], small[:, 16:24]))
                    for g in range(G):
                        for h in range(H):
                            ins = V.scalar_tensor_tensor(out=even_gate(h, g), in0=ps[:, 6 + g, h * P:(h + 1) * P],
                                                         scalar=mv[:, 4 * g + h, 0:1], in1=even_gate(h, g),
                                                         op0=ALU.subtract, op1=ALU.mult)
                    link(ins)
                    for g in range(G):
                        for h in range(H):
                            ins = V.tensor_scalar(even_gate(h, g), even_gate(h, g), small[:, 50 + 4 * g + h:51 + 4 * g + h], None,
                                                  ALU.mult)
                    ins.then_inc(ret_ready, 1)
                mods(MIX_MODS[l][2])
                att_out(l, 0, 3 if l == 0 else 1)
                att_out(l, 1, 0 if l == 0 else 2)
                if l == 0:
                    for g in range(G):
                        dve.wait_ge(ret_t, g + 1)
                        link(V.tensor_copy(x_feat[:, 0:H, g * P:(g + 1) * P], ps[:, 6 + g, :].rearrange("p (h t) -> p h t", h=H)))
                V.memset(small[:, 48:49], 0.0).then_inc(cat_ready, 1)
                split_to(out_unit(l, 1))
                cat_lo(l)
                split_to(out_unit(l, OUT_UNITS - 1))
                post_norm(l, 0, NORM_MODS[l])
                make_x(l, 1, 2, 3)
                route(l)
                experts(l)
                post_norm(l, 1, LAST_MODS[l])

        @block.tensor
        def _(pe):
            def mm(out, w, x, start, stop):
                return nc.tensor.matmul(out, w, x, start=start, stop=stop)

            def turned(out, x, ident=None):
                return nc.tensor.transpose(out, x, K("ident") if ident is None else ident)

            def parts(out, pairs, first=True, last=True):
                n = len(pairs)
                for i, (w, x) in enumerate(pairs):
                    ins = mm(out, w, x, first and i == 0, last and i == n - 1)
                return ins

            def bank_free(u):
                kind, l, n = KIND.get(u - 2, ("none", 0, 0))
                if kind == "mod":
                    pe.wait_ge(mod_rows_out, MOD_NO[kind, l, n] + 1)
                if kind == "in":
                    pe.wait_ge(in_out, in_before(l) + n + 1)
                if KIND.get(u - 1) in FOLD_NO:
                    pe.wait_ge(mod_t_out, FOLD_NO[KIND[u - 1]] + 1)

            def mod(l, n):
                u = mod_unit(l, n)
                bank_free(u)
                if u == 0:
                    pe.wait_ge(cond_ready, 2)
                w = raw_main[:, u % RAW, :].rearrange("p (k n) -> p k n", k=KC)
                pe.wait_ge(main_loaded[u % RAW], LOADED[u])
                for i in range(KC // 4):
                    for j in range(4):
                        k = 4 * i + j
                        ins = mm(ps[COL * j:COL * (j + 1), 4 + u % 2, 0:UNIT], cond_pad[:, k, :], w[:, k], i == 0, k >= KC - 4)
                ins.then_inc(main_used, 1)
                if ("mod", l, n) in FOLD_NO:
                    pe.wait_ge(mod_rows_out, MOD_NO["mod", l, n] + 1)
                    rows = mod_row[:, :].rearrange("r (p k) -> r k p", k=KC)
                    for k in range(KC):
                        ins = mm(ps[:, 4 + (u + 1) % 2, G * k:G * k + G], rows[:, k], K("fold"), True, True)
                    ins.then_inc(mod_t, 1)

            def mods(these):
                for l, n in these:
                    mod(l, n)

            def x_turned(l, n):
                for g in range(G):
                    if l == 0 and n == 0:
                        pe.wait_ge(x_in, 32)
                    else:
                        pe.wait_ge(normed, G * (2 * l + n - 1) + g + 1)
                    v = x_tok[:, g, :].rearrange("p (m k) -> p k m", k=KC)
                    for k in range(KC):
                        ins = turned(ps[:, 2 * g + k // 4, (k % 4) * P:(k % 4 + 1) * P], v[:, k])
                    ins.then_inc(xt_done, 1)

            def x_parts_ready(l, n):
                pe.wait_ge(x_hi_done, 2 * (3 * l + n + 1))
                pe.wait_ge(x_lo_done, 2 * (3 * l + n + 1))

            def by_features(u, bank):
                w = [t[:, SPLIT_NO[u] % 2, :].rearrange("p (k n) -> p k n", k=KC) for t in (hi_main, lo_main)]
                for t in range(2):
                    c = slice(t * P, (t + 1) * P)
                    if t == 0:
                        pe.wait_ge(main_hi, SPLIT_NO[u] + 1)
                    hh = [(w[0][:, k, c], x_hi[:, k, :]) for k in range(KC)] + [(w[0][:, k, c], x_lo[:, k, :]) for k in range(KC)]
                    lh = [(w[1][:, k, c], x_hi[:, k, :]) for k in range(KC)]
                    parts(ps[:, bank, t * TOK:(t + 1) * TOK], hh, last=False)
                    if t == 0:
                        pe.wait_ge(main_lo, SPLIT_NO[u] + 1)
                    ins = parts(ps[:, bank, t * TOK:(t + 1) * TOK], lh, first=False)
                ins.then_inc(main_used, 1)

            def by_tokens(u, bank):
                w = [t[:, SPLIT_NO[u] % 2, :].rearrange("p (k n) -> p k n", k=KC) for t in (hi_main, lo_main)]
                for g in range(G):
                    c = slice(g * P, (g + 1) * P)
                    if g == 0:
                        pe.wait_ge(main_hi, SPLIT_NO[u] + 1)
                    hh = [(x_hi[:, k, c], w[0][:, k]) for k in range(KC)] + [(x_lo[:, k, c], w[0][:, k]) for k in range(KC)]
                    hl = [(x_hi[:, k, c], w[1][:, k]) for k in range(KC)]
                    parts(ps[:, bank, g * UNIT:(g + 1) * UNIT], hh, last=False)
                    if g == 0:
                        pe.wait_ge(main_lo, SPLIT_NO[u] + 1)
                    ins = parts(ps[:, bank, g * UNIT:(g + 1) * UNIT], hl, first=False)
                ins.then_inc(main_used, 1)

            def head(bank, h, width=P):
                return ps[:, bank, h * width:(h + 1) * width]

            def probs_turned(l, banks):
                pe.wait_ge(probs, 2 * l + 1)
                for h in range(H):
                    ins = turned(head(banks[0], h), sc_ctx[:, h])
                ins.then_inc(probs_t, 1)
                pe.wait_ge(probs, 2 * l + 2)
                for n in range(2):
                    for h in range(H):
                        ins = turned(head(banks[1 + n], h), sc_lat[:, h, n * P:(n + 1) * P])
                    ins.then_inc(probs_t, 1)

            def attended(l, values, cached, banks):
                pe.wait_ge(probs_t_out, 3 * l + 1)
                for h in range(H):
                    ins = mm(head(banks[0], h), values(h, 0), pr_t[:, 0, h], True, True)
                ins.then_inc(att_o, 1)
                pe.wait_ge(probs_t_out, 3 * l + 3)
                pe.wait_ge(cache_v_in, 16 * (l + 1))
                for h in range(H):
                    mm(head(banks[1], h), values(h, 1), pr_t[:, 1, h], True, False)
                    ins = mm(head(banks[1], h), cached(h), pr_t[:, 2, h], False, True)
                ins.then_inc(att_o, 1)

            def gates_spread(l, n):
                for g in range(G):
                    sel = K("pick")[:, g * P:(g + 1) * P]
                    for c in range(2):
                        ins = mm(ps[:, 4 + 2 * g + c, :], sel, gate_row[:, n, c * 512:(c + 1) * 512], True, True)
                    ins.then_inc(gates_mm, 1)

            def experts(l):
                u0 = turn_unit(l, 0)
                s0 = SPLIT_NO[u0]

                def gate_up(s, half, bank):
                    w = [t[:, half, :].rearrange("p (k w n) -> p w k n", k=KC, w=2) for t in (hi_main, lo_main)]
                    pe.wait_ge(main_hi, s + 1)
                    for i in range(2):
                        out = ps[:, bank, i * TOK:(i + 1) * TOK]
                        hh = [(w[0][:, i, k], x_hi[:, k, :]) for k in range(KC)] + [(w[0][:, i, k], x_lo[:, k, :]) for k in range(KC)]
                        lh = [(w[1][:, i, k], x_hi[:, k, :]) for k in range(KC)]
                        parts(out, hh, last=False)
                        if i == 0:
                            pe.wait_ge(main_lo, s + 1)
                        ins = parts(out, lh, first=False)
                    ins.then_inc(main_used, 1)

                def down(t, slot, first, last):
                    done = l * TURNS + 1 + t
                    pe.wait_ge(down_hi, done)
                    pe.wait_ge(down_lo, done)
                    pe.wait_ge(h_hi, done)
                    pe.wait_ge(h_lo, done)
                    for g in range(G):
                        hh, hl = (x[:, slot, g * P:(g + 1) * P] for x in (hid_hi, hid_lo))
                        for c in range(2):
                            wh, wl = (x[:, slot, c * 512:(c + 1) * 512] for x in (hi_down, lo_down))
                            ins = parts(ps[:, 2 * g + c, :], [(hh, wh), (hh, wl), (hl, wh)], first=first, last=last)
                    ins.then_inc(down_used, 1)

                def turn(t, j):
                    gate_up(s0 + t, (s0 + j) % 2, 4 + (u0 + j) % 2)
                    down(t - 1, pair(l, j - 1), j == 1, False)

                bank_free(u0)
                gate_up(s0, s0 % 2, 4 + u0 % 2)
                bank_free(u0 + 1)
                for t in range(1, 5):
                    turn(t, t)
                with pe.Fori(0, LOOPS) as i:
                    for j in range(4):
                        turn(5 + j + 4 * i, 5 + j)
                down(TURNS - 1, pair(l, TURNS - 1), False, True)

            pe.wait_ge(consts_in, 16)
            for l in range(DEPTH):
                if l == 0:
                    mods(FIRST_MODS)
                    pe.wait_ge(cache_k_in, 16)
                    for h in range(H):
                        ins = turned(head(7, h), kc_in[:, h])
                    ins.then_inc(cache_t, 1)
                x_turned(l, 0)
                x_parts_ready(l, 0)
                for n in range(IN_UNITS[l]):
                    u = in_unit(l, n)
                    bank_free(u)
                    feat = n in (0, 1, 6, 7, 8, 9) if l == 0 else n < 6
                    (by_features if feat else by_tokens)(u, 4 + u % 2)
                pe.wait_ge(in_out, in_before(l) + IN_UNITS[l])
                if l == 0:
                    pe.wait_ge(cache_t_out, 1)
                    for h in range(H):
                        for g in range(G):
                            at = (2 * g + h // 2) * P
                            ins = mm(ps[:, 6 + h % 2, at:at + P], k_low[:, h, g * P:(g + 1) * P],
                                     q_dup[0:DK, h, g * P:(g + 1) * P], True, True)
                    ins.then_inc(att_s, 1)
                    for h in range(H):
                        ins = turned(head(3, h, DK), k_low[:, h, 0:P], K("ident", DK)[:, 0:DK])
                    ins.then_inc(k_t, 1)
                    for h in range(H):
                        ins = mm(head(0, h), na_q(h, 0), na_k(h, 0), True, True)
                    ins.then_inc(scores, 1)
                    for h in range(H):
                        mm(head(1, h), na_q(h, 1), na_k(h, 1), True, True)
                    for h in range(H):
                        ins = mm(head(2, h), na_q(h, 1), kc_t[:, h], True, True)
                    ins.then_inc(scores, 1)
                    mods(MIX_MODS[l][0])
                    pe.wait_ge(k_dec_ready, 2)
                    for h in range(H):
                        ins = mm(head(3, h), k_dec[:, h].rearrange("p d k -> p (d k)"), even_v(h, 0), True, True)
                    ins.then_inc(state_mm, 1)
                    pe.wait_ge(att_d_ready, 1)
                    pe.wait_ge(state_in, 32)
                    for g in range(G):
                        for h in range(H):
                            ins = mm(head(6 + g, h), att_d[:, h % 2, g, h // 2], even_v(h, g), True, g == 0)
                            if g == 1:
                                ins = mm(head(6 + g, h), q_dec[:, h], s0[:, h], False, True)
                        ins.then_inc(ret_o, 1)
                    mods(MIX_MODS[l][1])
                    probs_turned(l, (0, 1, 2))
                    mods(MIX_MODS[l][2])
                    pe.wait_ge(state_copied, 1)
                    attended(l, na_v, lambda h: vc[:, h], (3, 0))
                    pe.wait_ge(ret_ready, 1)
                    for g in range(G):
                        for h in range(H):
                            ins = turned(head(6 + g, h), even_gate(h, g))
                        ins.then_inc(ret_t, 1)
                    for h in range(H):
                        ins = turned(head(2, h), na_k(h, 0))
                    ins.then_inc(kn_t, 1)
                else:
                    pe.wait_ge(qk_normed, 2)
                    for n in range(6):
                        ins = turned(head(0 if n < 4 else 1, n % 4), proj[:, 6 + n // 2, (n % 2) * P:(n % 2) * P + P])
                        if n in (3, 5):
                            ins.then_inc(qk_tr, 1)
                    pe.wait_ge(roped_ready, 1)
                    for n in range(6):
                        ins = turned(head(2 if n < 4 else 3, n % 4), roped[:, n])
                        if n in (3, 5):
                            ins.then_inc(qk_tr, 1)
                    pe.wait_ge(cache_k_in, 32)
                    for h in range(KVH):
                        ins = turned(head(7, h), kc_in1[:, h])
                    ins.then_inc(cache_t, 1)
                    pe.wait_ge(qk_t_out, 4)
                    for h in range(H):
                        ins = mm(head(6, h), qk_t[:, h], qk_t[:, 4 + h // 2], True, True)
                    pe.wait_ge(cache_t_out, 2)
                    for h in range(H):
                        mm(head(7, h), qk_t[:, 6 + h], qk_t[:, 10 + h // 2], True, True)
                    for h in range(H):
                        ins = mm(head(0, h), qk_t[:, 6 + h], kc_t1[:, h // 2], True, True)
                    ins.then_inc(scores, 2)
                    mods(MIX_MODS[l][0] + MIX_MODS[l][1])
                    probs_turned(l, (6, 7, 0))
                    mods(MIX_MODS[l][2])
                    attended(l, lambda h, g: att_v(h // 2, g), lambda h: vc1[:, h // 2], (1, 2))
                x_parts_ready(l, 1)
                if l == 0:
                    pe.wait_ge(kn_out, 1)
                for n in range(OUT_UNITS):
                    by_tokens(out_unit(l, n), n)
                rows, folds = mods_before(out_unit(l, 0))
                pe.wait_ge(mod_rows_out, rows)
                pe.wait_ge(mod_t_out, folds)
                gates_spread(l, 0)
                pe.wait_ge(gate_copied, G * (2 * l + 1))
                mods(NORM_MODS[l])
                x_turned(l, 1)
                x_parts_ready(l, 2)
                pe.wait_ge(router_in, 32 * (l + 1))
                for g in range(G):
                    for k in range(KC):
                        ins = mm(ps[:, 6, g * EXPERTS:(g + 1) * EXPERTS], x_feat[:, k, g * P:(g + 1) * P], rw[:, k], k == 0, k == KC - 1)
                ins.then_inc(logits, 1)
                mods(ROUTE_MODS[l])
                pe.wait_ge(gates_made, l + 1)
                for g in range(G):
                    ins = turned(ps[0:EXPERTS, 7, g * P:(g + 1) * P], taken[:, g * EXPERTS:(g + 1) * EXPERTS])
                ins.then_inc(gates_t, 1)
                experts(l)
                gates_spread(l, 1)
                pe.wait_ge(gate_copied, G * (2 * l + 2))
                mods(LAST_MODS[l])


_INS = ['x_prompt', 'x_sample', 'c', 'state_ret', 'cache_na_k', 'cache_na_v', 'cache_att_k', 'cache_att_v', 'c_ctx',
        'w_mod', 'b_mod', 'ln_g', 'ln_b', 'w_in_even', 'w_out_even', 'ret_decay_logit', 'na_rpb', 'w_in_odd', 'w_out_odd',
        'conv_w', 'q_norm_g', 'k_norm_g', 'router_w', 'router_b', 'exp_w_gate', 'exp_w_up', 'exp_w_down',
        'sh_w_gate', 'sh_w_up', 'sh_w_down']
_OUTS = [('y_prompt', (1, 128, 1024)), ('y_sample', (1, 128, 1024)), ('state', (1, 1, 2, 4, 64, 128)),
         ('na_k', (1, 1, 128, 4, 128)), ('na_v', (1, 1, 128, 4, 128)),
         ('att_k', (1, 1, 128, 2, 128)), ('att_v', (1, 1, 128, 2, 128))]


def kernel(**inputs):
    import concourse.bacc as _bacc
    from concourse.bass_utils import run_bass_kernel_spmd as _run

    nc = _bacc.Bacc("TRN2", target_bir_lowering=False, num_devices=1)
    arrays = {name: np.ascontiguousarray(inputs[name]) for name in _INS}
    arrays["shape_consts"] = shape_constants()
    ins = {}
    for name, a in arrays.items():
        ins[name] = nc.dram_tensor(f"in_{name}", a.shape, mybir.dt.from_np(a.dtype), kind="ExternalInput").ap()
    outs = {name: nc.dram_tensor(f"out_{name}", shape, F32, kind="ExternalOutput").ap() for name, shape in _OUTS}
    build(nc, ins, outs)
    r = _run(nc, [{f"in_{name}": a for name, a in arrays.items()}], core_ids=[0])
    return tuple(r.results[0][f"out_{name}"] for name, _ in _OUTS)
```

```python
from contextlib import ExitStack

import numpy as np

import concourse.bass as bass
from concourse import mybir

F32 = mybir.dt.float32
F32R = mybir.dt.float32r
ACT = mybir.ActivationFunctionType
ALU = mybir.AluOpType
AX = mybir.AxisListType

P = 128
D = 1024
KC = D // P
G = 2
TOK = G * P
DEPTH = 2
GRID_W = 64
H = 4
DK = 64
KVH = 2
UNIT = 256
COL = 32
EXPERTS = 64
HID = 128
GROUPS = 8
PER_GROUP = EXPERTS // GROUPS
TOPK_GROUPS = 4
ROUTED_SCALE = 2.5
ALPHA = (2 * DEPTH) ** 0.25
LN_EPS = 1e-5
RMS_EPS = 1e-6
ATT_SCALE = float(P) ** -0.5
KEY_SCALE = float(DK) ** -0.5
LOW = -1.0e30
GONE = -3.0e38

SEC = D // UNIT
IN_UNITS = (12, 10)
OUT_UNITS = D // UNIT
TURNS = EXPERTS + 1
LOOPS = (TURNS - 5) // 4

FIRST_MODS = [(0, n) for n in range(8)]
IN_MODS = [[[(0, 8 + n)] for n in range(11)] + [[(0, 19), (0, 20)]], [[(1, 13 + n)] if 2 <= n < 7 else [] for n in range(10)]]
NORM_MODS = [[(0, n) for n in range(21, 24)], [(1, n) for n in range(22, 24)]]
LAST_MODS = [[(1, n) for n in range(20, 22)], []]
NEXT = LOOPS


def stream():
    out = [("mod", *m) for m in FIRST_MODS]
    for l in range(DEPTH):
        for n in range(IN_UNITS[l]):
            out += [("in", l, n)] + [("mod", *m) for m in IN_MODS[l][n]]
        out += [("out", l, n) for n in range(OUT_UNITS)]
        out += [("mod", *m) for m in NORM_MODS[l]]
        out += [("turn", l, t) for t in range(TURNS)]
        out += [("mod", *m) for m in LAST_MODS[l]]
    return out


STREAM = stream()
UNIT_NO = {key: u for u, key in enumerate(STREAM)}
SPLIT = [u for u, key in enumerate(STREAM) if key[0] != "mod"]
SPLIT_NO = {u: s for s, u in enumerate(SPLIT)}
MODS = [key[1:] for key in STREAM if key[0] == "mod"]
MOD_NO = {key: m for m, key in enumerate(MODS)}
FOLDS = [(l, n) for l in range(DEPTH) for n in (3, 7, 15, 19)]
FOLD_NO = {key: i for i, key in enumerate(FOLDS)}


def mod_unit(l, n):
    return UNIT_NO["mod", l, n]


def in_unit(l, n):
    return UNIT_NO["in", l, n]


def out_unit(l, n):
    return UNIT_NO["out", l, n]


def turn_unit(l, t):
    return UNIT_NO["turn", l, t]


def pair(l, t):
    return (l * TURNS + t) % 2


def in_before(l):
    return sum(IN_UNITS[:l])


def cat_parts(l):
    return sum((4, 3)[:l])


def mods_before(u):
    return sum(mod_unit(*m) < u for m in MODS)


def mod_bank(l, n):
    among = any((l, n) in m for m in IN_MODS[l] + LAST_MODS)
    return (6 if among else 4) + MOD_NO[l, n] % 2


RAW = 4
MOD_RAW = 3
LOADED, _at = [], [0] * RAW
for _s, _u in enumerate(SPLIT):
    _at[_s % RAW] += 32 if STREAM[_u][0] == "turn" else 16
    LOADED.append(_at[_s % RAW])

KEPT = dict(ident=128, cos=64, sin=64, window=128, pick=2 * 128, one=1, ln_eps=1, rms_eps=1, fold=2, plus=1)
EARLY = dict(rel_f=128, rel_b=128, mask_f=128, mask_b=128, pos_row=128, pos_col=2)


def columns(widths, at=0):
    out = {}
    for name, w in widths.items():
        out[name] = (at, at + w)
        at += w
    return out, at


KEPT_AT, KEPT_N = columns(KEPT)
EARLY_AT, EARLY_END = columns(EARLY, KEPT_N)
EARLY_N = EARLY_END - KEPT_N


def shape_constants():
    c = np.zeros((P, EARLY_END), np.float32)

    def put(name, value):
        a, b = {**KEPT_AT, **EARLY_AT}[name]
        c[:, a:b] = value

    i = np.arange(P)
    put("ident", np.eye(P))
    n_freq = P // 4
    freqs = np.float32(10000.0) ** (-np.arange(n_freq, dtype=np.float32) / np.float32(n_freq))
    row, col = (i // GRID_W).astype(np.float32), (i % GRID_W).astype(np.float32)
    ang = np.concatenate([row[:, None] * freqs, col[:, None] * freqs], axis=1)
    put("cos", np.cos(ang))
    put("sin", np.sin(ang))
    start = np.clip(i % GRID_W - 8, 0, GRID_W - 16)
    kc = (i % GRID_W)[None, :]
    put("window", np.where((kc >= start[:, None]) & (kc < start[:, None] + 16), 0.0, LOW))
    pick = np.zeros((P, G, P))
    for g in range(G):
        pick[g::COL, g] = 1.0
    put("pick", pick.reshape(P, G * P))
    put("one", 1.0)
    fold = np.zeros((P, G))
    for g in range(G):
        fold[g::COL, g] = 1.0
    put("fold", fold)
    plus = np.zeros((P, 1))
    plus[:G] = 1.0
    put("plus", plus)
    put("ln_eps", LN_EPS)
    put("rms_eps", RMS_EPS)
    rel = (i[None, :] - i[:, None]).astype(np.float32)
    put("rel_f", np.maximum(rel, 0))
    put("rel_b", np.maximum(-rel, 0))
    put("mask_f", rel >= 0)
    put("mask_b", rel <= 0)
    put("pos_row", np.where(i[:, None] < DK, i[None, :] + 1.0, P - i[None, :]))
    put("pos_col", np.stack([P - 1.0 - i, i], axis=1))
    return c


def build(nc, A, O):
    with ExitStack() as ctx:
        def sb(name, shape, dt=F32):
            return ctx.enter_context(nc.sbuf_tensor(name, shape, dt))

        def sem(name):
            return ctx.enter_context(nc.semaphore(name))

        raw_main = sb("raw_main", [P, RAW, KC * UNIT])
        raw_down = sb("raw_down", [P, 2, D])
        raw_mod = sb("raw_mod", [P, KC * UNIT])
        hi_main = sb("hi_main", [P, 2, KC * UNIT], F32R)
        lo_main = sb("lo_main", [P, 2, KC * UNIT], F32R)
        hi_down = sb("hi_down", [P, 2, D], F32R)
        lo_down = sb("lo_down", [P, 2, D], F32R)
        x_tok = sb("x_tok", [P, G, D])
        x_feat = sb("x_feat", [P, KC, TOK])
        x_hi = sb("x_hi", [P, KC, TOK], F32R)
        x_lo = sb("x_lo", [P, KC, TOK], F32R)
        proj = sb("proj", [P, 14, 512])
        temp = sb("temp", [P, 7168])
        const = sb("const", [P, KEPT_N])
        cond = sb("cond", [P, G, KC])
        cond_s = sb("cond_s", [P, G, KC])
        cond_pad = sb("cond_pad", [P, KC, COL])
        b_rows = sb("b_rows", [P, MOD_RAW, UNIT])
        mod_row = sb("mod_row", [P, D])
        gate_row = sb("gate_row", [P, 2, D])
        mod_feat = sb("mod_feat", [P, 4, KC, G])
        hid_hi = sb("hid_hi", [P, 2, TOK], F32R)
        hid_lo = sb("hid_lo", [P, 2, TOK], F32R)
        small = sb("small", [P, 176])
        decay = sb("decay", [P, 5 * 12])

        ps = ctx.enter_context(nc.psum_tensor("ps", [P, 8, 512], F32))

        def K(name, rows=P):
            a, b = KEPT_AT[name]
            return const[0:rows, a:b]

        ln_feat = K("window")[:, 0:2 * 2 * DEPTH * KC].rearrange("p (w n k) -> p w n k", w=2, k=KC)
        early = proj[:, :, :].rearrange("p a b -> p (a b)")[:, 0:EARLY_N]

        def E(name):
            a, b = EARLY_AT[name]
            return early[:, a - KEPT_N:b - KEPT_N]

        def T(at, *shape):
            n = int(np.prod(shape))
            flat = temp[:, at:at + n]
            if len(shape) == 1:
                return flat
            letters = "abcd"[:len(shape)]
            return flat.rearrange(f"p ({' '.join(letters)}) -> p {' '.join(letters)}",
                                  **{x: s for x, s in zip(letters[1:], shape[1:])})

        sc_ctx = T(0, H, P)
        sc_lat = T(512, H, 2 * P)
        att_d = T(1536, 2, G, 2, P)
        pr_t = T(1536, 3, H, P)
        dmat = T(3072, H, P)
        k_out = T(3072, H, P)
        q_dec = T(3584, H, P)
        k_dec = T(4096, H, 2, DK)
        q_pow = T(4608, H, P)
        st_out = T(4608, H, P)
        kc_t = T(5120, H, P)
        vc = T(5632, H, P)
        s0 = T(6144, H, P)
        bias = T(6656, H, 2, GRID_W)
        kc_in = T(1536, H, P)
        rows_pad = T(0, H * 3, 127)
        dec_e = T(2048, 2, H, P)
        z_pad = T(3072, 2 * 2 * G, P + 2)
        conv_o = T(4112, 4, G, P)
        cv_w = small[:, 60:72].rearrange("p (w t) -> p w t", w=3)
        kc_t1 = T(5632, KVH, P)
        vc1 = T(5888, KVH, P)
        kc_in1 = T(6144, KVH, P)
        gains = T(6400, 2, P)
        sq = T(1536, 12, P)
        roped = T(3072, 6, P)
        qk_t = T(0, 0 + 12, P)
        ln_g = T(0, D)
        ln_b = T(1024, D)
        z = T(2048, G, D)
        rw = T(6144, KC, EXPERTS)
        rb = T(6656, EXPERTS)
        pf = proj[:, :, :].rearrange("p a b -> p (a b)")
        ex_silu = pf[:, 0:512].rearrange("p (a b) -> p a b", a=2)
        ex_up = pf[:, 512:1024].rearrange("p (a b) -> p a b", a=2)
        ex_h = pf[:, 1024:1536].rearrange("p (a b) -> p a b", a=2)
        ex_gate = pf[:, 1536:2560].rearrange("p (a b) -> p a b", a=4)
        score = pf[:, 2560:2688]
        select = pf[:, 2688:2816]
        gsel = pf[:, 2816:2944]
        taken = pf[:, 2944:3072]
        top = pf[:, 3072:3200].rearrange("p (a b) -> p a b", b=8)
        gscore = pf[:, 3200:3216]
        gtaken = pf[:, 3216:3232]
        gmask = pf[:, 3232:3248]
        gpen = pf[:, 3248:3264]
        top4 = pf[:, 3264:3280].rearrange("p (a b) -> p a b", a=2)
        top8 = pf[:, 3280:3296].rearrange("p (a b) -> p a b", a=2)
        wsum = pf[:, 3296:3298]
        gate_t = T(6720, TOK)[0:EXPERTS]
        next_raw = T(4096, KC, UNIT)
        next_rows = pf[:, 3328:3328 + NEXT * UNIT]

        def mod_raw(l, n):
            slot = MOD_NO[l, n] % MOD_RAW
            if slot == 0:
                at = raw_down[:, :, :].rearrange("p a b -> p (a b)")
            elif slot == 1:
                at = raw_mod[:, :]
            elif (l, n) in FIRST_MODS:
                at = raw_main[:, RAW - 1, :]
            elif (l, n) in NORM_MODS[l]:
                at = T(4096, KC * UNIT)
            elif (l, n) in LAST_MODS[0]:
                at = pf[:, 0:KC * UNIT]
            elif l > 0:
                at = pf[:, 5120:5120 + KC * UNIT]
            else:
                at = T(0, KC * UNIT)
            return at.rearrange("p (k n) -> p k n", k=KC)

        q_dup = proj[:, 0:2, :].rearrange("p a (b c) -> p (a b) c", b=2)
        k_low = proj[0:DK, 2:4, :].rearrange("p a (b c) -> p (a b) c", b=2)

        def even_v(h, g):
            return proj[:, 4 + h // 2, g * UNIT + (h % 2) * P:g * UNIT + (h % 2) * P + P]

        def even_gate(h, g):
            return proj[:, 6 + h // 2, g * UNIT + (h % 2) * P:g * UNIT + (h % 2) * P + P]

        def na_q(h, g):
            return proj[:, 8 + h // 2, (h % 2) * TOK + g * P:(h % 2) * TOK + g * P + P]

        def na_k(h, g):
            return proj[:, 10 + h // 2, (h % 2) * TOK + g * P:(h % 2) * TOK + g * P + P]

        def na_v(h, g):
            return proj[:, 12 + h // 2, g * UNIT + (h % 2) * P:g * UNIT + (h % 2) * P + P]

        def att_v(h, g):
            return proj[:, 9, g * UNIT + h * P:g * UNIT + h * P + P]

        pad_dram = nc.dram_tensor("pad_rows", [GRID_W, H * 3 * 127], F32, kind="Internal").ap()
        gate_dram = [nc.dram_tensor(f"gates{l}", [EXPERTS, TOK], F32, kind="Internal").ap() for l in range(DEPTH)]

        def gate_bank(l, n, g):
            return 6 if n == 1 else 4 if g == 0 else (2, 6)[l]

        def logits_of(l):
            return ps[:, 4 + (SPLIT_NO[turn_unit(l, 0)] + 1) % 2, 0:G * EXPERTS]

        def cat_part(l, part):
            def bank(b):
                return ps[:, b, :].rearrange("p (h t) -> p h t", h=H)

            latent, context = slice(P, TOK), slice(0, P)
            if l == 0:
                return ((bank(3), slice(H, 2 * H), context), (bank(0), slice(H, 2 * H), latent),
                        (bank(6), slice(0, H), context), (bank(7), slice(0, H), latent))[part]
            return ((x_feat[:, 0:H, :], slice(0, H), slice(0, TOK)), (bank(1), slice(H, 2 * H), context),
                    (bank(2), slice(H, 2 * H), latent))[part]

        main_loaded = [sem(f"main_loaded{i}") for i in range(RAW)]
        down_loaded = [sem(f"down_loaded{i}") for i in range(2)]
        mod_loaded = [sem(f"mod_loaded{i}") for i in range(MOD_RAW)]
        bias_loaded = [sem(f"bias_loaded{i}") for i in range(MOD_RAW)]
        next_loaded, next_mm, next_out = sem("next_loaded"), sem("next_mm"), sem("next_out")
        next_zero, next_bias, next_kept = sem("next_zero"), sem("next_bias"), sem("next_kept")
        gate_loaded = [sem(f"gate_loaded{i}") for i in range(4)]
        main_hi, main_lo, main_used = sem("main_hi"), sem("main_lo"), sem("main_used")
        down_hi, down_lo, down_used = sem("down_hi"), sem("down_lo"), sem("down_used")
        consts_in, early_in, x_in, cond_in = sem("consts_in"), sem("early_in"), sem("x_in"), sem("cond_in")
        decay_in, cache_k_in, cache_v_in = sem("decay_in"), sem("cache_k_in"), sem("cache_v_in")
        state_in, rpb_in, bias_in, pad_out = sem("state_in"), sem("rpb_in"), sem("bias_in"), sem("pad_out")
        window_used, ln_feat_in, ln_folded = sem("window_used"), sem("ln_feat_in"), sem("ln_folded")
        y_context = sem("y_context")
        ln_factors, standard = sem("ln_factors"), sem("standard")
        ln_in, router_in, small_in = sem("ln_in"), sem("router_in"), sem("small_in")
        pad_zero, bias_zero = sem("pad_zero"), sem("bias_zero")
        cond_ready = sem("cond_ready")
        mod_rows_out, mod_t, mod_t_out = sem("mod_rows_out"), sem("mod_t"), sem("mod_t_out")
        xt_done, x_feat_act, x_feat_dve = sem("xt_done"), sem("x_feat_act"), sem("x_feat_dve")
        x_hi_done, x_lo_done = sem("x_hi_done"), sem("x_lo_done")
        in_out = sem("in_out")
        act_chain, dve_chain = sem("act_chain"), sem("dve_chain")
        decay_ready = sem("decay_ready")
        cache_t, cache_t_out = sem("cache_t"), sem("cache_t_out")
        att_s, att_d_ready, k_t, k_dec_ready = sem("att_s"), sem("att_d_ready"), sem("k_t"), sem("k_dec_ready")
        scores, centred, exped, probs = sem("scores"), sem("centred"), sem("exped"), sem("probs")
        state_mm, state_copied = sem("state_mm"), sem("state_copied")
        ret_o, ret_var, ret_sd, ret_ready = sem("ret_o"), sem("ret_var"), sem("ret_sd"), sem("ret_ready")
        probs_t, probs_t_out, att_o = sem("probs_t"), sem("probs_t_out"), sem("att_o")
        ret_t, kn_t, kn_out = sem("ret_t"), sem("kn_t"), sem("kn_out")
        conv_ready, cat_hi_done, cat_lo_done = sem("conv_ready"), sem("cat_hi_done"), sem("cat_lo_done")
        qk_normed, roped_ready, sq_ready = sem("qk_normed"), sem("roped_ready"), sem("sq_ready")
        ms_ready, rms_ready = sem("ms_ready"), sem("rms_ready")
        qk_tr, qk_t_out = sem("qk_tr"), sem("qk_t_out")
        gates_mm, gate_copied, ln_var, ln_sd, normed = sem("gates_mm"), sem("gate_copied"), sem("ln_var"), sem("ln_sd"), sem("normed")
        logits, sigmoid_out, gates_made = sem("logits"), sem("sigmoid_out"), sem("gates_made")
        gates_t, gates_t_out, gates_stored = sem("gates_t"), sem("gates_t_out"), sem("gates_stored")
        ones_set = sem("ones_set")
        silu_out, up_read, h_ready, h_hi, h_lo = sem("silu_out"), sem("up_read"), sem("h_ready"), sem("h_hi"), sem("h_lo")
        stored, y_stored = sem("stored"), sem("y_stored")

        block = ctx.enter_context(nc.Block())

        w_in = (A["w_in_even"][0], A["w_in_odd"][0])
        w_out = (A["w_out_even"][0], A["w_out_odd"][0])

        @block.sync
        def _(sp):
            def slot_free(s):
                if s >= RAW:
                    sp.wait_ge(main_lo, s - RAW + 1)
                elif s == RAW - 1:
                    sp.wait_ge(main_used, max(m for m in range(len(FIRST_MODS)) if m % MOD_RAW == 2) + 1)

            def load_unit(u, source):
                slot = SPLIT_NO[u] % RAW
                slot_free(SPLIT_NO[u])
                sp.dma_start(raw_main[:, slot, :].rearrange("p (k n) -> p k n", k=KC), source) \
                    .then_inc(main_loaded[slot], 16)

            def load_projection(l, n):
                if n < IN_UNITS[l]:
                    load_unit(in_unit(l, n), w_in[l].rearrange("(p k) n -> p k n", k=KC)[:, :, n * UNIT:(n + 1) * UNIT])
                else:
                    n -= IN_UNITS[l]
                    load_unit(out_unit(l, n), w_out[l].rearrange("(k p) n -> p k n", k=KC)[:, :, n * UNIT:(n + 1) * UNIT])

            def load_mod(l, n):
                m, cols = MOD_NO[l, n], slice(n * UNIT, (n + 1) * UNIT)
                slot = m % MOD_RAW
                if m >= MOD_RAW:
                    sp.wait_ge(mod_rows_out, m - MOD_RAW + 1)
                else:
                    sp.wait_ge(bias_zero, 1)
                if slot == 0 and l > 0:
                    sp.wait_ge(down_lo, l * TURNS)
                if slot == 2 and (l, n) in NORM_MODS[l]:
                    sp.wait_ge(cat_lo_done, cat_parts(l + 1))
                    sp.wait_ge(stored, 16 * 4)
                elif slot == 2 and (l, n) in LAST_MODS[0]:
                    sp.wait_ge(down_used, TURNS)
                elif slot == 2 and l > 0:
                    sp.wait_ge(mod_t, FOLD_NO[l, 7] + 1)
                    sp.wait_ge(next_kept, 2)
                elif slot == 2 and (l, n) not in FIRST_MODS:
                    sp.wait_ge(pad_out, 16)
                    sp.wait_ge(cache_t, 1)
                    sp.wait_ge(k_dec_ready, 1)
                sp.dma_start(mod_raw(l, n), A["w_mod"][l].rearrange("(p k) n -> p k n", k=KC)[:, :, cols]) \
                    .then_inc(mod_loaded[slot], 16)
                sp.dma_start(b_rows[0:G, slot, :], A["b_mod"][l:l + 1, cols].partition_broadcast(G)) \
                    .then_inc(bias_loaded[slot], 16)

            def load_turn(l, t, slot, down, gate, up, out_w):
                if isinstance(t, int):
                    slot_free(SPLIT_NO[turn_unit(l, t)])
                else:
                    sp.wait_ge(main_lo, SPLIT_NO[turn_unit(l, 0)] - RAW + 1 + t)
                view = raw_main[:, slot, :].rearrange("p (k w n) -> p w k n", k=KC, w=2)
                sp.dma_start(view[:, 0], gate.rearrange("(p k) n -> p k n", k=KC)).then_inc(main_loaded[slot], 16)
                sp.dma_start(view[:, 1], up.rearrange("(p k) n -> p k n", k=KC)).then_inc(main_loaded[slot], 16)
                if isinstance(t, int) and t < 2:
                    sp.wait_ge(main_used, turn_unit(l, 0))
                else:
                    sp.wait_ge(down_lo, l * TURNS - 1 + t)
                sp.dma_start(raw_down[:, down, :], out_w).then_inc(down_loaded[down], 16)

            def expert(l, e):
                return A["exp_w_gate"][l, e], A["exp_w_up"][l, e], A["exp_w_down"][l, e]

            for l, n in FIRST_MODS:
                load_mod(l, n)
            for n in range(RAW):
                load_projection(0, n)
            for l in range(DEPTH):
                for n in range(IN_UNITS[l] + OUT_UNITS - RAW):
                    for m in IN_MODS[l][n]:
                        load_mod(*m)
                    load_projection(l, n + RAW)
                for m in NORM_MODS[l]:
                    load_mod(*m)
                s0 = SPLIT_NO[turn_unit(l, 0)]
                load_turn(l, 0, s0 % RAW, pair(l, 0), A["sh_w_gate"][l], A["sh_w_up"][l], A["sh_w_down"][l])
                for t in range(1, 5):
                    load_turn(l, t, (s0 + t) % RAW, pair(l, t), *expert(l, t - 1))
                with sp.Fori(0, LOOPS) as i:
                    for j in range(4):
                        load_turn(l, 5 + j + 4 * i, (s0 + 5 + j) % RAW, pair(l, 5 + j), *expert(l, 4 + j + 4 * i))
                        if j == 1 and l + 1 < DEPTH:
                            sp.wait_ge(next_out, i + 1)
                            source = A["w_mod"][l + 1].rearrange("(p k) n -> p k n", k=KC)
                            sp.dma_start(next_raw, source[:, :, bass.ds(i * UNIT, UNIT)]).then_inc(next_loaded, 16)
                if l + 1 < DEPTH:
                    for n in range(RAW):
                        load_projection(l + 1, n)
                for m in LAST_MODS[l]:
                    load_mod(*m)

            for g, y in enumerate((O["y_prompt"], O["y_sample"])):
                sp.wait_ge(normed, 3 * G + g + 1)
                sp.dma_start(y[0], x_tok[:, g, :]).then_inc(y_stored, 16)
            sp.wait_ge(y_stored, 32)

        @block.gpsimd
        def _(pool):
            nc.gpsimd.memset(b_rows[:, :, :], 0.0).then_inc(bias_zero, 1)
            nc.gpsimd.memset(rows_pad[0:GRID_W], 0.0).then_inc(pad_zero, 1)
            pool.wait_ge(pad_zero, 1)
            for h in range(H):
                pool.dma_start(rows_pad[0:GRID_W, 3 * h:3 * h + 3, 48:79],
                               A["na_rpb"][0, h, 6:9, :].partition_broadcast(GRID_W)).then_inc(rpb_in, 16)
            pool.wait_ge(main_used, len(FIRST_MODS) - MOD_RAW)
            pool.dma_start(kc_in, A["cache_na_k"][0, 0]).then_inc(cache_k_in, 16)
            pool.dma_start(vc, A["cache_na_v"][0, 0]).then_inc(cache_v_in, 16)
            for d in range(2):
                pool.dma_start(s0[d * DK:(d + 1) * DK], A["state_ret"][0, 0, d].rearrange("h k v -> k h v")) \
                    .then_inc(state_in, 16)
            pool.wait_ge(rpb_in, 16 * H)
            pool.dma_start(pad_dram, rows_pad[0:GRID_W].rearrange("p a b -> p (a b)")).then_inc(pad_out, 16)
            pool.wait_ge(pad_out, 16)
            for r in range(2):
                for h in range(H):
                    skew = bass.AP(pad_dram.tensor, 63 + (3 * h + 1 - r) * 127,
                                   [[H * 3 * 127 - 1, GRID_W], [127, 2], [1, GRID_W]])
                    pool.dma_start(bias[r * GRID_W:(r + 1) * GRID_W, h], skew).then_inc(bias_in, 16)

            def load_norm(l, n):
                pool.dma_start(ln_g, A["ln_g"][l, n:n + 1, :].partition_broadcast(P)).then_inc(ln_in, 16)
                pool.dma_start(ln_b, A["ln_b"][l, n:n + 1, :].partition_broadcast(P)).then_inc(ln_in, 16)

            for l in range(DEPTH):
                if l == 1:
                    pool.wait_ge(normed, 2 * G)
                    pool.dma_start(kc_in1, A["cache_att_k"][0, 0]).then_inc(cache_k_in, 16)
                    pool.dma_start(vc1, A["cache_att_v"][0, 0]).then_inc(cache_v_in, 16)
                    pool.dma_start(gains[:, 0:1], A["q_norm_g"][0:1].partition_broadcast(P)).then_inc(small_in, 16)
                    pool.dma_start(gains[:, 1:2], A["k_norm_g"][0:1].partition_broadcast(P)).then_inc(small_in, 16)
                    with nc.allow_non_contiguous_dma("1,536 values of the convolution"):
                        for w in range(3):
                            pool.dma_start(cv_w[:, w], A["conv_w"][0, w].rearrange("(t p) -> p t", p=P)) \
                                .then_inc(small_in, 16)
                if l == 0:
                    pool.wait_ge(in_out, 12)
                    pool.dma_start(O["na_v"][0, 0].rearrange("t h d -> t (h d)").rearrange("t (u c) -> t u c", u=2),
                                   proj[:, 12:14, 0:UNIT]).then_inc(stored, 16)
                    pool.wait_ge(state_copied, 1)
                    for d in range(2):
                        pool.dma_start(O["state"][0, 0, d].rearrange("h k v -> k h v"), st_out[d * DK:(d + 1) * DK]) \
                            .then_inc(stored, 16)
                    pool.wait_ge(kn_out, 1)
                    pool.dma_start(O["na_k"][0, 0], k_out).then_inc(stored, 16)
                else:
                    pool.wait_ge(in_out, in_before(1) + 10)
                    pool.dma_start(O["att_v"][0, 0].rearrange("t h d -> t (h d)"), proj[:, 9, 0:UNIT]).then_inc(stored, 16)
                    pool.wait_ge(qk_normed, 2)
                    pool.dma_start(O["att_k"][0, 0].rearrange("t h d -> t (h d)"), proj[:, 8, 0:UNIT]).then_inc(stored, 16)
                pool.wait_ge(cat_lo_done, cat_parts(l + 1))
                pool.wait_ge(stored, 16 * (4 if l == 0 else 6))
                if l == 0:
                    pool.wait_ge(window_used, 1)
                    for w, rows in enumerate((A["ln_g"], A["ln_b"])):
                        pool.dma_start(ln_feat[:, w], rows.rearrange("l n (p k) -> p (l n) k", k=KC)).then_inc(ln_feat_in, 16)
                if l + 1 < DEPTH:
                    nc.gpsimd.memset(next_rows, 0.0).then_inc(next_zero, 1)
                    pool.wait_ge(next_zero, 1)
                    pool.dma_start(next_rows[0:G], A["b_mod"][l + 1:l + 2, 0:NEXT * UNIT].partition_broadcast(G)) \
                        .then_inc(next_bias, 16)
                load_norm(l, 0)
                pool.dma_start(rw, A["router_w"][l].rearrange("(p k) e -> p k e", k=KC)).then_inc(router_in, 16)
                pool.dma_start(rb, A["router_b"][l:l + 1, :].partition_broadcast(P)).then_inc(router_in, 16)
                nc.gpsimd.memset(ex_gate[:, 0, :], 1.0).then_inc(ones_set, 1)
                if l + 1 < DEPTH:
                    pool.wait_ge(next_bias, 16)
                    ones = next_rows[:, D:3 * D]
                    nc.gpsimd.tensor_scalar(ones, ones, K("plus"), None, ALU.add).then_inc(next_out, 1)
                pool.wait_ge(gates_t_out, l + 1)
                pool.dma_start(gate_dram[l], gate_t).then_inc(gates_stored, 16)
                pool.wait_ge(gates_stored, 16 * (l + 1))

                def load_gate(t, slot):
                    if not (isinstance(t, int) and t < 4):
                        pool.wait_ge(h_ready, l * TURNS - 3 + t)
                    pool.dma_start(ex_gate[:, slot, :], gate_dram[l][bass.ds(t - 1, 1), :].partition_broadcast(P)) \
                        .then_inc(gate_loaded[slot], 16)

                for t in range(1, 5):
                    load_gate(t, t % 4)
                pool.wait_ge(normed, (2 * l + 1) * G)
                load_norm(l, 1)
                with pool.Fori(0, LOOPS) as i:
                    for j in range(4):
                        load_gate(5 + j + 4 * i, (5 + j) % 4)
                if l + 1 < DEPTH:
                    pool.wait_ge(next_out, NEXT + 1)
                    nc.gpsimd.tensor_copy(gate_row[:, 0, :], next_rows[:, 2 * D:3 * D]).then_inc(next_kept, 1)
                    nc.gpsimd.tensor_copy(mod_row[:, 0:NEXT * UNIT - 3 * D], next_rows[:, 3 * D:NEXT * UNIT]) \
                        .then_inc(next_kept, 1)

            pool.wait_ge(stored, 16 * 6)

        @block.scalar
        def _(act):
            chain = [0]

            def link(ins):
                chain[0] += 1
                ins.then_inc(act_chain, 1)
                act.wait_ge(act_chain, chain[0])

            split = [0]

            def hi_main_of(slot, half, loaded, free):
                act.wait_ge(main_loaded[slot], loaded)
                if free is not None:
                    act.wait_ge(main_used, free)
                nc.scalar.activation(hi_main[:, half, :], raw_main[:, slot, :], ACT.Copy).then_inc(main_hi, 1)

            def split_to(u):
                while split[0] < len(SPLIT) and SPLIT[split[0]] <= u:
                    s = split[0]
                    hi_main_of(s % RAW, s % 2, LOADED[s], SPLIT[s - 2] + 1 if s >= 2 else None)
                    split[0] += 1

            act.dma_start(const[:, :], A["shape_consts"][:, 0:KEPT_N]).then_inc(consts_in, 16)
            act.dma_start(cond[:, 0, :], A["c_ctx"].rearrange("(p k) -> p k", k=KC)).then_inc(cond_in, 16)
            act.dma_start(cond[:, 1, :], A["c"][0].rearrange("(p k) -> p k", k=KC)).then_inc(cond_in, 16)
            act.dma_start(x_tok[:, 0, :], A["x_prompt"][0]).then_inc(x_in, 16)
            act.dma_start(x_tok[:, 1, :], A["x_sample"][0]).then_inc(x_in, 16)
            act.dma_start(early, A["shape_consts"][:, KEPT_N:EARLY_END]).then_inc(early_in, 16)
            logit = decay[:, 0:12]
            flat = A["ret_decay_logit"].rearrange("a d h -> a (d h)")
            act.dma_start(logit[:, 0:8], flat.partition_broadcast(P)).then_inc(decay_in, 16)
            for d in range(2):
                act.dma_start(logit[d * DK:(d + 1) * DK, 8:12],
                              A["ret_decay_logit"][:, d].partition_broadcast(DK)).then_inc(decay_in, 16)
            act.wait_ge(cond_in, 32)
            nc.scalar.activation(cond_s[:, :, :], cond[:, :, :], ACT.Silu).then_inc(cond_ready, 1)

            act.wait_ge(decay_in, 48)
            act.wait_ge(consts_in, 16)
            link(nc.scalar.activation(decay[:, 12:24], logit, ACT.Abs))
            link(nc.scalar.activation(decay[:, 24:36], decay[:, 12:24], ACT.Exp, scale=-1.0))
            nc.scalar.activation(decay[:, 36:48], decay[:, 24:36], ACT.Ln, bias=K("one")).then_inc(decay_ready, 1)
            act.wait_ge(decay_ready, 2)
            act.wait_ge(early_in, 16)
            for d, rel in enumerate(("rel_f", "rel_b")):
                for h in range(H):
                    nc.scalar.activation(dec_e[:, d, h], E(rel), ACT.Exp,
                                         scale=decay[:, 48 + 4 * d + h:49 + 4 * d + h]).then_inc(decay_ready, 1)
            for h in range(H):
                nc.scalar.activation(q_pow[:, h], E("pos_row"), ACT.Exp, scale=decay[:, 56 + h:57 + h]) \
                    .then_inc(decay_ready, 1)
            act.wait_ge(decay_ready, 16)
            nc.scalar.activation(small[:, 0:8], small[:, 8:16], ACT.Exp).then_inc(decay_ready, 1)
            def make_x(l, n, shift, scale):
                if l + n == 0:
                    act.wait_ge(mod_t_out, FOLD_NO[0, 7] + 1)
                else:
                    act.wait_ge(ln_folded, 2 * l + n)
                act.wait_ge(xt_done, 2 * (2 * l + n) + 1)
                for k in range(KC):
                    ins = nc.scalar.activation(x_feat[:, k, 0:P], ps[:, k // 4, (k % 4) * P:(k % 4 + 1) * P], ACT.Identity,
                                               scale=mod_feat[:, scale, k, 0:1], bias=mod_feat[:, shift, k, 0:1])
                ins.then_inc(x_feat_act, 1)
                act.wait_ge(x_feat_act, 2 * l + n + 1)
                nc.scalar.activation(x_hi[:, :, 0:P], x_feat[:, :, 0:P], ACT.Copy).then_inc(x_hi_done, 1)
                act.wait_ge(x_feat_dve, 2 * l + n + 1)
                nc.scalar.activation(x_hi[:, :, P:TOK], x_feat[:, :, P:TOK], ACT.Copy).then_inc(x_hi_done, 1)

            def cat_hi(l, part):
                if l == 1 and part == 0:
                    act.wait_ge(conv_ready, 1)
                elif l == 1:
                    act.wait_ge(att_o, G + part)
                elif part < G:
                    act.wait_ge(att_o, part + 1)
                else:
                    act.wait_ge(ret_t, part - G + 1)
                source, k, t = cat_part(l, part)
                nc.scalar.activation(x_hi[:, k, t], source, ACT.Copy).then_inc(cat_hi_done, 1)

            def unit_copy(l, n):
                u = in_unit(l, n)
                act.wait_ge(main_used, u + 1)
                bank = ps[:, 4 + SPLIT_NO[u] % 2, :]
                if l == 1 and n == 0:
                    act.wait_ge(next_kept, 2)
                if l == 0 and n == 0:
                    act.wait_ge(k_dec_ready, 1)
                    b3 = bank.rearrange("p (t c) -> p t c", t=2)
                    for odd in range(2):
                        for half in range(2):
                            ins = nc.scalar.activation(q_dup[half * DK:(half + 1) * DK, odd::2, :],
                                                       b3[odd * DK:(odd + 1) * DK], ACT.Copy)
                    ins.then_inc(in_out, 1)
                elif l == 0 and n == 1:
                    b3 = bank.rearrange("p (t c) -> p t c", t=2)
                    for odd in range(2):
                        ins = nc.scalar.activation(k_low[:, odd::2, :], b3[odd * DK:(odd + 1) * DK], ACT.Copy,
                                                   scale=KEY_SCALE)
                    ins.then_inc(in_out, 1)
                elif l == 0:
                    nc.scalar.activation(proj[:, n + 2, :], bank, ACT.Silu if n in (4, 5) else ACT.Copy).then_inc(in_out, 1)
                else:
                    nc.scalar.activation(proj[:, n, :], bank, ACT.Copy).then_inc(in_out, 1)

            def softmax_exp(l):
                for n, s in enumerate((sc_ctx, sc_lat)):
                    act.wait_ge(centred, 2 * l + n + 1)
                    if (l, n) == (0, 1):
                        act.wait_ge(state_mm, 1)
                        nc.scalar.activation(st_out, ps[:, 3, :].rearrange("p (h v) -> p h v", h=H), ACT.Copy) \
                            .then_inc(state_copied, 1)
                    nc.scalar.activation(s, s, ACT.Exp, scale=1.0 if (l, n) == (0, 1) else ATT_SCALE).then_inc(exped, 1)

            def probs_copy(l, banks):
                for n in range(3):
                    act.wait_ge(probs_t, 3 * l + n + 1)
                    nc.scalar.activation(pr_t[:, n], ps[:, banks[n], :].rearrange("p (h t) -> p h t", h=H), ACT.Copy) \
                        .then_inc(probs_t_out, 1)

            def gate_copy(l, n, g):
                if (l, n, g) == (0, 0, 0):
                    act.wait_ge(stored, 16 * 4)
                if n == 1:
                    act.wait_ge(normed, G * 2 * l + g + 1)
                act.wait_ge(gates_mm, G * (2 * l + n) + g + 1)
                a = gate_bank(l, n, g)
                nc.scalar.activation(z[:, g, :], ps[:, a:a + 2, :].rearrange("p a b -> p (a b)"), ACT.Copy) \
                    .then_inc(gate_copied, 1)

            def norm_sd(l, n):
                for g in range(G):
                    act.wait_ge(ln_var, G * (2 * l + n) + g + 1)
                    nc.scalar.activation(small[:, 40 + g:41 + g], small[:, 33 + 2 * g:34 + 2 * g], ACT.Sqrt, bias=K("ln_eps")) \
                        .then_inc(ln_sd, 1)
                    if (l, n) != (DEPTH - 1, 1):
                        act.wait_ge(ln_factors, G * (2 * l + n) + g + 1)
                        nc.scalar.activation(z[:, g, :], z[:, g, :], ACT.Identity, scale=small[:, 42 + g:43 + g],
                                             bias=small[:, 44 + g:45 + g]).then_inc(standard, 1)

            def experts(l):
                u0 = turn_unit(l, 0)
                s0 = SPLIT_NO[u0]

                def hi_down_of(t, slot, loaded):
                    act.wait_ge(down_loaded[slot], loaded)
                    if not (isinstance(t, int) and l * TURNS + t < 2):
                        act.wait_ge(down_used, l * TURNS - 1 + t)
                    nc.scalar.activation(hi_down[:, slot, :], raw_down[:, slot, :], ACT.Copy).then_inc(down_hi, 1)

                def silu_of(t, slot, bank):
                    act.wait_ge(main_used, u0 + 1 + t)
                    if not (isinstance(t, int) and l * TURNS + t < 2):
                        act.wait_ge(up_read, l * TURNS - 1 + t)
                    nc.scalar.activation(ex_silu[:, slot, :], ps[:, bank, 0:TOK], ACT.Silu).then_inc(silu_out, 1)

                def down_count(t):
                    return 16 * ((l * TURNS + t) // 2 + 1)

                def turn(t, j, extra=0):
                    b = pair(l, j - 1)
                    hi_down_of(t - 1, b, down_count(j - 1) + 8 * extra)
                    if j > 1:
                        hi_main_of((s0 + j) % RAW, (s0 + j) % 2, LOADED[s0 + j] + 8 * extra,
                                   SPLIT[s0 + t - 2] + 1 if isinstance(t, int) else u0 + t - 1)
                    silu_of(t - 1, b, 4 + (s0 + j - 1) % 2)

                for t in range(1, 5):
                    turn(t, t)
                    if t > 2:
                        gate_copy(l, 1, t - 3)
                with act.Fori(0, LOOPS) as i:
                    for j in range(4):
                        turn(5 + j + 4 * i, 5 + j, 4 * i)
                hi_down_of(TURNS - 1, pair(l, TURNS - 1), down_count(TURNS - 1))
                silu_of(TURNS - 1, pair(l, TURNS - 1), 4 + (s0 + TURNS - 1) % 2)
                split[0] = s0 + TURNS

            split_to(in_unit(0, 0))
            for l in range(DEPTH):
                make_x(l, 0, 0, 1)
                if l == 0:
                    act.wait_ge(cache_t, 1)
                    nc.scalar.activation(kc_t, ps[:, 7, :].rearrange("p (h t) -> p h t", h=H), ACT.Copy) \
                        .then_inc(cache_t_out, 1)
                for n in range(IN_UNITS[l]):
                    split_to(in_unit(l, n + 1) if n + 1 < IN_UNITS[l] else out_unit(l, 0))
                    unit_copy(l, n)
                    if l == 1 and n == 8:
                        act.wait_ge(in_out, in_before(1) + 9)
                        nc.scalar.activation(sq, proj[:, 6:9, :].rearrange("p a (b c) -> p (a b) c", b=4), ACT.Square) \
                            .then_inc(sq_ready, 1)
                        act.wait_ge(ms_ready, 1)
                        nc.scalar.activation(small[:, 80:92], small[:, 92:104], ACT.Sqrt, scale=1.0 / P, bias=K("rms_eps")) \
                            .then_inc(rms_ready, 1)
                split_to(out_unit(l, 1))
                if l == 1:
                    cat_hi(l, 0)
                    for n in range(4):
                        act.wait_ge(qk_tr, n + 1)
                        first, count = ((0, 4), (4, 2), (6, 4), (10, 2))[n]
                        nc.scalar.activation(qk_t[:, first:first + count],
                                             ps[:, n, 0:count * P].rearrange("p (h t) -> p h t", h=count), ACT.Copy) \
                            .then_inc(qk_t_out, 1)
                    act.wait_ge(cache_t, 2)
                    nc.scalar.activation(kc_t1, ps[:, 7, 0:KVH * P].rearrange("p (h t) -> p h t", h=KVH), ACT.Copy) \
                        .then_inc(cache_t_out, 1)
                softmax_exp(l)
                probs_copy(l, (0, 1, 2) if l == 0 else (6, 7, 0))
                if l == 1:
                    cat_hi(l, 1)
                    cat_hi(l, 2)
                if l == 0:
                    act.wait_ge(ret_var, 1)
                    nc.scalar.activation(small[:, 16:24], small[:, 24:32], ACT.Sqrt, bias=K("ln_eps")).then_inc(ret_sd, 1)
                if l == 0:
                    cat_hi(l, 0)
                    cat_hi(l, 1)
                    act.wait_ge(kn_t, 1)
                    nc.scalar.activation(k_out, ps[:, 2, :].rearrange("p (h t) -> p h t", h=H), ACT.Copy).then_inc(kn_out, 1)
                    cat_hi(l, 2)
                    cat_hi(l, 3)
                gate_copy(l, 0, 0)
                gate_copy(l, 0, 1)
                split_to(out_unit(l, OUT_UNITS - 1))
                norm_sd(l, 0)
                make_x(l, 1, 2, 3)
                split_to(turn_unit(l, 1))
                act.wait_ge(logits, l + 1)
                nc.scalar.activation(score, logits_of(l), ACT.Sigmoid).then_inc(sigmoid_out, 1)
                experts(l)
                if l + 1 < DEPTH:
                    split_to(in_unit(l + 1, 1))
                norm_sd(l, 1)

        @block.vector
        def _(dve):
            chain = [0]
            V = nc.vector

            def link(ins):
                chain[0] += 1
                ins.then_inc(dve_chain, 1)
                dve.wait_ge(dve_chain, chain[0])

            split = [0]

            def lo_main_of(s, slot, half):
                dve.wait_ge(main_hi, s + 1)
                V.tensor_tensor(lo_main[:, half, :], raw_main[:, slot, :], hi_main[:, half, :].bitcast(F32), ALU.subtract) \
                    .then_inc(main_lo, 1)

            def split_to(u):
                while split[0] < len(SPLIT) and SPLIT[split[0]] <= u:
                    lo_main_of(split[0], split[0] % RAW, split[0] % 2)
                    split[0] += 1

            def along(ap, n):
                return ap.unsqueeze(2).broadcast_to([ap.shape[0], ap.shape[1], n])

            def over(ap, n):
                return ap.unsqueeze(1).broadcast_to([ap.shape[0], n, ap.shape[1]])

            def mod_row_out(l, n):
                m, sec = MOD_NO[l, n], n // SEC
                slot, bank = m % MOD_RAW, mod_bank(l, n)
                cols = slice((n % SEC) * UNIT, (n % SEC + 1) * UNIT)
                out = gate_row[:, sec // 3, cols] if sec % 3 == 2 else mod_row[:, cols]
                dve.wait_ge(main_used, mod_unit(l, n) + 1)
                dve.wait_ge(bias_loaded[slot], 16 * (m // MOD_RAW + 1))
                src = ps[:, bank, 0:UNIT]
                if sec % 3 == 0:
                    V.tensor_tensor(out, src, b_rows[:, slot, :], ALU.add).then_inc(mod_rows_out, 1)
                else:
                    V.scalar_tensor_tensor(out=out, in0=src, scalar=K("plus"), in1=b_rows[:, slot, :],
                                           op0=ALU.add, op1=ALU.add).then_inc(mod_rows_out, 1)
                if (l, n) in FOLD_NO:
                    feat_out(l, n, bank)

            def feat_out(l, n, bank):
                dve.wait_ge(mod_t, FOLD_NO[l, n] + 1)
                s = {3: 0, 7: 1, 15: 2, 19: 3}[n]
                V.tensor_copy(mod_feat[:, s].rearrange("p k g -> p (k g)"), ps[:, bank, 0:KC * G]).then_inc(mod_t_out, 1)

            def mods(these):
                for l, n in these:
                    mod_row_out(l, n)

            def make_x(l, n, shift, scale):
                if l + n == 0:
                    dve.wait_ge(mod_t_out, FOLD_NO[0, 7] + 1)
                else:
                    dve.wait_ge(ln_folded, 2 * l + n)
                dve.wait_ge(xt_done, 2 * (2 * l + n) + 2)
                for k in range(KC):
                    ins = V.tensor_scalar(x_feat[:, k, P:TOK], ps[:, 2 + k // 4, (k % 4) * P:(k % 4 + 1) * P],
                                          mod_feat[:, scale, k, 1:2], mod_feat[:, shift, k, 1:2], ALU.mult, ALU.add)
                ins.then_inc(x_feat_dve, 1)
                for g in range(G):
                    dve.wait_ge(x_hi_done, 2 * (2 * l + n) + g + 1)
                    V.tensor_tensor(x_lo[:, :, g * P:(g + 1) * P], x_feat[:, :, g * P:(g + 1) * P],
                                    x_hi[:, :, g * P:(g + 1) * P].bitcast(F32), ALU.subtract).then_inc(x_lo_done, 1)

            def cat_lo(l, part):
                dve.wait_ge(cat_hi_done, cat_parts(l) + part + 1)
                source, k, t = cat_part(l, part)
                V.tensor_tensor(x_lo[:, k, t], source, x_hi[:, k, t].bitcast(F32), ALU.subtract).then_inc(cat_lo_done, 1)

            def normalise(s, keys, n):
                den = small[:, 108:112] if keys == P else small[:, 156:160]
                dve.wait_ge(exped, n)
                link(V.tensor_reduce(den, s, AX.X, ALU.add))
                link(V.reciprocal(den, den))
                V.tensor_tensor(s, s, along(den, keys), ALU.mult).then_inc(probs, 1)

            def softmax_in(l, banks):
                ctx, own, cached = (ps[:, b, :].rearrange("p (h t) -> p h t", h=H) for b in banks)
                mx, mx_own, mx_cached = small[:, 104:108], small[:, 152:156], small[:, 156:160]
                dve.wait_ge(scores, 2 * l + 1)
                link(V.tensor_reduce(mx, ctx, AX.X, ALU.max))
                V.tensor_tensor(sc_ctx, ctx, along(mx, P), ALU.subtract).then_inc(centred, 1)
                dve.wait_ge(scores, 2 * l + 2)
                if l == 0:
                    link(V.scalar_tensor_tensor(out=sc_lat[:, :, 0:P], in0=own, scalar=ATT_SCALE,
                                                in1=bias.rearrange("p h a c -> p h (a c)"), op0=ALU.mult, op1=ALU.add))
                    link(V.tensor_scalar(sc_lat[:, :, P:2 * P], cached, ATT_SCALE, None, ALU.mult))
                    link(V.tensor_reduce(mx_own, sc_lat, AX.X, ALU.max))
                    V.tensor_tensor(sc_lat, sc_lat, along(mx_own, 2 * P), ALU.subtract).then_inc(centred, 1)
                else:
                    V.tensor_reduce(mx_own, own, AX.X, ALU.max)
                    link(V.tensor_reduce(mx_cached, cached, AX.X, ALU.max))
                    link(V.tensor_tensor(mx_own, mx_own, mx_cached, ALU.max))
                    V.tensor_tensor(sc_lat[:, :, 0:P], own, along(mx_own, P), ALU.subtract)
                    V.tensor_tensor(sc_lat[:, :, P:2 * P], cached, along(mx_own, P), ALU.subtract).then_inc(centred, 1)

            z_conv = conv_o.rearrange("p t g n -> p t (g n)")

            def conv(step):
                if step == 0:
                    dve.wait_ge(in_out, in_before(1) + 6)
                    cg = proj[:, 2:4, :].rearrange("p a (b c) -> p (a b) c", b=4)
                    ug = proj[:, 4:6, :].rearrange("p a (b c) -> p (a b) c", b=4)
                    link(V.memset(z_pad, 0.0))
                    link(V.tensor_tensor(z_pad[:, :, 1:P + 1], cg, ug, ALU.mult))
                    dve.wait_ge(small_in, 80)
                for w in ((0,), (1, 2))[step]:
                    for t in range(4):
                        zi = z_pad[:, 2 * t:2 * t + 2, w:w + P]
                        if w == 0:
                            ins = V.tensor_scalar(conv_o[:, t], zi, cv_w[:, w, t:t + 1], None, ALU.mult)
                        else:
                            ins = V.scalar_tensor_tensor(out=conv_o[:, t], in0=zi, scalar=cv_w[:, w, t:t + 1],
                                                         in1=conv_o[:, t], op0=ALU.mult, op1=ALU.add)
                    link(ins)
                if step == 1:
                    bg = proj[:, 0:2, :].rearrange("p a (b c) -> p (a b) c", b=2)
                    V.tensor_tensor(x_feat[:, 0:4, :], bg, z_conv, ALU.mult).then_inc(conv_ready, 1)

            def rms_rope():
                qk = proj[:, 6:9, :].rearrange("p a (b c) -> p (a b) c", b=4)
                dve.wait_ge(sq_ready, 1)
                V.tensor_reduce(small[:, 92:104], sq, AX.X, ALU.add).then_inc(ms_ready, 1)
                dve.wait_ge(small_in, 80)
                dve.wait_ge(rms_ready, 1)
                link(V.reciprocal(small[:, 124:136], small[:, 80:92]))
                link(V.tensor_tensor(qk, qk, along(small[:, 124:136], P), ALU.mult))
                V.tensor_tensor(qk[:, 0:8], qk[:, 0:8], over(gains[:, 0], 8), ALU.mult).then_inc(qk_normed, 1)
                V.tensor_tensor(qk[:, 8:12], qk[:, 8:12], over(gains[:, 1], 4), ALU.mult).then_inc(qk_normed, 1)
                dve.wait_ge(qk_normed, 2)
                lat = proj[:, 6:9, UNIT:2 * UNIT].rearrange("p a (b c e) -> p a b c e", b=2, e=2)
                ro = roped.rearrange("p (a b) (c e) -> p a b c e", b=2, e=2)
                tmp = sq.rearrange("p h t -> p (h t)")
                t1 = tmp[:, 0:384].rearrange("p (a b c) -> p a b c", a=3, b=2)
                t2 = tmp[:, 384:768].rearrange("p (a b c) -> p a b c", a=3, b=2)

                def ang(x):
                    return x.unsqueeze(1).unsqueeze(1).broadcast_to([P, 3, 2, P // 2])

                V.tensor_tensor(ro[:, :, :, :, 0], lat[:, :, :, :, 0], ang(K("cos")), ALU.mult)
                V.tensor_tensor(ro[:, :, :, :, 1], lat[:, :, :, :, 0], ang(K("sin")), ALU.mult)
                V.tensor_tensor(t1, lat[:, :, :, :, 1], ang(K("sin")), ALU.mult)
                link(V.tensor_tensor(t2, lat[:, :, :, :, 1], ang(K("cos")), ALU.mult))
                V.tensor_tensor(ro[:, :, :, :, 0], ro[:, :, :, :, 0], t1, ALU.subtract)
                V.tensor_tensor(ro[:, :, :, :, 1], ro[:, :, :, :, 1], t2, ALU.add).then_inc(roped_ready, 1)

            def fold_norm(l, n):
                dve.wait_ge(mod_t_out, FOLD_NO[l, 12 * n + 7] + 1)
                dve.wait_ge(ln_feat_in, 32)
                shift, scale = mod_feat[:, 2 * n], mod_feat[:, 2 * n + 1]
                last_g, last_b = (along(ln_feat[:, w, 2 * l + n - 1], G) for w in range(2))
                tmp = small[:, 60:76].rearrange("p (k g) -> p k g", g=G)
                link(V.tensor_tensor(tmp, scale, last_b, ALU.mult))
                link(V.tensor_tensor(shift, shift, tmp, ALU.add))
                V.tensor_tensor(scale, scale, last_g, ALU.mult).then_inc(ln_folded, 1)

            def post_norm(l, n, waiting):
                for g in range(G):
                    if n == 0:
                        if g == 0:
                            dve.wait_ge(main_used, out_unit(l, OUT_UNITS - 1) + 1)
                    else:
                        dve.wait_ge((y_context, down_used)[g], (l + 1) * (1, TURNS)[g])
                        dve.wait_ge(gate_copied, G * (2 * l + n) + g + 1)
                        norm_sum(n, g, 0)
                    if g == 1:
                        norm_factors(l, n, 0)
                    link(norm_sum(n, g, 1))
                    V.bn_aggr(small[:, 32 + 2 * g:34 + 2 * g], small[:, 112 + 48 * g:124 + 48 * g]).then_inc(ln_var, 1)
                    dve.wait_ge(ln_var, G * (2 * l + n) + g + 1)
                    if g == 0:
                        mods(waiting[:2])
                norm_factors(l, n, 1)
                mods(waiting[2:])

            def norm_sum(n, g, half):
                c = slice(half * 512, (half + 1) * 512)
                zh = z[:, g, c]
                if n == 0:
                    y = ps[:, 2 * half:2 * half + 2, g * UNIT:(g + 1) * UNIT]
                    zv = zh.rearrange("p (a b) -> p a b", b=UNIT)
                else:
                    y, zv = ps[:, 2 * g + half, :], zh
                link(V.tensor_tensor(zv, zv, y, ALU.mult))
                link(V.scalar_tensor_tensor(out=zh, in0=x_tok[:, g, c], scalar=ALPHA, in1=zh, op0=ALU.mult, op1=ALU.add))
                at = 112 + 48 * g + 6 * half
                return V.bn_stats(small[:, at:at + 6], zh)

            def norm_factors(l, n, g):
                sd, mean = small[:, 42 + g:43 + g], small[:, 32 + 2 * g:33 + 2 * g]
                dve.wait_ge(ln_sd, G * (2 * l + n) + g + 1)
                link(V.reciprocal(sd, small[:, 40 + g:41 + g]))
                V.scalar_tensor_tensor(out=small[:, 44 + g:45 + g], in0=mean, scalar=-1.0, in1=sd,
                                       op0=ALU.mult, op1=ALU.mult).then_inc(ln_factors, 1)

            def norm_tokens(l, n, g):
                dve.wait_ge(ln_in, 32 * (2 * l + n + 1))
                dve.wait_ge(standard, G * (2 * l + n) + g + 1)
                link(V.tensor_tensor(x_tok[:, g, :], z[:, g, :], ln_g, ALU.mult))
                V.tensor_tensor(x_tok[:, g, :], x_tok[:, g, :], ln_b, ALU.add).then_inc(normed, 1)

            def last_norm(l, n):
                dve.wait_ge(ln_in, 32 * (2 * l + n + 1))
                for g in range(G):
                    zg = z[:, g, :]
                    link(V.scalar_tensor_tensor(out=zg, in0=zg, scalar=small[:, 32 + 2 * g:33 + 2 * g], in1=ln_g,
                                                op0=ALU.subtract, op1=ALU.mult))
                    V.scalar_tensor_tensor(out=x_tok[:, g, :], in0=zg, scalar=small[:, 42 + g:43 + g], in1=ln_b,
                                           op0=ALU.mult, op1=ALU.add).then_inc(normed, 1)

            def route(l):
                dve.wait_ge(router_in, 32 * (l + 1))
                dve.wait_ge(sigmoid_out, l + 1)
                sel3 = select.rearrange("p (g e) -> p g e", g=G)
                link(V.tensor_tensor(sel3, score.rearrange("p (g e) -> p g e", g=G), over(rb, G), ALU.add))
                for n in range(G * GROUPS):
                    ins = V.max(top[:, n], select[:, n * PER_GROUP:(n + 1) * PER_GROUP])
                link(ins)
                link(V.tensor_tensor(gscore, top[:, :, 0], top[:, :, 1], ALU.add))
                for g in range(G):
                    ins = V.max(top4[:, g], gscore[:, g * GROUPS:(g + 1) * GROUPS])
                link(ins)
                link(V.memset(top4[:, :, TOPK_GROUPS:GROUPS], GONE / 2))
                for g in range(G):
                    ins = V.match_replace(gtaken[:, g * GROUPS:(g + 1) * GROUPS], top4[:, g],
                                          gscore[:, g * GROUPS:(g + 1) * GROUPS], GONE)
                link(ins)
                link(V.tensor_tensor(gmask, gtaken, gscore, ALU.not_equal))
                link(V.tensor_scalar(gpen, gmask, -LOW, LOW, ALU.mult, ALU.add))
                gsel3 = gsel.rearrange("p (a b) -> p a b", b=PER_GROUP)
                link(V.tensor_tensor(gsel3, select.rearrange("p (a b) -> p a b", b=PER_GROUP), along(gmask, PER_GROUP), ALU.mult))
                link(V.tensor_tensor(gsel3, gsel3, along(gpen, PER_GROUP), ALU.add))
                for g in range(G):
                    ins = V.max(top8[:, g], gsel[:, g * EXPERTS:(g + 1) * EXPERTS])
                link(ins)
                for g in range(G):
                    ins = V.match_replace(taken[:, g * EXPERTS:(g + 1) * EXPERTS], top8[:, g],
                                          gsel[:, g * EXPERTS:(g + 1) * EXPERTS], GONE)
                link(ins)
                link(V.tensor_tensor(taken, taken, gsel, ALU.not_equal))
                link(V.tensor_tensor(taken, taken, score, ALU.mult))
                taken3 = taken.rearrange("p (g e) -> p g e", g=G)
                link(V.tensor_reduce(wsum, taken3, AX.X, ALU.add))
                link(V.reciprocal(wsum, wsum))
                link(V.tensor_tensor(taken3, taken3, along(wsum, EXPERTS), ALU.mult))
                V.tensor_scalar(taken, taken, ROUTED_SCALE, None, ALU.mult).then_inc(gates_made, 1)

            def gates_out(l):
                dve.wait_ge(gates_t, l + 1)
                V.tensor_copy(gate_t, ps[0:EXPERTS, 3, 0:TOK]).then_inc(gates_t_out, 1)

            def experts(l):
                u0 = turn_unit(l, 0)
                s0 = SPLIT_NO[u0]

                def lo_down_of(t, slot):
                    dve.wait_ge(down_hi, l * TURNS + 1 + t)
                    V.tensor_tensor(lo_down[:, slot, :], raw_down[:, slot, :], hi_down[:, slot, :].bitcast(F32), ALU.subtract) \
                        .then_inc(down_lo, 1)

                def hidden_of(t, slot, bank, gslot, gate_count):
                    done = l * TURNS + 1 + t
                    dve.wait_ge(silu_out, done)
                    V.tensor_tensor(ex_up[:, slot, :], ex_silu[:, slot, :], ps[:, bank, TOK:2 * TOK], ALU.mult).then_inc(up_read, 1)
                    dve.wait_ge(up_read, done)
                    if gate_count is None:
                        dve.wait_ge(ones_set, l + 1)
                    else:
                        dve.wait_ge(gate_loaded[gslot], gate_count)
                    V.tensor_tensor(ex_h[:, slot, :], ex_up[:, slot, :], ex_gate[:, gslot, :], ALU.mult).then_inc(h_ready, 1)
                    dve.wait_ge(h_ready, done)
                    if not (isinstance(t, int) and l * TURNS + t < 2):
                        dve.wait_ge(down_used, l * TURNS - 1 + t)
                    V.tensor_copy(hid_hi[:, slot, :], ex_h[:, slot, :]).then_inc(h_hi, 1)
                    dve.wait_ge(h_hi, done)
                    V.tensor_tensor(hid_lo[:, slot, :], ex_h[:, slot, :], hid_hi[:, slot, :].bitcast(F32), ALU.subtract) \
                        .then_inc(h_lo, 1)

                def gate_count(t):
                    return None if t == 0 else 16 * (l * (EXPERTS // 4) + (t + 3) // 4)

                def turn(t, j, extra=0):
                    b = pair(l, j - 1)
                    lo_down_of(t - 1, b)
                    if j == 1:
                        gates_out(l)
                    if j > 1:
                        lo_main_of(s0 + t, (s0 + j) % RAW, (s0 + j) % 2)
                    c = gate_count(j - 1)
                    hidden_of(t - 1, b, 4 + (s0 + j - 1) % 2, (j - 1) % 4, None if c is None else c + 4 * extra)

                for t in range(1, 5):
                    turn(t, t)
                    if 1 < t < 4:
                        norm_tokens(l, 0, t - 2)
                with dve.Fori(0, LOOPS) as i:
                    for j in range(4):
                        turn(5 + j + 4 * i, 5 + j, 4 * i)
                        if j == 2 and l + 1 < DEPTH:
                            dve.wait_ge(next_mm, i + 1)
                            row = next_rows[:, bass.ds(i * UNIT, UNIT)]
                            V.tensor_tensor(row, row, ps[:, 6, 0:UNIT], ALU.add).then_inc(next_out, 1)
                last = TURNS - 1
                lo_down_of(last, pair(l, last))
                hidden_of(last, pair(l, last), 4 + (s0 + last) % 2, last % 4, gate_count(last))
                split[0] = s0 + TURNS

            link(V.memset(cond_pad[:, :, :], 0.0))
            dve.wait_ge(cond_ready, 1)
            V.tensor_copy(cond_pad[:, :, 0:G], cond_s[:, :, :].rearrange("p g k -> p k g")).then_inc(cond_ready, 1)
            mods(FIRST_MODS[:3])
            dve.wait_ge(decay_ready, 1)
            link(V.tensor_scalar(decay[:, 48:60], decay[:, 0:12], 0.0, None, ALU.min))
            V.tensor_tensor(decay[:, 48:60], decay[:, 48:60], decay[:, 36:48], ALU.subtract).then_inc(decay_ready, 1)
            dve.wait_ge(decay_ready, 2)
            dve.wait_ge(early_in, 16)
            for d in range(2):
                ins = V.tensor_scalar(small[:, 8 + 4 * d:12 + 4 * d], decay[:, 48 + 4 * d:52 + 4 * d], E("pos_col")[:, d:d + 1],
                                      None, ALU.mult)
                ins.then_inc(decay_ready, 1)
            mods(FIRST_MODS[3:6])
            dve.wait_ge(decay_ready, 16)
            for d, mask in enumerate(("mask_f", "mask_b")):
                ins = V.tensor_tensor(dec_e[:, d], dec_e[:, d], over(E(mask), H), ALU.mult)
            link(ins)
            link(V.tensor_tensor(dmat, dec_e[:, 0], dec_e[:, 1], ALU.add))
            dve.wait_ge(decay_ready, 17)
            V.memset(small[:, 48:49], 0.0).then_inc(k_dec_ready, 1)
            dve.wait_ge(consts_in, 16)

            for l in range(DEPTH):
                if l == 0:
                    mods(FIRST_MODS[6:])
                    split_to(in_unit(0, 0))
                if l > 0:
                    feat_out(l, 3, 6)
                    feat_out(l, 7, 7)
                    fold_norm(l, 0)
                make_x(l, 0, 0, 1)
                if l > 0:
                    mods(LAST_MODS[l - 1])
                for n in range(IN_UNITS[l]):
                    split_to(in_unit(l, n + 1) if n + 1 < IN_UNITS[l] else out_unit(l, 0))
                    if l > 0 and n < G:
                        norm_tokens(l - 1, 1, n)
                    mods(IN_MODS[l][n])
                    if l == 1 and n in (6, 7):
                        conv(n - 6)
                    if l == 1 and n == 8:
                        rms_rope()
                if l == 0:
                    dve.wait_ge(in_out, 1)
                    link(V.tensor_tensor(q_dec, q_dup[:, :, P:TOK], q_pow, ALU.mult))
                    dve.wait_ge(att_s, 1)
                    for par in range(2):
                        for g in range(G):
                            ins = V.tensor_tensor(att_d[:, par, g],
                                                  ps[:, 6 + par, g * 2 * P:(g + 1) * 2 * P].rearrange("p (h t) -> p h t", h=2),
                                                  dmat[:, par::2, :], ALU.mult)
                    ins.then_inc(att_d_ready, 1)
                    dve.wait_ge(k_t, 1)
                    kt = ps[:, 3, 0:H * DK].rearrange("p (h d) -> p h d", h=H)
                    for d in range(2):
                        ins = V.tensor_tensor(k_dec[:, :, d, :], kt, along(small[:, 4 * d:4 * d + 4], DK), ALU.mult)
                    ins.then_inc(k_dec_ready, 1)
                    dve.wait_ge(bias_in, 16 * 2 * H)
                    bias3 = bias.rearrange("p h a c -> p h (a c)")
                    V.tensor_tensor(bias3, bias3, over(K("window"), H), ALU.add).then_inc(window_used, 1)
                    dve.wait_ge(window_used, 1)
                    softmax_in(0, (0, 1, 2))
                else:
                    cat_lo(l, 0)
                    softmax_in(1, (6, 7, 0))
                normalise(sc_ctx, P, 2 * l + 1)
                normalise(sc_lat, 2 * P, 2 * l + 2)
                if l == 0:
                    stats = decay.rearrange("p (n c) -> p n c", c=6)
                    for g in range(G):
                        dve.wait_ge(ret_o, g + 1)
                        for h in range(H):
                            ins = V.bn_stats(stats[:, 4 * g + h], ps[:, 6 + g, h * P:(h + 1) * P])
                    link(ins)
                    for n in range(G * H):
                        ins = V.bn_aggr(small[:, 136 + 2 * n:138 + 2 * n], stats[:, n])
                    link(ins)
                    mv = small[:, 136:152].rearrange("p (n c) -> p n c", c=2)
                    V.tensor_copy(small[:, 24:32], mv[:, :, 1]).then_inc(ret_var, 1)
                    dve.wait_ge(ret_sd, 1)
                    link(V.reciprocal(small[:, 50:58], small[:, 16:24]))
                    for g in range(G):
                        for h in range(H):
                            ins = V.scalar_tensor_tensor(out=even_gate(h, g), in0=ps[:, 6 + g, h * P:(h + 1) * P],
                                                         scalar=mv[:, 4 * g + h, 0:1], in1=even_gate(h, g),
                                                         op0=ALU.subtract, op1=ALU.mult)
                    link(ins)
                    for g in range(G):
                        for h in range(H):
                            ins = V.tensor_scalar(even_gate(h, g), even_gate(h, g), small[:, 50 + 4 * g + h:51 + 4 * g + h], None,
                                                  ALU.mult)
                    ins.then_inc(ret_ready, 1)
                if l == 1:
                    split_to(out_unit(l, 1))
                for part in range(l, cat_parts(l + 1) - cat_parts(l)):
                    cat_lo(l, part)
                split_to(out_unit(l, 1))
                split_to(out_unit(l, OUT_UNITS - 1))
                fold_norm(l, 1)
                dve.wait_ge(main_used, out_unit(l, 1) + 1)
                for g in range(G):
                    dve.wait_ge(gate_copied, G * 2 * l + g + 1)
                    norm_sum(0, g, 0)
                post_norm(l, 0, NORM_MODS[l])
                make_x(l, 1, 2, 3)
                split_to(turn_unit(l, 1))
                route(l)
                experts(l)
                if l + 1 < DEPTH:
                    split_to(in_unit(l + 1, 0))
                post_norm(l, 1, [])
                if l + 1 == DEPTH:
                    last_norm(l, 1)

        @block.tensor
        def _(pe):
            def mm(out, w, x, start, stop):
                return nc.tensor.matmul(out, w, x, start=start, stop=stop)

            def turned(out, x, ident=None):
                return nc.tensor.transpose(out, x, K("ident") if ident is None else ident)

            def parts(out, pairs, first=True, last=True):
                n = len(pairs)
                for i, (w, x) in enumerate(pairs):
                    ins = mm(out, w, x, first and i == 0, last and i == n - 1)
                return ins

            def fold(rows, bank):
                v = rows.rearrange("r (p k) -> r k p", k=KC)
                for k in range(KC):
                    ins = mm(ps[:, bank, G * k:G * k + G], v[:, k], K("fold"), True, True)
                ins.then_inc(mod_t, 1)

            def mod(l, n):
                m, bank = MOD_NO[l, n], mod_bank(l, n)
                if m >= 2:
                    pe.wait_ge(mod_rows_out, m - 1)
                    if MODS[m - 2] in FOLD_NO:
                        pe.wait_ge(mod_t_out, FOLD_NO[MODS[m - 2]] + 1)
                elif m == 0:
                    pe.wait_ge(cond_ready, 2)
                w = mod_raw(l, n)
                pe.wait_ge(mod_loaded[m % MOD_RAW], 16 * (m // MOD_RAW + 1))
                mod_rows(w, bank).then_inc(main_used, 1)
                if (l, n) in FOLD_NO:
                    pe.wait_ge(mod_rows_out, m + 1)
                    if (l, n) == (1, 15):
                        pe.wait_ge(next_kept, 2)
                    fold(mod_row, bank)

            def mod_rows(w, bank):
                for i in range(KC // 4):
                    for j in range(4):
                        k = 4 * i + j
                        ins = mm(ps[COL * j:COL * (j + 1), bank, 0:UNIT], cond_pad[:, k, :], w[:, k], i == 0, k >= KC - 4)
                return ins

            def mods(these):
                for l, n in these:
                    mod(l, n)

            def x_turned(l, n):
                for g in range(G):
                    if l == 0 and n == 0:
                        pe.wait_ge(x_in, 32)
                        v = x_tok[:, g, :].rearrange("p (m k) -> p k m", k=KC)
                    else:
                        pe.wait_ge(standard, G * (2 * l + n - 1) + g + 1)
                        v = z[:, g, :].rearrange("p (m k) -> p k m", k=KC)
                    for k in range(KC):
                        ins = turned(ps[:, 2 * g + k // 4, (k % 4) * P:(k % 4 + 1) * P], v[:, k])
                    ins.then_inc(xt_done, 1)

            def x_parts_ready(l, n):
                pe.wait_ge(x_hi_done, 2 * (2 * l + n + 1))
                pe.wait_ge(x_lo_done, 2 * (2 * l + n + 1))

            def by_features(u, bank):
                w = [t[:, SPLIT_NO[u] % 2, :].rearrange("p (k n) -> p k n", k=KC) for t in (hi_main, lo_main)]
                for t in range(2):
                    c = slice(t * P, (t + 1) * P)
                    if t == 0:
                        pe.wait_ge(main_hi, SPLIT_NO[u] + 1)
                    hh = [(w[0][:, k, c], x_hi[:, k, :]) for k in range(KC)] + [(w[0][:, k, c], x_lo[:, k, :]) for k in range(KC)]
                    lh = [(w[1][:, k, c], x_hi[:, k, :]) for k in range(KC)]
                    parts(ps[:, bank, t * TOK:(t + 1) * TOK], hh, last=False)
                    if t == 0:
                        pe.wait_ge(main_lo, SPLIT_NO[u] + 1)
                    ins = parts(ps[:, bank, t * TOK:(t + 1) * TOK], lh, first=False)
                ins.then_inc(main_used, 1)

            def by_tokens(u, bank):
                w = [t[:, SPLIT_NO[u] % 2, :].rearrange("p (k n) -> p k n", k=KC) for t in (hi_main, lo_main)]
                for g in range(G):
                    c = slice(g * P, (g + 1) * P)
                    if g == 0:
                        pe.wait_ge(main_hi, SPLIT_NO[u] + 1)
                    hh = [(x_hi[:, k, c], w[0][:, k]) for k in range(KC)] + [(x_lo[:, k, c], w[0][:, k]) for k in range(KC)]
                    hl = [(x_hi[:, k, c], w[1][:, k]) for k in range(KC)]
                    parts(ps[:, bank, g * UNIT:(g + 1) * UNIT], hh, last=False)
                    if g == 0:
                        pe.wait_ge(main_lo, SPLIT_NO[u] + 1)
                    ins = parts(ps[:, bank, g * UNIT:(g + 1) * UNIT], hl, first=False)
                ins.then_inc(main_used, 1)

            def head(bank, h, width=P):
                return ps[:, bank, h * width:(h + 1) * width]

            def probs_turned(l, banks):
                pe.wait_ge(probs, 2 * l + 1)
                for h in range(H):
                    ins = turned(head(banks[0], h), sc_ctx[:, h])
                ins.then_inc(probs_t, 1)
                pe.wait_ge(probs, 2 * l + 2)
                for n in range(2):
                    for h in range(H):
                        ins = turned(head(banks[1 + n], h), sc_lat[:, h, n * P:(n + 1) * P])
                    ins.then_inc(probs_t, 1)

            def attended(l, values, cached, banks):
                pe.wait_ge(probs_t_out, 3 * l + 1)
                for h in range(H):
                    ins = mm(head(banks[0], h), values(h, 0), pr_t[:, 0, h], True, True)
                ins.then_inc(att_o, 1)
                pe.wait_ge(probs_t_out, 3 * l + 3)
                pe.wait_ge(cache_v_in, 16 * (l + 1))
                for h in range(H):
                    mm(head(banks[1], h), values(h, 1), pr_t[:, 1, h], True, False)
                    ins = mm(head(banks[1], h), cached(h), pr_t[:, 2, h], False, True)
                ins.then_inc(att_o, 1)

            def gate_spread(l, n, g):
                if (n, g) == (1, 1):
                    pe.wait_ge(gate_copied, G * (2 * l + 1) + 1)
                sel = K("pick")[:, g * P:(g + 1) * P]
                for c in range(2):
                    ins = mm(ps[:, gate_bank(l, n, g) + c, :], sel, gate_row[:, n, c * 512:(c + 1) * 512], True, True)
                ins.then_inc(gates_mm, 1)

            def experts(l):
                u0 = turn_unit(l, 0)
                s0 = SPLIT_NO[u0]

                def gate_up(s, half, bank):
                    w = [t[:, half, :].rearrange("p (k w n) -> p w k n", k=KC, w=2) for t in (hi_main, lo_main)]
                    pe.wait_ge(main_hi, s + 1)
                    for i in range(2):
                        out = ps[:, bank, i * TOK:(i + 1) * TOK]
                        hh = [(w[0][:, i, k], x_hi[:, k, :]) for k in range(KC)] + [(w[0][:, i, k], x_lo[:, k, :]) for k in range(KC)]
                        lh = [(w[1][:, i, k], x_hi[:, k, :]) for k in range(KC)]
                        parts(out, hh, last=False)
                        if i == 0:
                            pe.wait_ge(main_lo, s + 1)
                        ins = parts(out, lh, first=False)
                    ins.then_inc(main_used, 1)

                def down(t, slot, first, last):
                    done = l * TURNS + 1 + t
                    pe.wait_ge(down_hi, done)
                    pe.wait_ge(down_lo, done)
                    pe.wait_ge(h_hi, done)
                    pe.wait_ge(h_lo, done)
                    for g in range(G):
                        hh, hl = (x[:, slot, g * P:(g + 1) * P] for x in (hid_hi, hid_lo))
                        for c in range(2):
                            wh, wl = (x[:, slot, c * 512:(c + 1) * 512] for x in (hi_down, lo_down))
                            ins = parts(ps[:, 2 * g + c, :], [(hh, wh), (hh, wl), (hl, wh)], first=first, last=last)
                        if last and g == 0:
                            ins.then_inc(y_context, 1)
                    ins.then_inc(down_used, 1)

                def turn(t, j):
                    gate_up(s0 + t, (s0 + j) % 2, 4 + (s0 + j) % 2)
                    down(t - 1, pair(l, j - 1), j == 1, False)

                pe.wait_ge(mod_rows_out, mods_before(u0))
                gate_up(s0, s0 % 2, 4 + s0 % 2)
                pe.wait_ge(sigmoid_out, l + 1)
                gate_up(s0 + 1, (s0 + 1) % 2, 4 + (s0 + 1) % 2)
                pe.wait_ge(gates_made, l + 1)
                for g in range(G):
                    ins = turned(ps[0:EXPERTS, 3, g * P:(g + 1) * P], taken[:, g * EXPERTS:(g + 1) * EXPERTS])
                ins.then_inc(gates_t, 1)
                pe.wait_ge(gates_t_out, l + 1)
                down(0, pair(l, 0), True, False)
                for t in range(2, 5):
                    turn(t, t)
                    if t == 3:
                        gate_spread(l, 1, 1)
                if l + 1 < DEPTH:
                    pe.wait_ge(gate_copied, G * (2 * l + 2))
                with pe.Fori(0, LOOPS) as i:
                    for j in range(4):
                        turn(5 + j + 4 * i, 5 + j)
                        if j == 1 and l + 1 < DEPTH:
                            pe.wait_ge(next_out, i + 1)
                            pe.wait_ge(next_loaded, 16 * (i + 1))
                            mod_rows(next_raw, 6).then_inc(next_mm, 1)
                down(TURNS - 1, pair(l, TURNS - 1), False, True)
                if l + 1 < DEPTH:
                    pe.wait_ge(next_out, NEXT + 1)
                    fold(next_rows[:, 0:D], 6)
                    fold(next_rows[:, D:2 * D], 7)

            pe.wait_ge(consts_in, 16)
            for l in range(DEPTH):
                if l == 0:
                    mods(FIRST_MODS[:6])
                x_turned(l, 0)
                if l == 0:
                    mods(FIRST_MODS[6:])
                    pe.wait_ge(cache_k_in, 16)
                    for h in range(H):
                        ins = turned(head(7, h), kc_in[:, h])
                    ins.then_inc(cache_t, 1)
                if l > 0:
                    pe.wait_ge(mod_t_out, FOLD_NO[l, 7] + 1)
                    mods(LAST_MODS[l - 1])
                x_parts_ready(l, 0)
                for n in range(IN_UNITS[l]):
                    u = in_unit(l, n)
                    s = in_before(l) + n
                    if n < 2:
                        pe.wait_ge(mod_rows_out, mods_before(in_unit(l, 0)) - (len(LAST_MODS[0]) if l else 0))
                    else:
                        pe.wait_ge(in_out, s - 1)
                    feat = n in (0, 1, 6, 7, 8, 9) if l == 0 else n < 6
                    (by_features if feat else by_tokens)(u, 4 + SPLIT_NO[u] % 2)
                    if l == 0 and n == 0:
                        pe.wait_ge(cache_t_out, 1)
                    mods(IN_MODS[l][n])
                pe.wait_ge(in_out, in_before(l) + IN_UNITS[l])
                pe.wait_ge(mod_rows_out, mods_before(out_unit(l, 0)))
                pe.wait_ge(mod_t_out, FOLD_NO[l, 19] + 1)
                if l == 0:
                    pe.wait_ge(cache_t_out, 1)
                    for h in range(H):
                        for g in range(G):
                            at = (2 * g + h // 2) * P
                            ins = mm(ps[:, 6 + h % 2, at:at + P], k_low[:, h, g * P:(g + 1) * P],
                                     q_dup[0:DK, h, g * P:(g + 1) * P], True, True)
                    ins.then_inc(att_s, 1)
                    for h in range(H):
                        ins = turned(head(3, h, DK), k_low[:, h, 0:P], K("ident", DK)[:, 0:DK])
                    ins.then_inc(k_t, 1)
                    for h in range(H):
                        ins = mm(head(0, h), na_q(h, 0), na_k(h, 0), True, True)
                    ins.then_inc(scores, 1)
                    for h in range(H):
                        mm(head(1, h), na_q(h, 1), na_k(h, 1), True, True)
                    for h in range(H):
                        ins = mm(head(2, h), na_q(h, 1), kc_t[:, h], True, True)
                    ins.then_inc(scores, 1)
                    pe.wait_ge(k_dec_ready, 2)
                    for h in range(H):
                        ins = mm(head(3, h), k_dec[:, h].rearrange("p d k -> p (d k)"), even_v(h, 0), True, True)
                    ins.then_inc(state_mm, 1)
                    pe.wait_ge(att_d_ready, 1)
                    pe.wait_ge(state_in, 32)
                    for g in range(G):
                        for h in range(H):
                            ins = mm(head(6 + g, h), att_d[:, h % 2, g, h // 2], even_v(h, g), True, g == 0)
                            if g == 1:
                                ins = mm(head(6 + g, h), q_dec[:, h], s0[:, h], False, True)
                        ins.then_inc(ret_o, 1)
                    gate_spread(l, 0, 0)
                    probs_turned(l, (0, 1, 2))
                    pe.wait_ge(state_copied, 1)
                    attended(l, na_v, lambda h: vc[:, h], (3, 0))
                    for h in range(H):
                        ins = turned(head(2, h), na_k(h, 0))
                    ins.then_inc(kn_t, 1)
                    pe.wait_ge(ret_ready, 1)
                    for g in range(G):
                        for h in range(H):
                            ins = turned(head(6 + g, h), even_gate(h, g))
                        ins.then_inc(ret_t, 1)
                else:
                    pe.wait_ge(qk_normed, 2)
                    for n in range(6):
                        ins = turned(head(0 if n < 4 else 1, n % 4), proj[:, 6 + n // 2, (n % 2) * P:(n % 2) * P + P])
                        if n in (3, 5):
                            ins.then_inc(qk_tr, 1)
                    pe.wait_ge(roped_ready, 1)
                    for n in range(6):
                        ins = turned(head(2 if n < 4 else 3, n % 4), roped[:, n])
                        if n in (3, 5):
                            ins.then_inc(qk_tr, 1)
                    pe.wait_ge(cache_k_in, 32)
                    for h in range(KVH):
                        ins = turned(head(7, h), kc_in1[:, h])
                    ins.then_inc(cache_t, 1)
                    pe.wait_ge(qk_t_out, 4)
                    for h in range(H):
                        ins = mm(head(6, h), qk_t[:, h], qk_t[:, 4 + h // 2], True, True)
                    ins.then_inc(scores, 1)
                    pe.wait_ge(cache_t_out, 2)
                    for h in range(H):
                        mm(head(7, h), qk_t[:, 6 + h], qk_t[:, 10 + h // 2], True, True)
                    for h in range(H):
                        ins = mm(head(0, h), qk_t[:, 6 + h], kc_t1[:, h // 2], True, True)
                    ins.then_inc(scores, 1)
                    gate_spread(l, 0, 0)
                    probs_turned(l, (6, 7, 0))
                    attended(l, lambda h, g: att_v(h // 2, g), lambda h: vc1[:, h // 2], (1, 2))
                if l == 0:
                    pe.wait_ge(cat_lo_done, 1)
                    pe.wait_ge(kn_out, 1)
                gate_spread(l, 0, 1)
                pe.wait_ge(cat_hi_done, cat_parts(l + 1))
                pe.wait_ge(cat_lo_done, cat_parts(l + 1))
                for n in range(OUT_UNITS):
                    by_tokens(out_unit(l, n), n)
                    if n == 1:
                        pe.wait_ge(gate_copied, G * (2 * l + 1))
                mods(NORM_MODS[l])
                x_turned(l, 1)
                pe.wait_ge(mod_rows_out, mods_before(turn_unit(l, 0)))
                pe.wait_ge(gate_copied, G * (2 * l + 1))
                gate_spread(l, 1, 0)
                pe.wait_ge(x_feat_act, 2 * l + 2)
                pe.wait_ge(x_feat_dve, 2 * l + 2)
                pe.wait_ge(router_in, 32 * (l + 1))
                for g in range(G):
                    for k in range(KC):
                        ins = mm(logits_of(l)[:, g * EXPERTS:(g + 1) * EXPERTS], x_feat[:, k, g * P:(g + 1) * P], rw[:, k], k == 0, k == KC - 1)
                ins.then_inc(logits, 1)
                x_parts_ready(l, 1)
                experts(l)


_INS = ['x_prompt', 'x_sample', 'c', 'state_ret', 'cache_na_k', 'cache_na_v', 'cache_att_k', 'cache_att_v', 'c_ctx',
        'w_mod', 'b_mod', 'ln_g', 'ln_b', 'w_in_even', 'w_out_even', 'ret_decay_logit', 'na_rpb', 'w_in_odd', 'w_out_odd',
        'conv_w', 'q_norm_g', 'k_norm_g', 'router_w', 'router_b', 'exp_w_gate', 'exp_w_up', 'exp_w_down',
        'sh_w_gate', 'sh_w_up', 'sh_w_down']
_OUTS = [('y_prompt', (1, 128, 1024)), ('y_sample', (1, 128, 1024)), ('state', (1, 1, 2, 4, 64, 128)),
         ('na_k', (1, 1, 128, 4, 128)), ('na_v', (1, 1, 128, 4, 128)),
         ('att_k', (1, 1, 128, 2, 128)), ('att_v', (1, 1, 128, 2, 128))]


def kernel(**inputs):
    import concourse.bacc as _bacc
    from concourse.bass_utils import run_bass_kernel_spmd as _run

    nc = _bacc.Bacc("TRN2", target_bir_lowering=False, num_devices=1)
    arrays = {name: np.ascontiguousarray(inputs[name]) for name in _INS}
    arrays["shape_consts"] = shape_constants()
    ins = {}
    for name, a in arrays.items():
        ins[name] = nc.dram_tensor(f"in_{name}", a.shape, mybir.dt.from_np(a.dtype), kind="ExternalInput").ap()
    outs = {name: nc.dram_tensor(f"out_{name}", shape, F32, kind="ExternalOutput").ap() for name, shape in _OUTS}
    build(nc, ins, outs)
    r = _run(nc, [{f"in_{name}": a for name, a in arrays.items()}], core_ids=[0])
    return tuple(r.results[0][f"out_{name}"] for name, _ in _OUTS)
```
